# Optimizing a Trainium2 kernel written in Bass

```python
import math
import jax, jax.numpy as jnp
from jax import lax
import numpy as np

D_MODEL = 1024
BATCH = 1
SEQ = 512
DEPTH = 1

CHUNK = 64
Q_BLOCK = 128
D_MIX = D_MODEL
D_ATT = D_MIX // 2
D_RNN = D_MIX - D_ATT
N_ATT_HEADS = 4
ATT_HEAD_DIM = D_ATT // (2 * N_ATT_HEADS)
ATT_V_DIM = 2 * ATT_HEAD_DIM
N_RNN_BLOCKS = 8
RNN_BLOCK = D_RNN // N_RNN_BLOCKS
CONV_WIDTH = 4
RGLRU_C = 8.0
D_FF = 2816
N_SUB = 3
W_IN_COLS = 3 * D_ATT + 2 * D_RNN
EPS = 1e-6

kernel_name = "hybrid_diffattn_rglru_macaron_adaln"

def _rmsnorm(x, g):
    xf = x.astype(jnp.float32)
    y = xf * lax.rsqrt(jnp.mean(xf * xf, axis=-1, keepdims=True) + EPS)
    return (y * g.astype(jnp.float32)).astype(x.dtype)

def _modulate(h, shift, scale):
    return h * (1.0 + scale[:, None, :]) + shift[:, None, :]

def _swiglu(h, w_gate, w_up, w_down):
    return (jax.nn.silu(h @ w_gate) * (h @ w_up)) @ w_down

def _alibi_slopes(n_heads):
    return 2.0 ** (-8.0 * (jnp.arange(n_heads, dtype=jnp.float32) + 1.0) / n_heads)

def _diff_attention(q, k, v, lam):
    S = q.shape[1]
    scale = ATT_HEAD_DIM ** -0.5
    slopes = _alibi_slopes(N_ATT_HEADS)
    outs = []
    for blk in range(S // Q_BLOCK):
        q0 = blk * Q_BLOCK
        kend = q0 + Q_BLOCK
        qb = q[:, q0:kend]
        kb = k[:, :kend]
        vb = v[:, :kend]
        s = jnp.einsum('bqhmd,bkhmd->bhmqk', qb, kb,
                       preferred_element_type=jnp.float32) * scale
        tq = jnp.arange(q0, kend)
        tk = jnp.arange(kend)
        dist = jnp.abs(tq[:, None] - tk[None, :]).astype(jnp.float32)
        allowed = (tk[None, :] // CHUNK) <= (tq[:, None] // CHUNK)
        s = s - slopes[None, :, None, None, None] * dist[None, None, None]
        s = jnp.where(allowed[None, None, None], s, -jnp.inf)
        p = jax.nn.softmax(s, axis=-1)
        a = p[:, :, 0] - lam * p[:, :, 1]
        outs.append(jnp.einsum('bhqk,bkhe->bqhe', a.astype(v.dtype), vb))
    return jnp.concatenate(outs, axis=1)

def _causal_depthwise_conv(x, w, b):
    S = x.shape[1]
    xp = jnp.pad(x, ((0, 0), (CONV_WIDTH - 1, 0), (0, 0)))
    y = xp[:, 0:S] * w[0]
    for i in range(1, CONV_WIDTH):
        y = y + xp[:, i:i + S] * w[i]
    return y + b

def _rglru(x, w_a, b_a, w_x, b_x, lru_lambda):
    B, S, _ = x.shape
    xf = x.astype(jnp.float32)
    xb = xf.reshape(B, S, N_RNN_BLOCKS, RNN_BLOCK)
    r = jax.nn.sigmoid(jnp.einsum('bsnc,ncd->bsnd', xb, w_a.astype(jnp.float32)).reshape(B, S, D_RNN)
                       + b_a.astype(jnp.float32))
    i = jax.nn.sigmoid(jnp.einsum('bsnc,ncd->bsnd', xb, w_x.astype(jnp.float32)).reshape(B, S, D_RNN)
                       + b_x.astype(jnp.float32))
    log_a = -RGLRU_C * r * jax.nn.softplus(-lru_lambda.astype(jnp.float32))
    a = jnp.exp(log_a)
    u = jnp.sqrt(-jnp.expm1(2.0 * log_a)) * (i * xf)

    def combine(left, right):
        a_l, u_l = left
        a_r, u_r = right
        return a_l * a_r, a_r * u_l + u_r

    _, h = lax.associative_scan(combine, (a, u), axis=1)
    return h.astype(x.dtype)

def setup_inputs(seed: int = 0) -> dict:
    key = jax.random.key(seed)
    ks = jax.random.split(key, 32)
    f32 = jnp.float32
    L = DEPTH
    nrm = lambda k, shape, s: jax.random.normal(k, shape, f32) * s
    u = jax.random.uniform(ks[20], (L, D_RNN), f32, 0.9, 0.999)
    sig_l = u ** (1.0 / RGLRU_C)
    lru_lambda = jnp.log(sig_l) - jnp.log1p(-sig_l)
    return {
        "x": nrm(ks[0], (BATCH, SEQ, D_MODEL), 1.0),
        "c": nrm(ks[1], (BATCH, D_MODEL), 1.0),
        "w_ada": nrm(ks[2], (L, D_MODEL, N_SUB * 3 * D_MODEL), 0.5 * D_MODEL ** -0.5),
        "b_ada": nrm(ks[3], (L, N_SUB * 3 * D_MODEL), 0.01),
        "g_norm": 1.0 + nrm(ks[4], (L, N_SUB, D_MODEL), 0.01),
        "ffn1_w_gate": nrm(ks[5], (L, D_MODEL, D_FF), D_MODEL ** -0.5),
        "ffn1_w_up": nrm(ks[6], (L, D_MODEL, D_FF), D_MODEL ** -0.5),
        "ffn1_w_down": nrm(ks[7], (L, D_FF, D_MODEL), D_FF ** -0.5),
        "w_in": nrm(ks[8], (L, D_MODEL, W_IN_COLS), D_MODEL ** -0.5),
        "q_norm_g": 1.0 + nrm(ks[9], (L, 2, ATT_HEAD_DIM), 0.01),
        "k_norm_g": 1.0 + nrm(ks[10], (L, 2, ATT_HEAD_DIM), 0.01),
        "lambda_params": nrm(ks[11], (L, 4, ATT_HEAD_DIM), 0.1),
        "head_norm_g": 1.0 + nrm(ks[12], (L, ATT_V_DIM), 0.01),
        "conv_w": nrm(ks[13], (L, CONV_WIDTH, D_RNN), CONV_WIDTH ** -0.5),
        "conv_b": nrm(ks[14], (L, D_RNN), 0.01),
        "w_rg_a": nrm(ks[15], (L, N_RNN_BLOCKS, RNN_BLOCK, RNN_BLOCK), RNN_BLOCK ** -0.5),
        "b_rg_a": nrm(ks[16], (L, D_RNN), 0.01),
        "w_rg_x": nrm(ks[17], (L, N_RNN_BLOCKS, RNN_BLOCK, RNN_BLOCK), RNN_BLOCK ** -0.5),
        "b_rg_x": nrm(ks[18], (L, D_RNN), 0.01),
        "lru_lambda": lru_lambda,
        "w_out": nrm(ks[19], (L, D_MIX, D_MODEL), D_MIX ** -0.5),
        "ffn2_w_gate": nrm(ks[21], (L, D_MODEL, D_FF), D_MODEL ** -0.5),
        "ffn2_w_up": nrm(ks[22], (L, D_MODEL, D_FF), D_MODEL ** -0.5),
        "ffn2_w_down": nrm(ks[23], (L, D_FF, D_MODEL), D_FF ** -0.5),
    }

def reference(x, c, w_ada, b_ada, g_norm, ffn1_w_gate, ffn1_w_up, ffn1_w_down,
              w_in, q_norm_g, k_norm_g, lambda_params, head_norm_g, conv_w, conv_b,
              w_rg_a, b_rg_a, w_rg_x, b_rg_x, lru_lambda, w_out,
              ffn2_w_gate, ffn2_w_up, ffn2_w_down):
    B, S, D = x.shape
    c_act = jax.nn.silu(c)
    for l in range(DEPTH):
        mod = (c_act @ w_ada[l] + b_ada[l]).reshape(B, N_SUB, 3, D)

        h = _modulate(_rmsnorm(x, g_norm[l, 0]), mod[:, 0, 0], mod[:, 0, 1])
        x = x + 0.5 * mod[:, 0, 2][:, None, :] * _swiglu(h, ffn1_w_gate[l], ffn1_w_up[l], ffn1_w_down[l])

        h = _modulate(_rmsnorm(x, g_norm[l, 1]), mod[:, 1, 0], mod[:, 1, 1])
        proj = h @ w_in[l]
        q = proj[..., 0:D_ATT].reshape(B, S, N_ATT_HEADS, 2, ATT_HEAD_DIM)
        k = proj[..., D_ATT:2 * D_ATT].reshape(B, S, N_ATT_HEADS, 2, ATT_HEAD_DIM)
        v = proj[..., 2 * D_ATT:3 * D_ATT].reshape(B, S, N_ATT_HEADS, ATT_V_DIM)
        gate_br = proj[..., 3 * D_ATT:3 * D_ATT + D_RNN]
        x_br = proj[..., 3 * D_ATT + D_RNN:]

        q = _rmsnorm(q, q_norm_g[l])
        k = _rmsnorm(k, k_norm_g[l])
        lam_init = 0.8 - 0.6 * math.exp(-0.3 * l)
        lp = lambda_params[l].astype(jnp.float32)
        lam = jnp.exp(jnp.sum(lp[0] * lp[1])) - jnp.exp(jnp.sum(lp[2] * lp[3])) + lam_init
        att = _diff_attention(q, k, v, lam)
        att = (_rmsnorm(att, head_norm_g[l]) * (1.0 - lam_init)).reshape(B, S, D_ATT)

        xr = _causal_depthwise_conv(x_br, conv_w[l], conv_b[l])
        hr = _rglru(xr, w_rg_a[l], b_rg_a[l], w_rg_x[l], b_rg_x[l], lru_lambda[l])
        rnn = jax.nn.gelu(gate_br) * hr

        mix = jnp.concatenate([att, rnn], axis=-1) @ w_out[l]
        x = x + mod[:, 1, 2][:, None, :] * mix

        h = _modulate(_rmsnorm(x, g_norm[l, 2]), mod[:, 2, 0], mod[:, 2, 1])
        x = x + 0.5 * mod[:, 2, 2][:, None, :] * _swiglu(h, ffn2_w_gate[l], ffn2_w_up[l], ffn2_w_down[l])
    return x


_drawn_inputs = setup_inputs


def setup_inputs(seed=0):
    import zlib

    import numpy as np

    out = dict(_drawn_inputs(seed))
    spreads = {}
    factors = {'b_ada': 3.908,
     'g_norm': 8.0,
     'q_norm_g': 40.055,
     'k_norm_g': 41.757,
     'lambda_params': 3.934,
     'head_norm_g': 64.0,
     'conv_b': 8.0,
     'b_rg_a': 64.0,
     'b_rg_x': 64.0}
    for name, (base, spread) in spreads.items():
        noise = np.random.default_rng([zlib.crc32(name.encode()), seed]).standard_normal(out[name].shape)
        drawn = base * np.exp(spread * noise) if base else spread * noise
        out[name] = __import__('jax').numpy.asarray(drawn.astype(out[name].dtype))
    for name, factor in factors.items():
        out[name] = (out[name] * factor).astype(out[name].dtype)
    return out
```

```python
from contextlib import ExitStack

import concourse.bass as bass
from concourse import mybir

F32 = mybir.dt.float32
F32R = mybir.dt.float32r
I32 = mybir.dt.int32
ALU = mybir.AluOpType
ACT = mybir.ActivationFunctionType
AX_X = mybir.AxisListType.X

P = 128
EPS = 1e-6
MASKED = -1e30
LAM_INIT = 0.2
RGLRU_C = 8.0
CHUNK = 64


class Chain:

    def __init__(self, sem):
        self.sem, self.at = sem, 0

    def link(self, eng, ins):
        ins.then_inc(self.sem, 1)
        self.at = self.at + 1
        eng.wait_ge(self.sem, self.at)


def encoder_layer(nc, x, c, w_ada, b_ada, g_norm, ffn1_w_gate, ffn1_w_up, ffn1_w_down, w_in, q_norm_g,
                  k_norm_g, lambda_params, head_norm_g, conv_w, conv_b, w_rg_a, b_rg_a, w_rg_x, b_rg_x,
                  lru_lambda, w_out, ffn2_w_gate, ffn2_w_up, ffn2_w_down, out):
    S, D = x.shape[1], x.shape[2]
    FF = ffn1_w_gate.shape[2]
    KD, FT, TT = D // P, FF // P, S // P
    PAIRS = FT // 2
    DA = q_norm_g.shape[1] * 0 + D // 2
    NH = DA // P
    HD = P // 2
    RT = DA // P
    CW = conv_w.shape[1]
    DOWN_CUTS = [(0, 8), (8, 16), (16, FT)]

    C_ACT, B_ADA, G_NORM = 0, KD, KD + 9 * KD
    ROWS_A = G_NORM + 3 * KD
    Q_G, K_G, H_G = ROWS_A, ROWS_A + 1, ROWS_A + 2
    CONV_W = H_G + 1
    CONV_B = CONV_W + CW * RT
    B_A, B_X, LRU = CONV_B + RT, CONV_B + 2 * RT, CONV_B + 3 * RT
    NCOLS = LRU + RT

    def mod(group, d=0):
        return B_ADA + group * KD + d

    P_FFN = [0, 4 * PAIRS + 3 * KD + 28]
    P_DOWN = [p + 4 * PAIRS for p in P_FFN]
    P_MIX = P_DOWN[0] + 3 * KD
    N_IN = 20
    SPLIT_FFN = [KD, 3 * KD + FT]

    with ExitStack() as ctx:
        def sem(name):
            return ctx.enter_context(nc.semaphore(name))

        top = [(nc.sbuf_base + 31) // 32 * 32]

        def place(name, shape, dt, offset=None):
            size = 4
            for n in shape[1:]:
                size *= n
            if offset is None:
                offset = top[0]
                top[0] += (size + 31) // 32 * 32
            return nc.alloc_sbuf_tensor_at(name, shape, dt, offset=offset), offset

        xT, _ = place("xT", [P, KD, S], F32)
        raw, raw_at = place("raw", [P, 4, 2048], F32)
        w_hi, _ = place("w_hi", [P, 4, 1024], F32R)
        w_lo, _ = place("w_lo", [P, 4, 1024], F32R)
        h_hi, h_at = place("h_hi", [P, KD, S], F32R)
        h_lo, h_lo_at = place("h_lo", [P, KD, S], F32R)
        a_hi, m_at = place("a_hi", [P, FT, S], F32R)
        a_lo, _ = place("a_lo", [P, FT, S], F32R)
        m_end = top[0]
        tmp, _ = place("tmp", [P, 2, S], F32)
        acc, _ = place("acc", [P, S], F32)
        ident, _ = place("ident", [P, P], F32)
        ones, _ = place("ones", [P, P], F32)
        cols, _ = place("cols", [P, NCOLS], F32)
        misc, _ = place("misc", [P, 64], F32)
        assert top[0] <= nc.sbuf_usable_end

        x_nat, _ = place("x_nat", [P, TT, D], F32, h_at)
        lam_in, _ = place("lam_in", [P, 4, HD], F32, h_lo_at)
        lam_pr, _ = place("lam_pr", [P, 2, HD], F32, h_lo_at + 4096)
        y_nat, _ = place("y_nat", [P, KD // 2, TT, 2 * P], F32, h_at)

        at = m_at
        mix = {}
        for name, shape, dt in [("q_hi", [P, NH, S], F32R), ("q_lo", [P, NH, S], F32R),
                                ("k_hi", [P, NH, S], F32R), ("k_lo", [P, NH, S], F32R),
                                ("v_hi", [P, TT, S], F32R), ("v_lo", [P, TT, S], F32R),
                                ("xr", [P, RT, S], F32), ("gate", [P, RT, S], F32),
                                ("alibi", [P, NH, S], F32), ("prob", [P, 2, 2, S], F32),
                                ("p_hi", [P, TT, P], F32R), ("p_lo", [P, TT, P], F32R),
                                ("c_hi", [P, S], F32R), ("c_lo", [P, S], F32R)]:
            mix[name], _ = place(name, shape, dt, at)
            n = 4
            for q in shape[1:]:
                n *= q
            at += n
        assert at <= m_end
        gate_at = m_at + 4 * S * (4 * NH + 2 * TT + RT)
        c_hi2, _ = place("c_hi2", [P, S], F32R, gate_at + 4 * S * 2)
        c_lo2, _ = place("c_lo2", [P, S], F32R, gate_at + 4 * S * 3)
        q_hi, q_lo, k_hi, k_lo, v_hi, v_lo = (mix[n] for n in ("q_hi", "q_lo", "k_hi", "k_lo", "v_hi", "v_lo"))
        xr, gate, alibi, prob = (mix[n] for n in ("xr", "gate", "alibi", "prob"))
        p_hi, p_lo = mix["p_hi"], mix["p_lo"]
        c_hi, c_lo = (mix["c_hi"], c_hi2), (mix["c_lo"], c_lo2)
        RAW = 8192
        bd_hi, _ = place("bd_hi", [P, 2, RT, P], F32R, raw_at + 2 * RAW)
        bd_lo, _ = place("bd_lo", [P, 2, RT, P], F32R, raw_at + 2 * RAW + 4096)
        bd, _ = place("bd", [P, 2, RT, P], F32, raw_at + 3 * RAW)
        ones_half, _ = place("ones_half", [P, P], F32, raw_at + 3 * RAW + 4096)
        dist, _ = place("dist", [P, S], I32, raw_at + 3 * RAW + 4608)
        decay, _ = place("decay", [P, RT, S], F32, raw_at + 3 * RAW)
        tanh_z, _ = place("tanh_z", [P, RT, S], F32, h_at)
        drive, _ = place("drive", [P, RT, S], F32, h_at + 8192)

        ps = ctx.enter_context(nc.psum_tensor("ps", [P, 8, 512], F32))

        EPS_C, NEG_LAM, LAM_E, LAM_S = 0, 1, 2, 4
        VAR, RSTD, NEWT = 8, 12, 16
        SP8, NSP8, HG8 = 20, 24, 28
        MX = [32, 44]
        SPT = 32

        raw_in = [sem(f"raw_in{i}") for i in range(4)]
        w_hi_ready, w_lo_ready = sem("w_hi_ready"), sem("w_lo_ready")
        panel_done = sem("panel_done")
        ada_sum, ada_done = sem("ada_sum"), sem("ada_done")
        mod_ready = sem("mod_ready")
        norm_ready, h_hi_ready = sem("norm_ready"), sem("h_hi_ready")
        silu_ready, prod_ready, a_hi_ready = sem("silu_ready"), sem("prod_ready"), sem("a_hi_ready")
        split_done = sem("split_done")
        x_updated, sq_ready, sq_added = sem("x_updated"), sem("sq_ready"), sem("sq_added")
        stat_done, var_ready, rough_ready = sem("stat_done"), sem("var_ready"), sem("rough_ready")
        diag_ready, rstd_done = sem("diag_ready"), sem("rstd_done")
        s_const, s_rows, s_x, s_lam = sem("consts_ready"), sem("rows_in"), sem("x_in"), sem("lambda_in")
        rows_done, cols_ready = sem("rows_transposed"), sem("cols_ready")
        c_ready, eye0 = sem("c_ready"), sem("ident_zeroed")
        xt_done, xt_out = sem("x_transposed"), sem("x_evicted")
        lam_dot, lam_exp, sp_exp = sem("lambda_dots"), sem("lambda_exps"), sem("softplus_exps")
        y_done, y_out, y_stored = sem("y_transposed"), sem("y_evicted"), sem("y_stored")
        dist_ready, bd_zero, bd_in, bd_hi_ready, bd_ready = (sem(n) for n in (
            "dist_ready", "bd_zeroed", "bd_in", "bd_hi_ready", "bd_ready"))
        alibi_ready, v_half_done, tile_free = sem("alibi_ready"), sem("v_half_done"), sem("tile_free")
        v_hi_ready, sqh_ready, sth_done = sem("v_hi_ready"), sem("qk_squared"), sem("qk_summed")
        ln_ready, qk_f32, qk_hi, qk_ready = sem("qk_rough_rstd"), sem("qk_scaled"), sem("qk_hi_ready"), sem("qk_ready")
        score_done, max_ready, exp_ready, diff_ready = (sem(n) for n in (
            "score_done", "max_ready", "exp_ready", "diff_ready"))
        pt_done, pt_hi, pt_ready, pv_done = sem("pt_done"), sem("pt_hi_ready"), sem("pt_ready"), sem("pv_done")
        o_sq, o_stat, o_rstd, o_f32, o_hi, o_ready = (sem(n) for n in (
            "o_squared", "o_summed", "o_rstd", "o_scaled", "o_hi_ready", "o_ready"))
        conv0, conv_ready, c_hi_ready, c_ready2 = sem("conv0"), sem("conv_ready"), sem("c_hi_ready"), sem("c_split")
        logit_done, r_ready, i_ready, ix_ready = sem("logit_done"), sem("r_ready"), sem("i_ready"), sem("ix_ready")
        gelu_ready, tanh_ready, a_ready, d_ready, sqrt_ready, rnn_f32, rnn_hi, rnn_ready = (sem(n) for n in (
            "gelu_ready", "tanh_ready", "decay_ready", "drive_ready", "sqrt_ready", "rnn_f32", "rnn_hi_ready",
            "rnn_ready"))
        act_chain, dve_chain, pool_chain = (Chain(sem(n)) for n in ("act_chain", "dve_chain", "pool_chain"))

        def f(ap):
            return ap.bitcast(F32)

        gate_v = [w.rearrange("l (k p) n -> p (l k) n", p=P) for w in (ffn1_w_gate, ffn2_w_gate)]
        up_v = [w.rearrange("l (k p) n -> p (l k) n", p=P) for w in (ffn1_w_up, ffn2_w_up)]
        down_v = [w.rearrange("l (k p) n -> p (l k) n", p=P) for w in (ffn1_w_down, ffn2_w_down)]
        ada_v = w_ada.rearrange("l (k p) n -> p (l k) n", p=P)
        in_v = w_in.rearrange("l (k p) n -> p (l k) n", p=P)
        out_v = w_out.rearrange("l (k p) n -> p (l k) n", p=P)
        x_v = x.rearrange("b (t p) d -> p (b t) d", p=P)
        y_v = out.rearrange("b (t p) d -> p (b t) d", p=P)
        IN_COLS = [2 * DA, 2 * DA + 256, 0, DA, 256, DA + 256, 4 * DA, 4 * DA + 256, 3 * DA, 3 * DA + 256]
        QK = {4: (0, 0), 5: (0, 1), 6: (1, 0), 7: (1, 1), 8: (0, 2), 9: (0, 3), 10: (1, 2), 11: (1, 3)}
        QK_BY_HEAD = {h: [n for n, s in enumerate(sorted(QK)) if QK[s][1] == h] for h in range(NH)}
        XR0, GATE0 = 12, 16

        def tile_bank(s):
            return s % 3 if s < XR0 else s % 2

        UNITS = {2 * 8 + 6 * h + (0, 1, 2, 4)[b]: (h, b) for h in range(NH) for b in range(TT)}
        UNIT_NO = {u: n for n, u in enumerate(UNITS[k] for k in sorted(UNITS))}
        HEAD_END = {16 + 6 * h + 4: h for h in range(NH)}
        LAST = 2 * N_IN + 6

        def raw2(slot, k0, k1, half):
            return raw[:, slot].rearrange("p (k n) -> p k n", n=256)[:, k0:k1, half * P:(half + 1) * P]

        def blk(t, slot, k):
            return t[:, slot, 0:k * P].rearrange("p (k n) -> p k n", n=P)

        block = ctx.enter_context(nc.Block())

        @block.sync
        def _(sp):
            def load(slot, src):
                n = src.shape[1] * src.shape[2]
                dst = raw[:, slot, 0:n].rearrange("p (k n) -> p k n", k=src.shape[1])
                sp.dma_start(dst, src).then_inc(raw_in[slot], 16)

            def load_ada(slot, ch):
                load(slot, ada_v[:, :, bass.ds(ch * 256, 256)])

            for ch in range(8):
                if ch >= 4:
                    sp.wait_ge(ada_done, ch - 3)
                load_ada(ch % 4, ch)
            for slot, w in ((0, gate_v[0]), (1, up_v[0])):
                sp.wait_ge(ada_done, 5 + slot)
                load(slot, w[:, :, 0:256])
            for slot in (2, 3):
                sp.wait_ge(ada_done, 5 + slot)
                load_ada(slot, 6 + slot)
            with sp.Fori(1, PAIRS) as j:
                sp.wait_ge(w_lo_ready, j * 4 - 1)
                load(0, gate_v[0][:, :, bass.ds(j * 256, 256)])
                sp.wait_ge(w_lo_ready, j * 4)
                load(1, up_v[0][:, :, bass.ds(j * 256, 256)])
                sp.wait_ge(ada_done, j * 2 + 7)
                load_ada(2, j * 2 + 8)
                sp.wait_ge(ada_done, j * 2 + 8)
                load_ada(3, j * 2 + 9)

            def down(n, it, waits):
                base = P_DOWN[n]
                for q in range(6):
                    k0, k1 = DOWN_CUTS[q % 3]
                    s, v = waits[q]
                    sp.wait_ge(s, v)
                    load((0, 1, 2, 3, 0, 1)[q], down_v[n][:, k0:k1, bass.ds(it * 512 + 256 * (q // 3), 256)])

            with sp.Fori(0, 2) as it:
                b = P_DOWN[0]
                down(0, it, [(w_lo_ready, it * 12 + (b - 1)), (w_lo_ready, it * 12 + b),
                             (ada_done, it * 2 + 29), (ada_done, it * 2 + 30),
                             (w_lo_ready, it * 12 + (b + 2)), (w_lo_ready, it * 12 + (b + 4))])
                sp.wait_ge(w_lo_ready, it * 12 + (b + 6))
                load_ada(2, it * 2 + 30)
                sp.wait_ge(w_lo_ready, it * 12 + (b + 8))
                load_ada(3, it * 2 + 31)
            for r in range(10):
                sp.wait_ge(w_lo_ready, P_MIX - 2 + 2 * r)
                load(r % 2, in_v[:, :, IN_COLS[r]:IN_COLS[r] + 256])
                if r == 1:
                    for slot in (2, 3):
                        sp.wait_ge(ada_done, 31 + slot)
                        load_ada(slot, 32 + slot)
            for r in range(4):
                sp.wait_ge(w_lo_ready, P_MIX - 2 + 2 * (10 + r))
                load(r % 2, out_v[:, 4 * (r // 2):4 * (r // 2) + 4, 512 * (r % 2):512 * (r % 2) + 512])
            b = P_FFN[1]
            for slot, w in ((0, gate_v[1]), (1, up_v[1])):
                sp.wait_ge(w_lo_ready, b - 2 + 2 * slot)
                load(slot, w[:, :, 0:256])
            sp.wait_ge(rnn_ready, RT)
            with sp.Fori(0, (PAIRS - 1) // 2) as it:
                for e in range(2):
                    sp.wait_ge(w_lo_ready, it * 8 + (b - 1 + 4 * e))
                    load(2 - 2 * e, gate_v[1][:, :, bass.ds(it * 512 + 256 * (1 + e), 256)])
                    sp.wait_ge(w_lo_ready, it * 8 + (b + 4 * e))
                    load(3 - 2 * e, up_v[1][:, :, bass.ds(it * 512 + 256 * (1 + e), 256)])
            with sp.Fori(0, 2) as it:
                b = P_DOWN[1]
                down(1, it, [(w_lo_ready, it * 12 + (b - 1)), (w_lo_ready, it * 12 + b),
                             (w_lo_ready, it * 12 + (b - 5)), (w_lo_ready, it * 12 + (b - 4)),
                             (w_lo_ready, it * 12 + (b + 2)), (w_lo_ready, it * 12 + (b + 4))])
            for dp in range(KD // 2):
                sp.wait_ge(y_out, 2 * (dp + 1))
                sp.dma_start(y_v[:, :, 256 * dp:256 * (dp + 1)], y_nat[:, dp]).then_inc(y_stored, 16)
            sp.wait_ge(y_stored, 16 * (KD // 2))

        @block.gpsimd
        def _(pool):
            pool_chain.link(pool, nc.gpsimd.memset(ident[:], 0.0))
            pool_chain.link(pool, nc.gpsimd.affine_select(
                out=ident[:], in_=ident[:], compare_op=ALU.not_equal, fill=1.0, base=0,
                pattern=[[-1, P]], channel_multiplier=1))
            nc.gpsimd.memset(misc[:, EPS_C:EPS_C + 1], EPS).then_inc(s_const, 1)
            nc.gpsimd.memset(ones[:], 1.0).then_inc(s_const, 1)
            pool.wait_ge(ada_done, 9 * KD // 2)
            nc.gpsimd.iota(dist[:], pattern=[[-1, S]], base=S - P, channel_multiplier=1).then_inc(dist_ready, 1)
            nc.gpsimd.memset(bd[:], 0.0).then_inc(bd_zero, 1)
            pool_chain.link(pool, nc.gpsimd.memset(ones_half[:], 0.0))
            nc.gpsimd.memset(ones_half[0:HD, 0:HD], 1.0).then_inc(bd_zero, 1)
            nc.gpsimd.memset(ones_half[HD:P, HD:P], 1.0).then_inc(bd_zero, 1)
            pool.wait_ge(bd_zero, 3)
            for g, w in enumerate((w_rg_a, w_rg_x)):
                wv = w.rearrange("l (t e) c d -> e c (l t) d", e=2)
                for e in range(2):
                    pool.dma_start(bd[e * HD:(e + 1) * HD, g, :, e * HD:(e + 1) * HD], wv[e]).then_inc(bd_in, 16)

        @block.scalar
        def _(act):
            act.dma_start(tmp[0:KD, 0, 0:P], c.rearrange("b (k p) -> (b k) p", p=P)).then_inc(s_rows, 16)
            act.dma_start(tmp[B_ADA:G_NORM, 0, 0:P], b_ada.rearrange("l (k p) -> (l k) p", p=P)).then_inc(s_rows, 16)
            act.dma_start(tmp[G_NORM:ROWS_A, 0, 0:P],
                          g_norm.rearrange("l s (k p) -> (l s k) p", p=P)).then_inc(s_rows, 16)
            row = 0
            for v in (q_norm_g.rearrange("l m d -> l (m d)"), k_norm_g.rearrange("l m d -> l (m d)"), head_norm_g,
                      conv_w.rearrange("l i (t p) -> (l i t) p", p=P), conv_b.rearrange("l (t p) -> (l t) p", p=P),
                      b_rg_a.rearrange("l (t p) -> (l t) p", p=P), b_rg_x.rearrange("l (t p) -> (l t) p", p=P),
                      lru_lambda.rearrange("l (t p) -> (l t) p", p=P)):
                act.dma_start(tmp[row:row + v.shape[0], 1, 0:P], v).then_inc(s_rows, 16)
                row += v.shape[0]
            for t in range(TT):
                act.dma_start(x_nat[:, t], x_v[:, t]).then_inc(s_x, 16)
            act.dma_start(lam_in[:], lambda_params.to_broadcast([P, 4, HD])).then_inc(s_lam, 16)

            act.wait_ge(cols_ready, 1)
            nc.scalar.activation(cols[:, 0:KD], cols[:, 0:KD], ACT.Silu).then_inc(c_ready, 1)
            for d in range(KD):
                act.wait_ge(xt_done, d + 1)
                nc.scalar.copy(xT[:, d], ps[:, 6 + d % 2])
                if d >= 2:
                    act.wait_ge(sq_added, d - 1)
                nc.scalar.activation(tmp[:, d % 2], ps[:, 6 + d % 2], ACT.Square).then_inc(sq_ready, 1)
            act.wait_ge(lam_dot, 1)
            nc.scalar.activation(misc[:, LAM_E:LAM_E + 2], misc[:, LAM_S:LAM_S + 2], ACT.Exp).then_inc(lam_exp, 1)
            act.wait_ge(sp_exp, 1)
            nc.scalar.activation(misc[:, SPT:SPT + RT], misc[:, SPT:SPT + RT], ACT.Exp, scale=-1.0)\
                .then_inc(lam_exp, 1)

            def hi(n, slot, src, k, width=P, fresh=None, wait=True):
                if wait:
                    act.wait_ge(panel_done, n - 3)
                if fresh is not None:
                    act.wait_ge(raw_in[fresh[0]], fresh[1])
                dst = w_hi[:, slot, 0:k * width].rearrange("p (k n) -> p k n", n=width)
                nc.scalar.copy(dst, src).then_inc(w_hi_ready, 1)

            def rough_rstd(n):
                act.wait_ge(var_ready, n + 1)
                act_chain.link(act, nc.scalar.activation(misc[:, RSTD:RSTD + TT], misc[:, VAR:VAR + TT], ACT.Ln))
                nc.scalar.activation(misc[:, RSTD:RSTD + TT], misc[:, RSTD:RSTD + TT], ACT.Exp, scale=-0.5)\
                    .then_inc(rough_ready, 1)

            def modulate(n):
                for d in range(KD):
                    act.wait_ge(norm_ready, n * KD + d + 1)
                    nc.scalar.activation(h_hi[:, d], tmp[:, d % 2], ACT.Identity,
                                         bias=cols[:, mod(3 * n, d):mod(3 * n, d) + 1]).then_inc(h_hi_ready, 1)

            def square(d, upd):
                act.wait_ge(x_updated, upd + 1)
                nc.scalar.activation(tmp[:, d % 2], xT[:, d], ACT.Square).then_inc(sq_ready, 1)

            def hidden(j, jl, n):
                act.wait_ge(panel_done, j * 2 + (P_FFN[n] + 2))
                act.wait_ge(split_done, j + (SPLIT_FFN[n] - 1))
                nc.scalar.activation(tmp[:, jl], ps[:, 2 * jl], ACT.Silu).then_inc(silu_ready, 1)
                act.wait_ge(prod_ready, j + (n * FT + 1))
                nc.scalar.copy(a_hi[:, j] if isinstance(j, int) else a_hi[:, bass.ds(j, 1)].rearrange(
                    "p a b -> p (a b)"), tmp[:, jl]).then_inc(a_hi_ready, 1)

            def ffn_panels(n, j, e, slots, ords):
                for g in range(2):
                    hi(j * 4 + (P_FFN[n] + 2 * e + g), 2 * e + g, raw2(slots[g], 0, KD, e), KD,
                       fresh=(slots[g], ords) if e == 0 else None)

            def down_panel(n, it, q):
                r, e = q // 2, q % 2
                slot = (0, 1, 2, 3, 0, 1)[r]
                k0, k1 = DOWN_CUTS[r % 3]
                per = 2
                if n == 0:
                    first = (14, 14, 14, 14, 15, 15)[r]
                else:
                    first, per = (31, 31, 24, 24, 32, 32)[r], (2, 2, 1, 1, 2, 2)[r]
                hi(it * 12 + (P_DOWN[n] + q), q % 4, raw2(slot, 0, k1 - k0, e), k1 - k0,
                   fresh=(slot, it * (16 * per) + 16 * first) if e == 0 else None)

            rough_rstd(0)
            modulate(0)

            for q in range(4):
                hi(q, q, raw2(q % 2, 0, KD, q // 2), KD, fresh=(q % 2, 16 * 3), wait=False)
            with act.Fori(0, PAIRS - 1) as j:
                for e in range(2):
                    ffn_panels(0, j + 1, e, (0, 1), j * 16 + 16 * 4)
                    hidden(j * 2 + e, e, 0)
            for e in range(2):
                down_panel(0, 0, 2 * e)
                down_panel(0, 0, 2 * e + 1)
                hidden(2 * (PAIRS - 1) + e, e, 0)

            def down_body(n, it, nxt, base):
                for half in range(2):
                    down_panel(n, it, 6 * half + 4)
                    down_panel(n, it, 6 * half + 5)
                    if half == 0:
                        for q in range(6, 10):
                            down_panel(n, it, q)
                    else:
                        nxt()
                    if n == 0:
                        for d in range(2):
                            square(2 * half + d, it * 4 + (base + 2 * half + d))

            def down1(it):
                pass

            def square_at(off, it, par, base):
                act.wait_ge(x_updated, it * 4 + (base + off + 1))
                src = xT[:, bass.ds(it * 4 + off, 1)].rearrange("p a b -> p (a b)")
                nc.scalar.activation(tmp[:, par], src, ACT.Square).then_inc(sq_ready, 1)

            def down_iteration(n, it, nxt):
                for half in range(2):
                    down_panel(n, it, 6 * half + 4)
                    down_panel(n, it, 6 * half + 5)
                    if half == 0:
                        for q in range(6, 10):
                            down_panel(n, it, q)
                    else:
                        nxt(it)
                    for e in range(2):
                        if n == 0:
                            act.wait_ge(sq_added, it * 4 + (KD + 2 * half - 1 + e))
                            square_at(2 * half + e, it, e, 0)

            for it in range(1):
                down_iteration(0, it, lambda i: [down_panel(0, i + 1, q) for q in range(4)])

            def first_mix(_):
                for q in range(4):
                    hi(P_MIX + q, q, raw[:, q // 2, 1024 * (q % 2):1024 * (q % 2 + 1)]
                       .rearrange("p (k n) -> p k n", n=256), 4, 256,
                       fresh=(q // 2, 16 * 18) if q % 2 == 0 else None)

            down_iteration(0, 1, first_mix)
            rough_rstd(1)
            modulate(1)

            act.wait_ge(bd_in, 64)
            nc.scalar.copy(bd_hi[:], bd[:]).then_inc(bd_hi_ready, 1)

            def mix_panel(m):
                if m < N_IN:
                    hi(P_MIX + m, m % 4, raw2((m // 2) % 2, 0, KD, m % 2), KD,
                       fresh=((m // 2) % 2, 16 * (18 + m // 4)) if m % 2 == 0 else None)
                else:
                    src = raw[:, (m // 2) % 2].rearrange("p (k n) -> p k n", n=512)[:, :, 256 * (m % 2):256 * (m % 2 + 1)]
                    hi(P_MIX + m, m % 4, src, 4, 256,
                       fresh=((m // 2) % 2, 16 * (18 + m // 4)) if m % 2 == 0 else None)

            def panels_at(s):
                return {2: (4, 5), 4: (6, 7)}.get(s, (s + 3,) if s >= 5 else ())

            for xh in range(LAST):
                s = xh // 2
                if 28 <= xh < 28 + 2 * RT + 1:
                    if xh % 2 == 0 and xh < 28 + 2 * RT:
                        n = (xh - 28) // 2
                        act.wait_ge(logit_done, 2 * n + 1)
                        nc.scalar.activation(decay[:, n], ps[:, 2], ACT.Sigmoid,
                                             bias=cols[:, B_A + n:B_A + n + 1]).then_inc(r_ready, 1)
                    if xh % 2 == 1:
                        n = (xh - 29) // 2
                        act.wait_ge(logit_done, 2 * n + 2)
                        nc.scalar.activation(ps[:, 2], ps[:, 2], ACT.Sigmoid,
                                             bias=cols[:, B_X + n:B_X + n + 1]).then_inc(i_ready, 1)
                if xh % 2 == 0 and xh > 0 and s <= N_IN:
                    for m in panels_at(s):
                        mix_panel(m)
                    t = s - 1
                    bank = ps[:, tile_bank(t)]
                    if t in (0, 2):
                        act.wait_ge(v_half_done, t // 2 + 1)
                    else:
                        act.wait_ge(panel_done, P_MIX + t + 1)
                    if t < 4:
                        tok = 2 * (t % 2)
                        nc.scalar.copy(v_hi[:, tok:tok + 2, 256 * (t // 2):256 * (t // 2) + 256],
                                       bank.rearrange("p (t n) -> p t n", t=2)).then_inc(v_hi_ready, 1)
                    elif t in QK:
                        n = t - 4
                        if n:
                            act.wait_ge(sth_done, n)
                        nc.scalar.activation(tmp[:, 0], bank, ACT.Square).then_inc(sqh_ready, 1)
                    elif t < GATE0:
                        n = t - XR0
                        nc.scalar.activation(xr[:, n], bank, ACT.Identity,
                                             scale=cols[:, CONV_W + 3 * RT + n:CONV_W + 3 * RT + n + 1],
                                             bias=cols[:, CONV_B + n:CONV_B + n + 1]).then_inc(conv0, 1)
                        act.wait_ge(conv_ready, n + 1)
                        if n >= 2:
                            act.wait_ge(logit_done, 2 * n - 2)
                        nc.scalar.copy(c_hi[n % 2][:], xr[:, n]).then_inc(c_hi_ready, 1)
                    else:
                        n = t - GATE0
                        if n == 2:
                            act.wait_ge(logit_done, 2 * RT)
                        nc.scalar.activation(gate[:, n], bank, ACT.Gelu_apprx_tanh).then_inc(gelu_ready, 1)
                if xh % 2 and (s - 1) in QK:
                    n = s - 5
                    act.wait_ge(sth_done, n + 1)
                    if n:
                        act.wait_ge(qk_f32, n)
                    act_chain.link(act, nc.scalar.activation(acc[:], ps[:, 7], ACT.Ln, scale=1.0 / HD,
                                                             bias=misc[:, EPS_C:EPS_C + 1]))
                    nc.scalar.activation(acc[:], acc[:], ACT.Exp, scale=-0.5).then_inc(ln_ready, 1)
                    act.wait_ge(qk_f32, n + 1)
                    w, h = QK[s - 1]
                    nc.scalar.copy((q_hi, k_hi)[w][:, h], tmp[:, 1]).then_inc(qk_hi, 1)
                if xh - 5 in HEAD_END:
                    h = HEAD_END[xh - 5]
                    act.wait_ge(o_stat, h + 1)
                    act_chain.link(act, nc.scalar.activation(acc[:], ps[:, 7], ACT.Ln, scale=1.0 / P,
                                                             bias=misc[:, EPS_C:EPS_C + 1]))
                    nc.scalar.activation(acc[:], acc[:], ACT.Exp, scale=-0.5).then_inc(o_rstd, 1)
                    act.wait_ge(o_f32, h + 1)
                    nc.scalar.copy(q_hi[:, h], tmp[:, 1]).then_inc(o_hi, 1)
                if xh - 2 in UNITS:
                    h, b = UNITS[xh - 2]
                    u = UNIT_NO[h, b]
                    act.wait_ge(pt_done, u + 1)
                    if u:
                        act.wait_ge(pv_done, u)
                    nc.scalar.copy(p_hi[:, 0:b + 1], ps[:, 5, 0:(b + 1) * P].rearrange("p (k n) -> p k n", n=P))\
                        .then_inc(pt_hi, 1)
                if xh in UNITS:
                    h, b = UNITS[xh]
                    u = UNIT_NO[h, b]
                    W, mc = (b + 1) * P, MX[u % 2]
                    act.wait_ge(max_ready, u + 1)
                    for m in range(2):
                        e = nc.scalar.activation(prob[:, u % 2, m, 0:W], prob[:, u % 2, m, 0:W], ACT.Exp,
                                                 bias=misc[:, mc + 2 + m:mc + 3 + m],
                                                 accum_out=misc[:, mc + 4 + m:mc + 5 + m])
                        e.then_inc(exp_ready, 1)
                if xh - 4 in HEAD_END:
                    h = HEAD_END[xh - 4]
                    act.wait_ge(pv_done, 4 * (h + 1))
                    if h == 0:
                        act.wait_ge(sth_done, len(QK))
                    nc.scalar.activation(tmp[:, 0], ps[:, 6], ACT.Square).then_inc(o_sq, 1)
                if xh == 2 * N_IN:
                    act.wait_ge(panel_done, P_MIX + N_IN)
                    for n in range(RT):
                        nc.scalar.activation(tanh_z[:, n], decay[:, n], ACT.Tanh,
                                             scale=misc[:, SP8 + n:SP8 + n + 1]).then_inc(tanh_ready, 1)
                        act.wait_ge(tanh_ready, n + 1)
                        nc.scalar.activation(decay[:, n], decay[:, n], ACT.Exp,
                                             scale=misc[:, NSP8 + n:NSP8 + n + 1]).then_inc(a_ready, 1)
            for n in range(RT):
                act.wait_ge(d_ready, n + 1)
                nc.scalar.activation(drive[:, n], drive[:, n], ACT.Sqrt).then_inc(sqrt_ready, 1)
            for n in range(RT):
                act.wait_ge(rnn_f32, n + 1)
                nc.scalar.copy(k_hi[:, n], gate[:, n]).then_inc(rnn_hi, 1)
                mix_panel(N_IN + 4 + n)
            for q in range(4):
                hi(P_FFN[1] + q, q, raw2(q % 2, 0, KD, q // 2), KD, fresh=(q % 2, 16 * 25))
                for e in range(2):
                    act.wait_ge(sq_added, 2 * KD + 2 * q - 1 + e)
                    square(2 * q + e, KD + 2 * q + e)
            rough_rstd(2)
            modulate(2)

            with act.Fori(0, (PAIRS - 1) // 2) as it:
                for m in range(2):
                    for e in range(2):
                        ffn_panels(1, it * 2 + (1 + m), e, ((2, 3), (0, 1))[m],
                                   it * 16 + 16 * (19, 26)[m])
                        hidden(it * 4 + (2 * m + e), e, 1)
            for e in range(2):
                down_panel(1, 0, 2 * e)
                down_panel(1, 0, 2 * e + 1)
                hidden(2 * (PAIRS - 1) + e, e, 1)

            def evict(d):
                act.wait_ge(y_done, d + 1)
                nc.scalar.copy(y_nat[:, d // 2, :, P * (d % 2):P * (d % 2 + 1)],
                               ps[:, 6 + d % 2].rearrange("p (t n) -> p t n", t=TT)).then_inc(y_out, 1)

            for q in range(4, 12):
                down_panel(1, 0, q)
            for q in range(4):
                down_panel(1, 1, q)
            evict(0)
            evict(1)
            for q in range(4, 10):
                down_panel(1, 1, q)
            evict(2)
            evict(3)
            for q in range(10, 12):
                down_panel(1, 1, q)
            for d in range(4, KD):
                evict(d)

        @block.vector
        def _(dve):
            link = lambda ins: dve_chain.link(dve, ins)

            dve.wait_ge(rows_done, 1)
            nc.vector.tensor_copy(cols[:], ps[:, 6, 0:NCOLS]).then_inc(cols_ready, 1)
            dve.wait_ge(cols_ready, 1)
            dve.wait_ge(s_lam, 16)
            for m in range(2):
                i = nc.vector.tensor_tensor_reduce(out=lam_pr[:, m], in0=lam_in[:, 2 * m], in1=lam_in[:, 2 * m + 1],
                                                   scale=1.0, scalar=0.0, op0=ALU.mult, op1=ALU.add,
                                                   accum_out=misc[:, LAM_S + m:LAM_S + m + 1])
            i.then_inc(lam_dot, 1)
            nc.vector.scalar_tensor_tensor(out=misc[:, SPT:SPT + RT], in0=cols[:, LRU:LRU + RT], scalar=-1.0,
                                           in1=cols[:, LRU:LRU + RT], op0=ALU.mult, op1=ALU.max).then_inc(sp_exp, 1)
            link(nc.vector.memset(acc[:], 0.0))

            def ada_chunk(slot, ordv):
                dve.wait_ge(raw_in[slot], ordv)
                r = raw[:, slot].rearrange("p (k n) -> p k n", n=256)
                link(nc.vector.tensor_scalar(r[:, 0], r[:, 0], cols[:, 0:1], None, ALU.mult))
                for k in range(1, KD):
                    i = nc.vector.scalar_tensor_tensor(out=r[:, 0], in0=r[:, k], scalar=cols[:, k:k + 1],
                                                       in1=r[:, 0], op0=ALU.mult, op1=ALU.add)
                    if k < KD - 1:
                        link(i)
                i.then_inc(ada_sum, 1)

            dve.wait_ge(c_ready, 1)
            for d in range(KD):
                ada_chunk(d % 4, 16 * (1 + d // 4))
                dve.wait_ge(sq_ready, d + 1)
                nc.vector.tensor_tensor(acc[:], acc[:], tmp[:, d % 2], ALU.add).then_inc(sq_added, 1)
                dve.wait_ge(sq_added, d + 1)

            def variance(n):
                dve.wait_ge(stat_done, n + 1)
                v, y, t = (misc[:, q:q + TT] for q in (VAR, RSTD, NEWT))
                nc.vector.tensor_scalar(v, ps[:, 5, 0:TT], 1.0 / D, EPS, ALU.mult, ALU.add).then_inc(var_ready, 1)
                dve.wait_ge(rough_ready, n + 1)
                link(nc.vector.tensor_tensor(t, y, y, ALU.mult))
                link(nc.vector.tensor_tensor(t, t, v, ALU.mult))
                link(nc.vector.tensor_scalar(t, t, -0.5, 1.5, ALU.mult, ALU.add))
                link(nc.vector.tensor_tensor(y, y, t, ALU.mult))
                for q in range(TT):
                    i = nc.vector.tensor_scalar(acc[:, q * P:(q + 1) * P], ident[:], misc[:, RSTD + q:RSTD + q + 1],
                                                None, ALU.mult)
                i.then_inc(diag_ready, 1)

            def modulate(n):
                dve.wait_ge(rstd_done, n + 1)

                def scaled(d):
                    if d >= 2:
                        dve.wait_ge(split_done, n * KD + (FT if n else 0) + d - 1)
                    nc.vector.scalar_tensor_tensor(
                        out=tmp[:, d % 2], in0=xT[:, d], scalar=cols[:, mod(3 * n + 1, d):mod(3 * n + 1, d) + 1],
                        in1=ps[:, 5], op0=ALU.mult, op1=ALU.mult).then_inc(norm_ready, 1)

                scaled(0)
                for d in range(KD):
                    if d + 1 < KD:
                        scaled(d + 1)
                    dve.wait_ge(h_hi_ready, n * KD + d + 1)
                    nc.vector.scalar_tensor_tensor(
                        out=h_lo[:, d], in0=tmp[:, d % 2], scalar=cols[:, mod(3 * n, d):mod(3 * n, d) + 1],
                        in1=f(h_hi[:, d]), op0=ALU.add, op1=ALU.subtract).then_inc(split_done, 1)

            def gain(n):
                m = cols[:, mod(3 * n + 1):mod(3 * n + 1) + KD]
                link(nc.vector.scalar_tensor_tensor(out=m, in0=m, scalar=1.0,
                                                    in1=cols[:, G_NORM + n * KD:G_NORM + (n + 1) * KD],
                                                    op0=ALU.add, op1=ALU.mult))

            dve.wait_ge(ada_done, 8)
            link(nc.vector.tensor_tensor(cols[:, mod(0):mod(2)], cols[:, mod(0):mod(2)], ps[:, 4, 0:2 * KD], ALU.add))
            gain(0)
            dve.wait_ge(lam_exp, 2)
            link(nc.vector.tensor_tensor(misc[:, NEG_LAM:NEG_LAM + 1], misc[:, LAM_E + 1:LAM_E + 2],
                                         misc[:, LAM_E:LAM_E + 1], ALU.subtract))
            link(nc.vector.tensor_scalar(misc[:, NEG_LAM:NEG_LAM + 1], misc[:, NEG_LAM:NEG_LAM + 1], -LAM_INIT,
                                         None, ALU.add))
            link(nc.vector.tensor_scalar(misc[:, HG8:HG8 + 1], cols[:, H_G:H_G + 1], 1.0 - LAM_INIT, None, ALU.mult))
            e_, s_, q_, a_ = (misc[:, SPT + RT * i:SPT + RT * (i + 1)] for i in range(4))
            link(nc.vector.tensor_scalar(s_, e_, 2.0, None, ALU.add))
            link(nc.vector.reciprocal(q_, s_))
            link(nc.vector.tensor_tensor(s_, e_, q_, ALU.mult))
            link(nc.vector.tensor_tensor(q_, s_, s_, ALU.mult))
            link(nc.vector.memset(a_, 1.0 / 19.0))
            for i in range(17, 0, -2):
                link(nc.vector.tensor_tensor(a_, a_, q_, ALU.mult))
                link(nc.vector.tensor_scalar(a_, a_, 1.0 / i, None, ALU.add))
            link(nc.vector.tensor_tensor(a_, a_, s_, ALU.mult))
            link(nc.vector.tensor_scalar(q_, cols[:, LRU:LRU + RT], -1.0, 0.0, ALU.mult, ALU.max))
            link(nc.vector.scalar_tensor_tensor(out=q_, in0=a_, scalar=2.0, in1=q_, op0=ALU.mult, op1=ALU.add))
            link(nc.vector.tensor_scalar(misc[:, SP8:SP8 + RT], q_, RGLRU_C, None, ALU.mult))
            link(nc.vector.tensor_scalar(misc[:, NSP8:NSP8 + RT], q_, -RGLRU_C, None, ALU.mult))
            variance(0)
            modulate(0)

            def lo(n, slot, src, k, width=P):
                dve.wait_ge(w_hi_ready, n + 1)
                h_, l_ = (t[:, slot, 0:k * width].rearrange("p (k n) -> p k n", n=width) for t in (w_hi, w_lo))
                nc.vector.tensor_tensor(l_, src, f(h_), ALU.subtract).then_inc(w_lo_ready, 1)

            def hidden(j, jl, n):
                dve.wait_ge(silu_ready, j + (n * FT + 1))
                nc.vector.tensor_tensor(tmp[:, jl], tmp[:, jl], ps[:, 2 * jl + 1], ALU.mult).then_inc(prod_ready, 1)
                at_j = (lambda t: t[:, j]) if isinstance(j, int) else (
                    lambda t: t[:, bass.ds(j, 1)].rearrange("p a b -> p (a b)"))
                dve.wait_ge(a_hi_ready, j + (n * FT + 1))
                nc.vector.tensor_tensor(at_j(a_lo), tmp[:, jl], f(at_j(a_hi)), ALU.subtract).then_inc(split_done, 1)

            def ffn_panels(n, j, e, slots):
                for g in range(2):
                    lo(j * 4 + (P_FFN[n] + 2 * e + g), 2 * e + g, raw2(slots[g], 0, KD, e), KD)

            def down_panel(n, it, q):
                r, e = q // 2, q % 2
                k0, k1 = DOWN_CUTS[r % 3]
                lo(it * 12 + (P_DOWN[n] + q), q % 4, raw2((0, 1, 2, 3, 0, 1)[r], 0, k1 - k0, e), k1 - k0)

            def mod_cols(first, count, done):
                dve.wait_ge(ada_done, done)
                m = cols[:, bass.ds(first, count)]
                link(nc.vector.tensor_tensor(m, m, ps[:, 4, 0:count], ALU.add))

            for q in range(4):
                lo(q, q, raw2(q % 2, 0, KD, q // 2), KD)
            LINKS = 2 * (KD - 1) + 1
            base = dve_chain.at
            with dve.Fori(0, PAIRS - 1) as j:
                dve_chain.at = j * LINKS + base
                for e in range(2):
                    ada_chunk(2 + e, j * 16 + 48)
                    ffn_panels(0, j + 1, e, (0, 1))
                    hidden(j * 2 + e, e, 0)
                mod_cols(j * 4 + mod(2), 4, j * 2 + 10)
            dve_chain.at = base + LINKS * (PAIRS - 1)
            for e in range(2):
                ada_chunk(2 + e, 16 * (3 + PAIRS - 1))
                down_panel(0, 0, 2 * e)
                down_panel(0, 0, 2 * e + 1)
                hidden(2 * (PAIRS - 1) + e, e, 0)
            mod_cols(mod(2) + 4 * (PAIRS - 1), 4, 8 + 2 * PAIRS)
            m = cols[:, mod(2):mod(2) + KD]
            link(nc.vector.tensor_scalar(m, m, 0.5, None, ALU.mult))
            gain(1)
            link(nc.vector.memset(acc[:], 0.0))

            def update(off, it, bank, n, panel, upd):
                dve.wait_ge(panel_done, panel)
                if isinstance(it, int):
                    xb, g = xT[:, it * 4 + off], cols[:, mod(3 * n + 2, it * 4 + off):mod(3 * n + 2, it * 4 + off) + 1]
                else:
                    xb = xT[:, bass.ds(it * 4 + off, 1)].rearrange("p a b -> p (a b)")
                    g = cols[:, bass.ds(it * 4 + (mod(3 * n + 2) + off), 1)]
                nc.vector.scalar_tensor_tensor(out=xb, in0=ps[:, bank], scalar=g, in1=xb,
                                               op0=ALU.mult, op1=ALU.add).then_inc(x_updated, 1)

            def add_square(par, value):
                dve.wait_ge(sq_ready, value)
                nc.vector.tensor_tensor(acc[:], acc[:], tmp[:, par], ALU.add).then_inc(sq_added, 1)
                dve.wait_ge(sq_added, value)

            def down1_iteration(it, nxt):
                for half in range(2):
                    down_panel(0, it, 6 * half + 4)
                    down_panel(0, it, 6 * half + 5)
                    if half == 0:
                        for q in range(6, 10):
                            down_panel(0, it, q)
                    else:
                        for e in range(2):
                            ada_chunk(2 + e, it * 32 + 16 * 15)
                        nxt(it)
                    for e in range(2):
                        update(2 * half + e, it, 2 * half + e, 0, it * 12 + (P_DOWN[0] + 6 * half + 6), None)
                    for e in range(2):
                        add_square(e, it * 4 + (KD + 2 * half + e + 1))
                mod_cols(it * 4 + (mod(2) + 4 * PAIRS), 4, it * 2 + (8 + 2 * PAIRS + 2))

            down1_iteration(0, lambda i: [down_panel(0, 1, q) for q in range(4)])

            def first_mix(_):
                for q in range(4):
                    lo(P_MIX + q, q, raw[:, q // 2, 1024 * (q % 2):1024 * (q % 2 + 1)]
                       .rearrange("p (k n) -> p k n", n=256), 4, 256)

            down1_iteration(1, first_mix)
            variance(1)
            modulate(1)

            for e in range(2):
                ada_chunk(2 + e, 16 * 18)
            mod_cols(mod(2) + 4 * PAIRS + 8, 4, 9 * KD // 2)
            gain(2)
            m = cols[:, mod(8):mod(8) + KD]
            link(nc.vector.tensor_scalar(m, m, 0.5, None, ALU.mult))
            dve.wait_ge(dist_ready, 1)
            for h in range(NH):
                slope = 2.0 ** (-8.0 * (h + 1) / NH) * HD ** 0.5
                link(nc.vector.tensor_scalar(alibi[:, h], dist[:], slope, None, ALU.mult))
                i = nc.vector.scalar_tensor_tensor(out=alibi[:, h], in0=dist[:], scalar=-slope, in1=alibi[:, h],
                                                   op0=ALU.mult, op1=ALU.min)
            link(i)
            nc.vector.memset(alibi[0:CHUNK, :, S - CHUNK:S], MASKED).then_inc(alibi_ready, 1)
            dve.wait_ge(bd_hi_ready, 1)
            nc.vector.tensor_tensor(bd_lo[:], bd[:], f(bd_hi[:]), ALU.subtract).then_inc(bd_ready, 1)

            def mix_panel(m):
                if m < N_IN:
                    lo(P_MIX + m, m % 4, raw2((m // 2) % 2, 0, KD, m % 2), KD)
                else:
                    src = raw[:, (m // 2) % 2].rearrange("p (k n) -> p k n", n=512)[:, :, 256 * (m % 2):256 * (m % 2 + 1)]
                    lo(P_MIX + m, m % 4, src, 4, 256)

            def panels_at(s):
                return {2: (4, 5), 4: (6, 7)}.get(s, (s + 3,) if s >= 5 else ())

            for xh in range(LAST):
                s = xh // 2
                if xh % 2 == 0 and xh > 0 and s <= N_IN:
                    for m in panels_at(s):
                        mix_panel(m)
                    t = s - 1
                    bank = ps[:, tile_bank(t)]
                    if t < 4:
                        tok = 2 * (t % 2)
                        sl = (slice(None), slice(tok, tok + 2), slice(256 * (t // 2), 256 * (t // 2) + 256))
                        dve.wait_ge(v_hi_ready, t + 1)
                        nc.vector.tensor_tensor(v_lo[sl], bank.rearrange("p (t n) -> p t n", t=2), f(v_hi[sl]),
                                                ALU.subtract).then_inc(tile_free, 1)
                    elif XR0 <= t < GATE0:
                        n = t - XR0
                        dve.wait_ge(conv0, n + 1)
                        for lag in range(1, CW):
                            w = CONV_W + (CW - 1 - lag) * RT + n
                            i = nc.vector.scalar_tensor_tensor(
                                out=xr[:, n, lag:S], in0=bank[:, 0:S - lag], scalar=cols[:, w:w + 1],
                                in1=xr[:, n, lag:S], op0=ALU.mult, op1=ALU.add)
                            if lag < CW - 1:
                                link(i)
                        i.then_inc(conv_ready, 1)
                        dve.wait_ge(c_hi_ready, n + 1)
                        nc.vector.tensor_tensor(c_lo[n % 2][:], xr[:, n], f(c_hi[n % 2][:]), ALU.subtract).then_inc(tile_free, 1)
                if xh % 2 and (s - 1) in QK:
                    n, (w, h) = s - 5, QK[s - 1]
                    bank = ps[:, tile_bank(s - 1)]
                    g = (Q_G, K_G)[w]
                    y, t = acc[:], tmp[:, 1]
                    dve.wait_ge(ln_ready, n + 1)
                    if n:
                        dve.wait_ge(qk_ready, n)
                    link(nc.vector.tensor_tensor(t, y, y, ALU.mult))
                    link(nc.vector.scalar_tensor_tensor(out=t, in0=ps[:, 7], scalar=EPS * HD, in1=t,
                                                        op0=ALU.add, op1=ALU.mult))
                    link(nc.vector.tensor_scalar(t, t, -0.5 / HD, 1.5, ALU.mult, ALU.add))
                    link(nc.vector.tensor_tensor(y, y, t, ALU.mult))
                    nc.vector.scalar_tensor_tensor(out=t, in0=bank, scalar=cols[:, g:g + 1], in1=y,
                                                   op0=ALU.mult, op1=ALU.mult).then_inc(qk_f32, 1)
                    dve.wait_ge(qk_hi, n + 1)
                    nc.vector.tensor_tensor((q_lo, k_lo)[w][:, h], t, f((q_hi, k_hi)[w][:, h]), ALU.subtract)\
                        .then_inc(qk_ready, 1)
                if xh - 5 in HEAD_END:
                    h = HEAD_END[xh - 5]
                    dve.wait_ge(o_rstd, h + 1)
                    dve.wait_ge(qk_ready, len(QK))
                    if h:
                        dve.wait_ge(o_ready, h)
                    nc.vector.scalar_tensor_tensor(out=tmp[:, 1], in0=ps[:, 6], scalar=misc[:, HG8:HG8 + 1],
                                                   in1=acc[:], op0=ALU.mult, op1=ALU.mult).then_inc(o_f32, 1)
                    dve.wait_ge(o_hi, h + 1)
                    nc.vector.tensor_tensor(q_lo[:, h], tmp[:, 1], f(q_hi[:, h]), ALU.subtract).then_inc(o_ready, 1)
                if xh - 1 in UNITS:
                    h, b = UNITS[xh - 1]
                    u = UNIT_NO[h, b]
                    W, mc = (b + 1) * P, MX[u % 2]
                    dve.wait_ge(exp_ready, 2 * u + 2)
                    link(nc.vector.reciprocal(misc[:, mc + 6:mc + 8], misc[:, mc + 4:mc + 6]))
                    link(nc.vector.tensor_tensor(misc[:, mc + 8:mc + 9], misc[:, mc + 7:mc + 8],
                                                 misc[:, NEG_LAM:NEG_LAM + 1], ALU.mult))
                    p0, p1 = prob[:, u % 2, 0, 0:W], prob[:, u % 2, 1, 0:W]
                    link(nc.vector.tensor_scalar(p1, p1, misc[:, mc + 8:mc + 9], None, ALU.mult))
                    nc.vector.scalar_tensor_tensor(out=p0, in0=p0, scalar=misc[:, mc + 6:mc + 7], in1=p1,
                                                   op0=ALU.mult, op1=ALU.add).then_inc(diff_ready, 1)
                if xh - 2 in UNITS:
                    h, b = UNITS[xh - 2]
                    u = UNIT_NO[h, b]
                    dve.wait_ge(pt_hi, u + 1)
                    nc.vector.tensor_tensor(p_lo[:, 0:b + 1], ps[:, 5, 0:(b + 1) * P].rearrange("p (k n) -> p k n", n=P),
                                            f(p_hi[:, 0:b + 1]), ALU.subtract).then_inc(pt_ready, 1)
                if xh in UNITS:
                    h, b = UNITS[xh]
                    u = UNIT_NO[h, b]
                    W, mc = (b + 1) * P, MX[u % 2]
                    if u == 0:
                        dve.wait_ge(alibi_ready, 1)
                    if u >= 2:
                        dve.wait_ge(pt_done, u - 1)
                    dve.wait_ge(score_done, u + 1)
                    for m in range(2):
                        i = nc.vector.tensor_tensor_reduce(
                            out=prob[:, u % 2, m, 0:W], in0=ps[:, 3 + m, 0:W], in1=alibi[:, h, S - W:S],
                            scale=HD ** -0.5, scalar=-3e38, op0=ALU.add, op1=ALU.max,
                            accum_out=misc[:, mc + m:mc + m + 1])
                    link(i)
                    nc.vector.tensor_scalar(misc[:, mc + 2:mc + 4], misc[:, mc:mc + 2], -1.0, None, ALU.mult)\
                        .then_inc(max_ready, 1)
                if 29 <= xh < 29 + 2 * RT and xh % 2:
                    n = (xh - 29) // 2
                    dve.wait_ge(i_ready, n + 1)
                    nc.vector.tensor_tensor(xr[:, n], xr[:, n], ps[:, 2], ALU.mult).then_inc(ix_ready, 1)
                if xh in (2 * N_IN, 2 * N_IN + 1):
                    for n in ((0, 1), (2, 3))[xh - 2 * N_IN]:
                        dve.wait_ge(a_ready, n + 1)
                        link(nc.vector.tensor_tensor(drive[:, n], decay[:, n], decay[:, n], ALU.mult))
                        nc.vector.scalar_tensor_tensor(out=drive[:, n], in0=drive[:, n], scalar=1.0,
                                                       in1=tanh_z[:, n], op0=ALU.add, op1=ALU.mult).then_inc(d_ready, 1)
            for n in range(RT):
                dve.wait_ge(sqrt_ready, n + 1)
                dve.wait_ge(ix_ready, n + 1)
                link(nc.vector.tensor_tensor(drive[:, n], drive[:, n], xr[:, n], ALU.mult))
                link(nc.vector.tensor_tensor_scan(xr[:, n], decay[:, n], drive[:, n], 0.0, ALU.mult, ALU.add))
                dve.wait_ge(gelu_ready, n + 1)
                nc.vector.tensor_tensor(gate[:, n], gate[:, n], xr[:, n], ALU.mult).then_inc(rnn_f32, 1)
                dve.wait_ge(rnn_hi, n + 1)
                nc.vector.tensor_tensor(k_lo[:, n], gate[:, n], f(k_hi[:, n]), ALU.subtract).then_inc(rnn_ready, 1)
                mix_panel(N_IN + 4 + n)
            link(nc.vector.memset(acc[:], 0.0))
            for q in range(4):
                lo(P_FFN[1] + q, q, raw2(q % 2, 0, KD, q // 2), KD)
                for e in range(2):
                    update(2 * (q % 2) + e, q // 2, 2 * q + e, 1, P_MIX + N_IN + 4 + q + 1, None)
                for e in range(2):
                    add_square(e, 2 * KD + 2 * q + e + 1)
            variance(2)
            modulate(2)

            with dve.Fori(0, (PAIRS - 1) // 2) as it:
                for m in range(2):
                    for e in range(2):
                        ffn_panels(1, it * 2 + (1 + m), e, ((2, 3), (0, 1))[m])
                        hidden(it * 4 + (2 * m + e), e, 1)
            for e in range(2):
                down_panel(1, 0, 2 * e)
                down_panel(1, 0, 2 * e + 1)
                hidden(2 * (PAIRS - 1) + e, e, 1)
            for it in range(2):
                for half in range(2):
                    down_panel(1, it, 6 * half + 4)
                    down_panel(1, it, 6 * half + 5)
                    if half == 0:
                        for q in range(6, 10):
                            down_panel(1, it, q)
                    elif it == 0:
                        for q in range(4):
                            down_panel(1, 1, q)
                    for e in range(2):
                        update(2 * half + e, it, 2 * half + e, 2, it * 12 + (P_DOWN[1] + 6 * half + 6), None)

        @block.tensor
        def _(pe):
            def mm3(o, w, r, first, last):
                nc.tensor.matmul(o, w[0], r[0], start=first, stop=False)
                nc.tensor.matmul(o, w[0], r[1], start=False, stop=False)
                return nc.tensor.matmul(o, w[1], r[0], start=False, stop=last)

            def wblk(slot, k):
                return w_hi[:, slot, k * P:(k + 1) * P], w_lo[:, slot, k * P:(k + 1) * P]

            def ada_cols(slot, n, col):
                pe.wait_ge(ada_sum, n)
                for e in range(2):
                    i = nc.tensor.matmul(ps[:, 4, col + e:col + e + 1], raw[:, slot, e * P:(e + 1) * P],
                                         ones[:, 0:1], start=True, stop=True)
                i.then_inc(ada_done, 1)

            pe.wait_ge(s_const, 2)
            pe.wait_ge(s_rows, 16 * 11)
            nc.tensor.transpose(ps[:, 6, 0:ROWS_A], tmp[0:ROWS_A, 0, 0:P], ident[0:ROWS_A, 0:ROWS_A])
            nb = NCOLS - ROWS_A
            nc.tensor.transpose(ps[:, 6, ROWS_A:NCOLS], tmp[0:nb, 1, 0:P], ident[0:nb, 0:nb]).then_inc(rows_done, 1)
            pe.wait_ge(s_x, 16 * TT)
            pe.wait_ge(cols_ready, 1)
            for d in range(KD):
                if d >= 2:
                    pe.wait_ge(sq_ready, d - 1)
                for t in range(TT):
                    i = nc.tensor.transpose(ps[:, 6 + d % 2, t * P:(t + 1) * P], x_nat[:, t, d * P:(d + 1) * P], ident[:])
                i.then_inc(xt_done, 1)
            for n in range(8):
                ada_cols(n % 4, n + 1, 2 * n)

            def row_stats(n, added):
                pe.wait_ge(sq_added, added)
                if n == 2:
                    pe.wait_ge(x_updated, 2 * KD)
                for t in range(TT):
                    i = nc.tensor.matmul(ps[:, 5, t:t + 1], acc[:, t * P:(t + 1) * P], ones[:, 0:1], start=True, stop=True)
                i.then_inc(stat_done, 1)
                pe.wait_ge(diag_ready, n + 1)
                nc.tensor.matmul(ps[:, 5], ones[:], acc[:], start=True, stop=True).then_inc(rstd_done, 1)

            row_stats(0, KD)

            def hidden_block(n, j, e, first):
                if not first:
                    pe.wait_ge(prod_ready, j + (n * FT - 1))
                for g in range(2):
                    slot = 2 * e + g
                    pe.wait_ge(w_lo_ready, j * 2 + (P_FFN[n] + g + 1))
                    for k in range(KD):
                        if first and e == 0 and g == 0:
                            pe.wait_ge(split_done, SPLIT_FFN[n] - KD + k + 1)
                        i = mm3(ps[:, slot], wblk(slot, k), (h_hi[:, k], h_lo[:, k]), k == 0, k == KD - 1)
                    i.then_inc(panel_done, 1)

            def down_pair(n, it, half):
                for r, (k0, k1) in enumerate(DOWN_CUTS):
                    for e in range(2):
                        q = 6 * half + 2 * r + e
                        pe.wait_ge(w_lo_ready, it * 12 + (P_DOWN[n] + q + 1))
                        if isinstance(it, int) and it == 0 and half == 0:
                            pe.wait_ge(split_done, SPLIT_FFN[n] + k1)
                        for k in range(k0, k1):
                            i = mm3(ps[:, 2 * half + e], wblk(q % 4, k - k0), (a_hi[:, k], a_lo[:, k]),
                                    k == 0, k == FT - 1)
                        i.then_inc(panel_done, 1)

            for e in range(2):
                hidden_block(0, e, e, True)
            ada_cols(2, 9, 0)
            ada_cols(3, 10, 2)
            with pe.Fori(1, PAIRS) as j:
                for e in range(2):
                    hidden_block(0, j * 2 + e, e, False)
                ada_cols(2, j * 2 + 9, 0)
                ada_cols(3, j * 2 + 10, 2)
            for it in range(2):
                for half in range(2):
                    if it == 1:
                        pe.wait_ge(x_updated, 2 * half + 2)
                    elif half == 0:
                        pe.wait_ge(prod_ready, FT - 1)
                    else:
                        pe.wait_ge(prod_ready, FT)
                    down_pair(0, it, half)
                ada_cols(2, 8 + 2 * PAIRS + 2 * it + 1, 0)
                ada_cols(3, 8 + 2 * PAIRS + 2 * it + 2, 2)
            row_stats(1, 2 * KD)

            def spread(xh):
                if xh - 2 in UNITS:
                    h, b = UNITS[xh - 2]
                    u = UNIT_NO[h, b]
                    pe.wait_ge(diff_ready, u + 1)
                    if u:
                        pe.wait_ge(pt_ready, u)
                    for k in range(b + 1):
                        i = nc.tensor.transpose(ps[:, 5, k * P:(k + 1) * P], prob[:, u % 2, 0, k * P:(k + 1) * P], ident[:])
                    i.then_inc(pt_done, 1)
                if xh - 3 in UNITS:
                    h, b = UNITS[xh - 3]
                    u = UNIT_NO[h, b]
                    pe.wait_ge(pt_ready, u + 1)
                    if b == 0 and h:
                        pe.wait_ge(o_f32, h)
                    if u == 0:
                        pe.wait_ge(tile_free, 4)
                    for k in range(b + 1):
                        i = mm3(ps[:, 6, b * P:(b + 1) * P],
                                (v_hi[:, k, h * P:(h + 1) * P], v_lo[:, k, h * P:(h + 1) * P]),
                                (p_hi[:, k], p_lo[:, k]), k == 0, k == b)
                    i.then_inc(pv_done, 1)
                if xh in UNITS:
                    h, b = UNITS[xh]
                    u = UNIT_NO[h, b]
                    if u:
                        pe.wait_ge(max_ready, u)
                    pe.wait_ge(qk_ready, max(QK_BY_HEAD[h]) + 1)
                    for m in range(2):
                        r = slice(m * HD, (m + 1) * HD)
                        i = mm3(ps[:, 3 + m, 0:(b + 1) * P],
                                (q_hi[r, h, b * P:(b + 1) * P], q_lo[r, h, b * P:(b + 1) * P]),
                                (k_hi[r, h, 0:(b + 1) * P], k_lo[r, h, 0:(b + 1) * P]), True, True)
                    i.then_inc(score_done, 1)
                if xh % 2 == 0 and xh // 2 - 1 in QK:
                    n = xh // 2 - 5
                    pe.wait_ge(sqh_ready, n + 1)
                    if n:
                        pe.wait_ge(qk_f32, n)
                    nc.tensor.matmul(ps[:, 7], ones_half[:], tmp[:, 0], start=True, stop=True).then_inc(sth_done, 1)
                if 27 <= xh < 27 + 2 * RT:
                    n, g = (xh - 27) // 2, (xh - 27) % 2
                    pe.wait_ge(tile_free, 4 + n + 1)
                    if g == 0:
                        if n:
                            pe.wait_ge(ix_ready, n)
                        else:
                            pe.wait_ge(bd_ready, 1)
                            pe.wait_ge(qk_f32, 8)
                    else:
                        pe.wait_ge(r_ready, n + 1)
                    mm3(ps[:, 2], (bd_hi[:, g, n], bd_lo[:, g, n]), (c_hi[n % 2][:], c_lo[n % 2][:]), True, True)\
                        .then_inc(logit_done, 1)
                if xh - 4 in HEAD_END:
                    h = HEAD_END[xh - 4]
                    pe.wait_ge(o_sq, h + 1)
                    if h:
                        pe.wait_ge(o_rstd, h)
                    else:
                        pe.wait_ge(qk_f32, len(QK))
                    nc.tensor.matmul(ps[:, 7], ones[:], tmp[:, 0], start=True, stop=True).then_inc(o_stat, 1)

            def c_ready2_of(n):
                return tile_free, 4 + n + 1

            for s in range(N_IN):
                prev = max([q for q in range(s) if tile_bank(q) == tile_bank(s)], default=None)
                if prev is not None:
                    if prev < 4:
                        pe.wait_ge(tile_free, prev + 1)
                    elif prev < XR0:
                        pe.wait_ge(qk_f32, prev - 3)
                    elif prev < GATE0:
                        pe.wait_ge(tile_free, 4 + prev - XR0 + 1)
                    else:
                        pe.wait_ge(gelu_ready, prev - GATE0 + 1)
                bank = ps[:, tile_bank(s)]
                for e in range(2):
                    xh = 2 * s + e
                    if s < 4:
                        t, pair = 2 * (s % 2) + e, 2 * ((s // 2) % 2)
                        pe.wait_ge(w_lo_ready, P_MIX + 2 * (s // 2) + 2)
                        for k in range(KD):
                            if s == 0 and e == 0:
                                pe.wait_ge(split_done, SPLIT_FFN[0] + FT + k + 1)
                            sl, kk = pair + k // 4, k % 4
                            w = [q[:, sl, kk * 256:(kk + 1) * 256] for q in (w_hi, w_lo)]
                            tok = slice(t * P, (t + 1) * P)
                            i = mm3(bank[:, e * 256:(e + 1) * 256], (h_hi[:, k, tok], h_lo[:, k, tok]), w,
                                    k == 0, k == KD - 1)
                        if e == 1 and s % 2:
                            i.then_inc(panel_done, 2)
                        elif e == 1:
                            i.then_inc(v_half_done, 1)
                        if s == 0 and e == 0:
                            ada_cols(2, 35, 0)
                            ada_cols(3, 36, 2)
                    else:
                        pe.wait_ge(w_lo_ready, P_MIX + s + 1)
                        for k in range(4 * e, 4 * e + 4):
                            i = mm3(bank, wblk(s % 4, k), (h_hi[:, k], h_lo[:, k]), k == 0, k == KD - 1)
                        if e == 1:
                            i.then_inc(panel_done, 1)
                    spread(xh)
            for xh in range(2 * N_IN, LAST):
                spread(xh)

            pe.wait_ge(gelu_ready, RT)
            pe.wait_ge(ix_ready, RT)
            pe.wait_ge(max_ready, NH * TT)
            pe.wait_ge(pt_ready, NH * TT)
            for q in range(8):
                pe.wait_ge(w_lo_ready, P_MIX + N_IN + q + 1)
                src = (q_hi, q_lo) if q < 4 else (k_hi, k_lo)
                for e in range(2):
                    for k in range(4):
                        if q in (0, 4) and e == 0:
                            pe.wait_ge((o_ready, rnn_ready)[q // 4], k + 1)
                        w = [t[:, q % 4, k * 256 + e * P:k * 256 + (e + 1) * P] for t in (w_hi, w_lo)]
                        i = mm3(ps[:, 2 * (q % 4) + e], w, (src[0][:, k], src[1][:, k]), q < 4 and k == 0, q >= 4 and k == 3)
                i.then_inc(panel_done, 1)
            row_stats(2, 3 * KD)

            for e in range(2):
                hidden_block(1, e, e, True)
            with pe.Fori(1, PAIRS) as j:
                for e in range(2):
                    hidden_block(1, j * 2 + e, e, False)

            def to_tokens(d):
                pe.wait_ge(x_updated, 2 * KD + d + 1)
                if d >= 2:
                    pe.wait_ge(y_out, d - 1)
                for t in range(TT):
                    i = nc.tensor.transpose(ps[:, 6 + d % 2, t * P:(t + 1) * P], xT[:, d, t * P:(t + 1) * P], ident[:])
                i.then_inc(y_done, 1)

            for it in range(2):
                for half in range(2):
                    if it == 1:
                        pe.wait_ge(x_updated, 2 * KD + 2 * half + 2)
                    else:
                        pe.wait_ge(prod_ready, 2 * FT - 1 + half)
                    down_pair(1, it, half)
                    if it + half:
                        dp = 2 * it + half - 1
                        to_tokens(2 * dp)
                        to_tokens(2 * dp + 1)
            to_tokens(KD - 2)
            to_tokens(KD - 1)


_INS = ["x", "c", "w_ada", "b_ada", "g_norm", "ffn1_w_gate", "ffn1_w_up", "ffn1_w_down", "w_in", "q_norm_g",
        "k_norm_g", "lambda_params", "head_norm_g", "conv_w", "conv_b", "w_rg_a", "b_rg_a", "w_rg_x", "b_rg_x",
        "lru_lambda", "w_out", "ffn2_w_gate", "ffn2_w_up", "ffn2_w_down"]


def kernel(**inputs):
    import numpy as _np
    import concourse.bacc as _bacc
    from concourse import mybir as _mybir
    from concourse.bass_utils import run_bass_kernel_spmd as _run

    nc = _bacc.Bacc("TRN2", target_bir_lowering=False, num_devices=1)
    arrays, args = {}, []
    for name in _INS:
        a = _np.ascontiguousarray(inputs[name])
        arrays[f"in_{name}_dram"] = a
        args.append(nc.dram_tensor(f"in_{name}_dram", a.shape, _mybir.dt.from_np(a.dtype), kind="ExternalInput").ap())
    out = nc.dram_tensor("out_0_dram", inputs["x"].shape, _mybir.dt.float32, kind="ExternalOutput").ap()
    encoder_layer(nc, *args, out)
    r = _run(nc, [arrays], core_ids=[0])
    return r.results[0]["out_0_dram"]
```

```python
from contextlib import ExitStack

import concourse.bass as bass
from concourse import mybir

F32 = mybir.dt.float32
F32R = mybir.dt.float32r
I32 = mybir.dt.int32
ALU = mybir.AluOpType
ACT = mybir.ActivationFunctionType
AX_X = mybir.AxisListType.X

P = 128
EPS = 1e-6
MASKED = 1e30
LAM_INIT = 0.2
RGLRU_C = 8.0
CHUNK = 64
LN_EXP = "natural_log_exp_and_others"


class Chain:

    def __init__(self, sem):
        self.sem, self.at = sem, 0

    def link(self, eng, ins):
        ins.then_inc(self.sem, 1)
        self.at = self.at + 1
        eng.wait_ge(self.sem, self.at)


def encoder_layer(nc, x, c, w_ada, b_ada, g_norm, ffn1_w_gate, ffn1_w_up, ffn1_w_down, w_in, q_norm_g,
                  k_norm_g, lambda_params, head_norm_g, conv_w, conv_b, w_rg_a, b_rg_a, w_rg_x, b_rg_x,
                  lru_lambda, w_out, ffn2_w_gate, ffn2_w_up, ffn2_w_down, out):
    S, D = x.shape[1], x.shape[2]
    FF = ffn1_w_gate.shape[2]
    KD, FT, TT = D // P, FF // P, S // P
    PAIRS = FT // 2
    DA = q_norm_g.shape[1] * 0 + D // 2
    NH = DA // P
    HD = P // 2
    RT = DA // P
    CW = conv_w.shape[1]
    DOWN_CUTS = [(0, 8), (8, 16), (16, FT)]

    C_ACT, B_ADA, G_NORM = 0, KD, KD + 9 * KD
    ROWS_A = G_NORM + 3 * KD
    Q_G, K_G, H_G = ROWS_A, ROWS_A + 1, ROWS_A + 2
    CONV_W = H_G + 1
    CONV_B = CONV_W + CW * RT
    B_A, B_X, LRU = CONV_B + RT, CONV_B + 2 * RT, CONV_B + 3 * RT
    NCOLS = LRU + RT

    def mod(group, d=0):
        return B_ADA + group * KD + d

    P_FFN = [0, 4 * PAIRS + 3 * KD + 28]
    P_DOWN = [p + 4 * PAIRS for p in P_FFN]
    P_MIX = P_DOWN[0] + 3 * KD
    N_IN = 20
    SPLIT_FFN = [KD, 3 * KD + FT]

    with ExitStack() as ctx:
        def sem(name):
            return ctx.enter_context(nc.semaphore(name))

        top = [(nc.sbuf_base + 31) // 32 * 32]

        def place(name, shape, dt, offset=None):
            size = 4
            for n in shape[1:]:
                size *= n
            if offset is None:
                offset = top[0]
                top[0] += (size + 31) // 32 * 32
            return nc.alloc_sbuf_tensor_at(name, shape, dt, offset=offset), offset

        xT, _ = place("xT", [P, KD, S], F32)
        raw, raw_at = place("raw", [P, 4, 2048], F32)
        w_hi, _ = place("w_hi", [P, 4, 1024], F32R)
        w_lo, _ = place("w_lo", [P, 4, 1024], F32R)
        h_hi, h_at = place("h_hi", [P, KD, S], F32R)
        h_lo, h_lo_at = place("h_lo", [P, KD, S], F32R)
        a_hi, m_at = place("a_hi", [P, FT, S], F32R)
        a_lo, _ = place("a_lo", [P, FT, S], F32R)
        m_end = top[0]
        tmp, _ = place("tmp", [P, 2, S], F32)
        acc, _ = place("acc", [P, S], F32)
        ident, _ = place("ident", [P, P], F32)
        ones, _ = place("ones", [P, P], F32)
        cols, _ = place("cols", [P, NCOLS], F32)
        misc, _ = place("misc", [P, 64], F32)
        assert top[0] <= nc.sbuf_usable_end

        x_nat, _ = place("x_nat", [P, TT, D], F32, h_at)
        lam_in, _ = place("lam_in", [P, 4, HD], F32, m_at + 8 * 8192 + 1024)
        row_in, _ = place("row_in", [P, 2, P], F32, m_at + 8 * 8192)
        lam_pr, _ = place("lam_pr", [P, 2, HD], F32, m_at + 8 * 8192 + 2048)
        x_sq, _ = place("x_sq", [P, 2, D], F32, m_at + 8 * 8192 + 4096)
        early, _ = place("early", [P, 8, 2048], F32, m_at)
        y_nat, _ = place("y_nat", [P, KD // 2, TT, 2 * P], F32, h_at)

        at = m_at
        mix = {}
        for name, shape, dt in [("q_hi", [P, NH, S], F32R), ("q_lo", [P, NH, S], F32R),
                                ("k_hi", [P, NH, S], F32R), ("k_lo", [P, NH, S], F32R),
                                ("v_hi", [P, TT, S], F32R), ("v_lo", [P, TT, S], F32R),
                                ("xr", [P, RT, S], F32), ("gate", [P, RT, S], F32),
                                ("alibi", [P, NH, S], F32), ("prob", [P, 2, 2, S], F32),
                                ("p_hi", [P, TT, P], F32R), ("p_lo", [P, TT, P], F32R),
                                ("c_hi", [P, S], F32R), ("c_lo", [P, S], F32R)]:
            mix[name], _ = place(name, shape, dt, at)
            n = 4
            for q in shape[1:]:
                n *= q
            at += n
        assert at <= m_end
        gate_at = m_at + 4 * S * (4 * NH + 2 * TT + RT)
        c_hi2, _ = place("c_hi2", [P, S], F32R, gate_at + 4 * S * 2)
        c_lo2, _ = place("c_lo2", [P, S], F32R, gate_at + 4 * S * 3)
        q_hi, q_lo, k_hi, k_lo, v_hi, v_lo = (mix[n] for n in ("q_hi", "q_lo", "k_hi", "k_lo", "v_hi", "v_lo"))
        xr, gate, alibi, prob = (mix[n] for n in ("xr", "gate", "alibi", "prob"))
        p_hi, p_lo = mix["p_hi"], mix["p_lo"]
        c_hi, c_lo = (mix["c_hi"], c_hi2), (mix["c_lo"], c_lo2)
        bd_hi, _ = place("bd_hi", [P, 2, RT, P], F32R, m_at)
        bd_lo, _ = place("bd_lo", [P, 2, RT, P], F32R, m_at + 4096)
        decay, _ = place("decay", [P, RT, S], F32, m_at + 2 * 4 * S * NH)
        heads, _ = place("heads", [P, 3, S], F32, raw_at + 3 * 8192)
        prob_at = gate_at + 4 * S * (RT + NH)
        bd, _ = place("bd", [P, 2, RT, P], F32, prob_at)
        dist, _ = place("dist", [P, S], I32, prob_at + 4096)
        drive, _ = place("drive", [P, RT, S], F32, prob_at)
        tanh_z, _ = place("tanh_z", [P, RT, S], F32, gate_at)
        ones_half, _ = place("ones_half", [P, P], F32, prob_at + 4 * S * 4 + 2 * 4 * S)

        o_square, o_inv, o_val = heads[:, 0], heads[:, 1], heads[:, 2]
        ps = ctx.enter_context(nc.psum_tensor("ps", [P, 8, 512], F32))

        EPS_C, NEG_LAM, LAM_E, LAM_S = 0, 1, 2, 4
        VAR, RSTD, NEWT = 8, 12, 16
        SP8, NSP8, HG8 = 20, 24, 28
        MX = [32, 44]
        SPT = 32

        raw_in = [sem(f"raw_in{i}") for i in range(4)]
        w_hi_ready, w_lo_ready = sem("w_hi_ready"), sem("w_lo_ready")
        panel_done = sem("panel_done")
        ada_sum, ada_done = sem("ada_sum"), sem("ada_done")
        early_in = [sem(f"early_in{i}") for i in range(8)]
        mod_ready = sem("mod_ready")
        norm_ready, h_hi_ready = sem("norm_ready"), sem("h_hi_ready")
        silu_ready, prod_ready, a_hi_ready = sem("silu_ready"), sem("prod_ready"), sem("a_hi_ready")
        split_done = sem("split_done")
        x_updated, sq_ready, sq_added = sem("x_updated"), sem("sq_ready"), sem("sq_added")
        stat_done, var_ready, rough_ready = sem("stat_done"), sem("var_ready"), sem("rough_ready")
        diag_ready, rstd_done = sem("diag_ready"), sem("rstd_done")
        s_const, s_rows, s_rows_b, s_lam = sem("consts_ready"), sem("rows_in"), sem("small_rows_in"), sem("lambda_in")
        rows_done, cols_ready = sem("rows_transposed"), sem("cols_ready")
        c_ready, eye0 = sem("c_ready"), sem("ident_zeroed")
        xt_done, xt_out, x_squared = sem("x_transposed"), sem("x_evicted"), sem("x_squared")
        x_in = [sem(f"x_in{t}") for t in range(TT)]
        lam_dot, lam_exp, sp_exp = sem("lambda_dots"), sem("lambda_exps"), sem("softplus_exps")
        y_done, y_out, y_stored = sem("y_transposed"), sem("y_evicted"), sem("y_stored")
        dist_ready, bd_zero, bd_in, bd_hi_ready, bd_ready = (sem(n) for n in (
            "dist_ready", "bd_zeroed", "bd_in", "bd_hi_ready", "bd_ready"))
        alibi_ready = sem("alibi_ready")
        v_half_done, v_ready, gate_out = sem("v_half_done"), sem("v_ready"), sem("gate_evicted")
        half_ready, conv_done, scan_done = sem("half_selector_ready"), sem("conv_done"), sem("scan_done")
        qk_sq_rstd, o_rstd = sem("qk_rstd_squared"), sem("o_rstd")
        v_hi_ready, sqh_ready, sth_done = sem("v_hi_ready"), sem("qk_squared"), sem("qk_summed")
        ln_ready, qk_f32, qk_hi, qk_ready = sem("qk_rough_rstd"), sem("qk_scaled"), sem("qk_hi_ready"), sem("qk_ready")
        score_done, max_ready, exp_ready, diff_ready = (sem(n) for n in (
            "score_done", "max_ready", "exp_ready", "diff_ready"))
        pt_done, pt_hi, pt_ready, pv_done = sem("pt_done"), sem("pt_hi_ready"), sem("pt_ready"), sem("pv_done")
        o_sq, o_stat, o_f32, o_hi, o_ready = (sem(n) for n in (
            "o_squared", "o_summed", "o_scaled", "o_hi_ready", "o_ready"))
        conv0, c_hi_ready, c_ready2 = sem("conv0"), sem("c_hi_ready"), sem("c_split")
        logit_done, r_ready, i_ready, ix_ready = sem("logit_done"), sem("r_ready"), sem("i_ready"), sem("ix_ready")
        gelu_ready, tanh_ready, a_ready, d_ready, sqrt_ready, rnn_f32, rnn_hi, rnn_ready = (sem(n) for n in (
            "gelu_ready", "tanh_ready", "decay_ready", "drive_ready", "sqrt_ready", "rnn_f32", "rnn_hi_ready",
            "rnn_ready"))
        act_chain, dve_chain, pool_chain = (Chain(sem(n)) for n in ("act_chain", "dve_chain", "pool_chain"))

        def f(ap):
            return ap.bitcast(F32)

        gate_v = [w.rearrange("l (k p) n -> p (l k) n", p=P) for w in (ffn1_w_gate, ffn2_w_gate)]
        up_v = [w.rearrange("l (k p) n -> p (l k) n", p=P) for w in (ffn1_w_up, ffn2_w_up)]
        down_v = [w.rearrange("l (k p) n -> p (l k) n", p=P) for w in (ffn1_w_down, ffn2_w_down)]
        ada_v = w_ada.rearrange("l (k p) n -> p (l k) n", p=P)
        in_v = w_in.rearrange("l (k p) n -> p (l k) n", p=P)
        out_v = w_out.rearrange("l (k p) n -> p (l k) n", p=P)
        x_v = x.rearrange("b (t p) d -> p (b t) d", p=P)
        y_v = out.rearrange("b (t p) d -> p (b t) d", p=P)
        IN_COLS = [4 * DA, 4 * DA + 256, 2 * DA, 2 * DA + 256, 0, DA, 256, DA + 256, 3 * DA, 3 * DA + 256]
        V0, QK0, GATE0 = 4, 8, 16
        QK = {8: (0, 0), 9: (0, 1), 10: (1, 0), 11: (1, 1), 12: (0, 2), 13: (0, 3), 14: (1, 2), 15: (1, 3)}
        QK_BY_HEAD = {h: [n for n, s in enumerate(sorted(QK)) if QK[s][1] == h] for h in range(NH)}

        def tile_bank(s):
            return s % 3 if s < 12 else s % 2

        def panels_at(s):
            return {1: (4,), 2: (5,), 3: (6,), 4: (7,), 6: (8, 9), 8: (10, 11)}.get(s, (s + 3,) if s > 8 else ())

        def head_bank(h):
            return (6, 2)[h % 2]

        OUT_BANK = [0, 1, 3, 4, 5, 6, 2, 7]

        EARLY_BANK = (4, 6, 7, 4)

        UNITS = {24 + TT * h + b: (h, b) for h in range(NH) for b in range(TT)}
        UNIT_NO = {u: n for n, u in enumerate(UNITS[k] for k in sorted(UNITS))}
        HEAD_END = {24 + TT * h + TT - 1: h for h in range(NH)}
        HEAD_STAT = {x + (7 if h == 0 else 5): h for x, h in HEAD_END.items()}
        LAST = 2 * N_IN + 7

        def raw2(slot, k0, k1, half):
            return raw[:, slot].rearrange("p (k n) -> p k n", n=256)[:, k0:k1, half * P:(half + 1) * P]

        def blk(t, slot, k):
            return t[:, slot, 0:k * P].rearrange("p (k n) -> p k n", n=P)

        block = ctx.enter_context(nc.Block())

        @block.sync
        def _(sp):
            def load(slot, src):
                n = src.shape[1] * src.shape[2]
                dst = raw[:, slot, 0:n].rearrange("p (k n) -> p k n", k=src.shape[1])
                sp.dma_start(dst, src).then_inc(raw_in[slot], 16)

            def load_ada(slot, ch):
                load(slot, ada_v[:, :, bass.ds(ch * 256, 256)])

            for t in range(TT):
                sp.dma_start(x_nat[:, t], x_v[:, t]).then_inc(x_in[t], 16)
            for i in range(8):
                if i == 2:
                    for slot, w in ((0, gate_v[0]), (1, up_v[0])):
                        load(slot, w[:, :, 0:256])
                ch = KD // 2 * (1 - i % 2) + i // 2
                sp.dma_start(early[:, i].rearrange("p (k n) -> p k n", n=256), ada_v[:, :, 256 * ch:256 * (ch + 1)])\
                    .then_inc(early_in[i], 16)
            for slot, w in ((0, gate_v[0]), (1, up_v[0])):
                sp.wait_ge(w_lo_ready, 3 + slot)
                load(slot, w[:, :, 256:512])
            for slot in (2, 3):
                load_ada(slot, 6 + slot)
            with sp.Fori(2, PAIRS) as j:
                sp.wait_ge(w_lo_ready, j * 4 - 1)
                load(0, gate_v[0][:, :, bass.ds(j * 256, 256)])
                sp.wait_ge(w_lo_ready, j * 4)
                load(1, up_v[0][:, :, bass.ds(j * 256, 256)])
                sp.wait_ge(ada_done, j * 2 + 5)
                load_ada(2, j * 2 + 6)
                sp.wait_ge(ada_done, j * 2 + 6)
                load_ada(3, j * 2 + 7)

            def down(n, it, waits):
                base = P_DOWN[n]
                for q in range(6):
                    k0, k1 = DOWN_CUTS[q % 3]
                    if n == 0 and it == 0 and q == 2:
                        for slot in (2, 3):
                            sp.wait_ge(ada_done, 2 * PAIRS + 3 + slot)
                            load_ada(slot, 2 * PAIRS + 4 + slot)
                    s, v = waits[q]
                    sp.wait_ge(s, v)
                    load((0, 1, 2, 3, 0, 1)[q], down_v[n][:, k0:k1, bass.ds(it * 512 + 256 * (q // 3), 256)])

            for it in range(2):
                b = P_DOWN[0]
                down(0, it, [(w_lo_ready, it * 12 + (b - 1)), (w_lo_ready, it * 12 + b),
                             (ada_done, it * 2 + 29), (ada_done, it * 2 + 30),
                             (w_lo_ready, it * 12 + (b + 2)), (w_lo_ready, it * 12 + (b + 4))])
                sp.wait_ge(w_lo_ready, it * 12 + (b + 6))
                load_ada(2, it * 2 + 30)
                sp.wait_ge(w_lo_ready, it * 12 + (b + 8))
                load_ada(3, it * 2 + 31)
            for r in range(10):
                sp.wait_ge(w_lo_ready, P_MIX - 2 + 2 * r)
                load(r % 2, in_v[:, :, IN_COLS[r]:IN_COLS[r] + 256])
                if r == 1:
                    for slot in (2, 3):
                        sp.wait_ge(ada_done, 31 + slot)
                        load_ada(slot, 32 + slot)
            for r in range(4):
                sp.wait_ge(w_lo_ready, P_MIX - 2 + 2 * (10 + r))
                load(r % 2, out_v[:, 4 - 4 * (r // 2):8 - 4 * (r // 2), 512 * (r % 2):512 * (r % 2) + 512])
            b = P_FFN[1]
            for slot, w in ((0, gate_v[1]), (1, up_v[1])):
                sp.wait_ge(w_lo_ready, b - 2 + 2 * slot)
                load(slot, w[:, :, 0:256])
            sp.wait_ge(ada_done, 9 * KD // 2)
            sp.wait_ge(o_ready, NH)
            with sp.Fori(0, (PAIRS - 1) // 2) as it:
                for e in range(2):
                    sp.wait_ge(w_lo_ready, it * 8 + (b - 1 + 4 * e))
                    load(2 - 2 * e, gate_v[1][:, :, bass.ds(it * 512 + 256 * (1 + e), 256)])
                    sp.wait_ge(w_lo_ready, it * 8 + (b + 4 * e))
                    load(3 - 2 * e, up_v[1][:, :, bass.ds(it * 512 + 256 * (1 + e), 256)])
            with sp.Fori(0, 2) as it:
                b = P_DOWN[1]
                down(1, it, [(w_lo_ready, it * 12 + (b - 1)), (w_lo_ready, it * 12 + b),
                             (w_lo_ready, it * 12 + (b - 5)), (w_lo_ready, it * 12 + (b - 4)),
                             (w_lo_ready, it * 12 + (b + 2)), (w_lo_ready, it * 12 + (b + 4))])
            for dp in range(KD // 2):
                sp.wait_ge(y_out, 2 * (dp + 1))
                sp.dma_start(y_v[:, :, 256 * dp:256 * (dp + 1)], y_nat[:, dp]).then_inc(y_stored, 16)
            sp.wait_ge(y_stored, 16 * (KD // 2))

        @block.gpsimd
        def _(pool):
            pool_chain.link(pool, nc.gpsimd.memset(ident[:], 0.0))
            pool_chain.link(pool, nc.gpsimd.affine_select(
                out=ident[:], in_=ident[:], compare_op=ALU.not_equal, fill=1.0, base=0,
                pattern=[[-1, P]], channel_multiplier=1))
            nc.gpsimd.memset(misc[:, EPS_C:EPS_C + 1], EPS).then_inc(s_const, 1)
            nc.gpsimd.memset(ones[:], 1.0).then_inc(s_const, 1)
            pool.wait_ge(panel_done, P_MIX)
            nc.gpsimd.iota(dist[:], pattern=[[-1, S]], base=S - P, channel_multiplier=1).then_inc(dist_ready, 1)
            nc.gpsimd.memset(bd[:], 0.0).then_inc(bd_zero, 1)
            pool.wait_ge(bd_zero, 1)
            for g, w in enumerate((w_rg_a, w_rg_x)):
                wv = w.rearrange("l (t e) c d -> e c (l t) d", e=2)
                for e in range(2):
                    pool.dma_start(bd[e * HD:(e + 1) * HD, g, :, e * HD:(e + 1) * HD], wv[e]).then_inc(bd_in, 16)
            pool.wait_ge(logit_done, 2 * RT)
            pool_chain.link(pool, nc.gpsimd.memset(ones_half[:], 0.0))
            nc.gpsimd.memset(ones_half[0:HD, 0:HD], 1.0).then_inc(half_ready, 1)
            nc.gpsimd.memset(ones_half[HD:P, HD:P], 1.0).then_inc(half_ready, 1)
            for n, t in enumerate(sorted(QK)):
                w, h = QK[t]
                pool.wait_ge(ln_ready, n + 1)
                if n:
                    pool.wait_ge(qk_ready, n)
                nc.gpsimd.tensor_tensor(tmp[:, 1], acc[:], acc[:], ALU.mult).then_inc(qk_sq_rstd, 1)
                pool.wait_ge(qk_hi, n + 1)
                nc.gpsimd.tensor_tensor((q_lo, k_lo)[w][:, h], tmp[:, 1], f((q_hi, k_hi)[w][:, h]), ALU.subtract)\
                    .then_inc(qk_ready, 1)

        @block.scalar
        def _(act):
            act.dma_start(row_in[0:KD, 0], c.rearrange("b (k p) -> (b k) p", p=P)).then_inc(s_rows, 16)
            act.dma_start(row_in[B_ADA:G_NORM, 0], b_ada.rearrange("l (k p) -> (l k) p", p=P)).then_inc(s_rows, 16)
            act.dma_start(row_in[G_NORM:ROWS_A, 0],
                          g_norm.rearrange("l s (k p) -> (l s k) p", p=P)).then_inc(s_rows, 16)
            row = 0
            for v in (q_norm_g.rearrange("l m d -> l (m d)"), k_norm_g.rearrange("l m d -> l (m d)"), head_norm_g,
                      conv_w.rearrange("l i (t p) -> (l i t) p", p=P), conv_b.rearrange("l (t p) -> (l t) p", p=P),
                      b_rg_a.rearrange("l (t p) -> (l t) p", p=P), b_rg_x.rearrange("l (t p) -> (l t) p", p=P),
                      lru_lambda.rearrange("l (t p) -> (l t) p", p=P)):
                act.dma_start(row_in[row:row + v.shape[0], 1], v).then_inc(s_rows_b, 16)
                row += v.shape[0]
            act.dma_start(lam_in[:], lambda_params.to_broadcast([P, 4, HD])).then_inc(s_lam, 16)

            def rough_rstd(n):
                nc.scalar.preload_act_table_set(LN_EXP)
                act.wait_ge(var_ready, n + 1)
                act_chain.link(act, nc.scalar.activation(misc[:, RSTD:RSTD + TT], misc[:, VAR:VAR + TT], ACT.Ln))
                nc.scalar.activation(misc[:, RSTD:RSTD + TT], misc[:, RSTD:RSTD + TT], ACT.Exp, scale=-0.5)\
                    .then_inc(rough_ready, 1)

            act.wait_ge(cols_ready, 1)
            nc.scalar.activation(cols[:, 0:KD], cols[:, 0:KD], ACT.Silu).then_inc(c_ready, 1)
            for t in range(TT):
                act.wait_ge(x_in[t], 16)
                i = nc.scalar.activation(x_sq[:, t % 2], x_nat[:, t], ACT.Square,
                                         accum_out=misc[:, RSTD + t:RSTD + t + 1])
                i.then_inc(x_squared, 1)
                if t < TT - 2:
                    act.wait_ge(x_squared, t + 1)
            rough_rstd(0)
            for d in range(KD):
                act.wait_ge(xt_done, d + 1)
                nc.scalar.copy(xT[:, d], ps[:, 6 + d % 2]).then_inc(xt_out, 1)

            def hi(n, slot, src, k, width=P, fresh=None, wait=True):
                if wait:
                    act.wait_ge(panel_done, n - 3)
                if fresh is not None:
                    act.wait_ge(raw_in[fresh[0]], fresh[1])
                dst = w_hi[:, slot, 0:k * width].rearrange("p (k n) -> p k n", n=width)
                nc.scalar.copy(dst, src).then_inc(w_hi_ready, 1)

            def modulate(n, blocks=range(KD)):
                for d in blocks:
                    act.wait_ge(norm_ready, n * KD + d + 1)
                    nc.scalar.activation(h_hi[:, d], tmp[:, d % 2], ACT.Identity,
                                         bias=cols[:, mod(3 * n, d):mod(3 * n, d) + 1]).then_inc(h_hi_ready, 1)

            def square(d, upd):
                act.wait_ge(x_updated, upd + 1)
                nc.scalar.activation(tmp[:, d % 2], xT[:, d], ACT.Square).then_inc(sq_ready, 1)

            def hidden(j, jl, n):
                act.wait_ge(panel_done, j * 2 + (P_FFN[n] + 2))
                act.wait_ge(split_done, j + (SPLIT_FFN[n] - 1))
                nc.scalar.activation(tmp[:, jl], ps[:, 2 * jl], ACT.Silu).then_inc(silu_ready, 1)
                act.wait_ge(prod_ready, j + (n * FT + 1))
                nc.scalar.copy(a_hi[:, j] if isinstance(j, int) else a_hi[:, bass.ds(j, 1)].rearrange(
                    "p a b -> p (a b)"), tmp[:, jl]).then_inc(a_hi_ready, 1)

            def ffn_panels(n, j, e, slots, ords):
                for g in range(2):
                    hi(j * 4 + (P_FFN[n] + 2 * e + g), 2 * e + g, raw2(slots[g], 0, KD, e), KD,
                       fresh=(slots[g], ords) if e == 0 else None)

            def down_panel(n, it, q):
                r, e = q // 2, q % 2
                slot = (0, 1, 2, 3, 0, 1)[r]
                k0, k1 = DOWN_CUTS[r % 3]
                per = 2
                if n == 0:
                    first = (12, 12, 12, 12, 13, 13)[r]
                else:
                    first, per = (29, 29, 22, 22, 30, 30)[r], (2, 2, 1, 1, 2, 2)[r]
                hi(it * 12 + (P_DOWN[n] + q), q % 4, raw2(slot, 0, k1 - k0, e), k1 - k0,
                   fresh=(slot, it * (16 * per) + 16 * first) if e == 0 else None)

            modulate(0, range(2))
            for q in range(4):
                hi(q, q, raw2(q % 2, 0, KD, q // 2), KD, fresh=(q % 2, 16), wait=False)
            act.wait_ge(lam_dot, 1)
            nc.scalar.activation(misc[:, LAM_E:LAM_E + 2], misc[:, LAM_S:LAM_S + 2], ACT.Exp).then_inc(lam_exp, 1)
            act.wait_ge(sp_exp, 1)
            nc.scalar.activation(misc[:, SPT:SPT + RT], misc[:, SPT:SPT + RT], ACT.Exp, scale=-1.0)\
                .then_inc(lam_exp, 1)
            modulate(0, range(2, KD))
            with act.Fori(0, PAIRS - 1) as j:
                for e in range(2):
                    ffn_panels(0, j + 1, e, (0, 1), j * 16 + 16 * 2)
                    hidden(j * 2 + e, e, 0)
            for e in range(2):
                down_panel(0, 0, 2 * e)
                down_panel(0, 0, 2 * e + 1)
                hidden(2 * (PAIRS - 1) + e, e, 0)

            def down_body(n, it, nxt, base):
                for half in range(2):
                    down_panel(n, it, 6 * half + 4)
                    down_panel(n, it, 6 * half + 5)
                    if half == 0:
                        for q in range(6, 10):
                            down_panel(n, it, q)
                    else:
                        nxt()
                    if n == 0:
                        for d in range(2):
                            square(2 * half + d, it * 4 + (base + 2 * half + d))

            def down1(it):
                pass

            def square_at(off, it, par, base):
                act.wait_ge(x_updated, it * 4 + (base + off + 1))
                src = xT[:, bass.ds(it * 4 + off, 1)].rearrange("p a b -> p (a b)")
                nc.scalar.activation(tmp[:, par], src, ACT.Square).then_inc(sq_ready, 1)

            def down_iteration(n, it, nxt):
                for half in range(2):
                    down_panel(n, it, 6 * half + 4)
                    down_panel(n, it, 6 * half + 5)
                    if half == 0:
                        for q in range(6, 10):
                            down_panel(n, it, q)
                    else:
                        nxt(it)
                    for e in range(2):
                        if n == 0:
                            if it + half:
                                act.wait_ge(sq_added, it * 4 + (2 * half - 1 + e))
                            square_at(2 * half + e, it, e, 0)

            for it in range(1):
                down_iteration(0, it, lambda i: [down_panel(0, i + 1, q) for q in range(4)])

            def mix_panel(m):
                fresh = ((m // 2) % 2, 16 * (16 + m // 4)) if m % 2 == 0 else None
                if V0 <= m < QK0:
                    hi(P_MIX + m, m % 4, raw[:, (m // 2) % 2, 1024 * (m % 2):1024 * (m % 2 + 1)]
                       .rearrange("p (k n) -> p k n", n=256), 4, 256, fresh=fresh)
                elif m < N_IN:
                    hi(P_MIX + m, m % 4, raw2((m // 2) % 2, 0, KD, m % 2), KD, fresh=fresh)
                else:
                    src = raw[:, (m // 2) % 2].rearrange("p (k n) -> p k n", n=512)[:, :, 256 * (m % 2):256 * (m % 2 + 1)]
                    hi(P_MIX + m, m % 4, src, 4, 256, fresh=fresh)

            down_iteration(0, 1, lambda _: [mix_panel(q) for q in range(4)])
            rough_rstd(1)
            modulate(1)

            act.wait_ge(bd_in, 64)
            nc.scalar.copy(bd_hi[:], bd[:]).then_inc(bd_hi_ready, 1)
            act.wait_ge(dist_ready, 1)
            for h in range(NH):
                slope = 2.0 ** (-8.0 * (h + 1) / NH) * HD ** 0.5
                i = nc.scalar.activation(alibi[:, h], dist[:], ACT.Abs, scale=slope)
            i.then_inc(alibi_ready, 1)

            def tile_out(t):
                bank = ps[:, tile_bank(t)]
                if t in (V0, V0 + 2):
                    act.wait_ge(v_half_done, (t - V0) // 2 + 1)
                else:
                    act.wait_ge(panel_done, P_MIX + t + 1)
                if t < V0:
                    nc.scalar.activation(xr[:, t], bank, ACT.Identity,
                                         scale=cols[:, CONV_W + 3 * RT + t:CONV_W + 3 * RT + t + 1],
                                         bias=cols[:, CONV_B + t:CONV_B + t + 1]).then_inc(conv0, 1)
                    act.wait_ge(conv_done, t + 1)
                    if t >= 2:
                        act.wait_ge(logit_done, 2 * t - 2)
                    nc.scalar.copy(c_hi[t % 2][:], xr[:, t]).then_inc(c_hi_ready, 1)
                elif t < QK0:
                    n = t - V0
                    tok = 2 * (n % 2)
                    nc.scalar.copy(v_hi[:, tok:tok + 2, 256 * (n // 2):256 * (n // 2) + 256],
                                   bank.rearrange("p (t n) -> p t n", t=2)).then_inc(v_hi_ready, 1)
                elif t in QK:
                    n = t - QK0
                    if n:
                        act.wait_ge(sth_done, n)
                    nc.scalar.activation(tmp[:, 0], bank, ACT.Square).then_inc(sqh_ready, 1)
                else:
                    n = t - GATE0
                    nc.scalar.copy(gate[:, n], bank).then_inc(gate_out, 1)

            def rough(src, dst, count, done):
                act_chain.link(act, nc.scalar.activation(dst, src, ACT.Ln, scale=1.0 / count,
                                                         bias=misc[:, EPS_C:EPS_C + 1]))
                nc.scalar.activation(dst, dst, ACT.Exp, scale=-0.5).then_inc(done, 1)

            def qk_hi_part(t):
                n, (w, h) = t - QK0, QK[t]
                act.wait_ge(qk_f32, n + 1)
                nc.scalar.copy((q_hi, k_hi)[w][:, h], tmp[:, 1]).then_inc(qk_hi, 1)

            for xh in range(LAST):
                s = xh // 2
                if xh % 2 == 0 and s - 2 in QK:
                    qk_hi_part(s - 2)
                if xh % 2 == 0 and 0 < s <= N_IN:
                    for m in panels_at(s):
                        mix_panel(m)
                    tile_out(s - 1)
                if xh in (2 * N_IN + 2, 2 * N_IN + 4, 2 * N_IN + 5, 2 * N_IN + 6):
                    mix_panel(N_IN + 4 + (2 * N_IN + 2, 2 * N_IN + 4, 2 * N_IN + 5, 2 * N_IN + 6).index(xh))
                if xh in range(6, 6 + 2 * RT, 2):
                    n = xh // 2 - 3
                    act.wait_ge(logit_done, 2 * n + 2)
                    nc.scalar.activation(decay[:, n], ps[:, 6], ACT.Sigmoid,
                                         bias=cols[:, B_A + n:B_A + n + 1]).then_inc(r_ready, 1)
                    nc.scalar.activation(ps[:, 7], ps[:, 7], ACT.Sigmoid,
                                         bias=cols[:, B_X + n:B_X + n + 1]).then_inc(i_ready, 1)
                if xh == 13:
                    for n in range(RT):
                        act.wait_ge(r_ready, n + 1)
                        nc.scalar.activation(tanh_z[:, n], decay[:, n], ACT.Tanh,
                                             scale=misc[:, SP8 + n:SP8 + n + 1]).then_inc(tanh_ready, 1)
                    for n in range(RT):
                        act.wait_ge(tanh_ready, n + 1)
                        nc.scalar.activation(decay[:, n], decay[:, n], ACT.Exp,
                                             scale=misc[:, NSP8 + n:NSP8 + n + 1]).then_inc(a_ready, 1)
                if xh == 16:
                    for n in range(RT):
                        act.wait_ge(d_ready, n + 1)
                        nc.scalar.activation(drive[:, n], drive[:, n], ACT.Sqrt).then_inc(sqrt_ready, 1)
                    nc.scalar.preload_act_table_set(LN_EXP)
                if xh % 2 and s - 1 in QK:
                    n = s - 1 - QK0
                    act.wait_ge(sth_done, n + 1)
                    rough(ps[:, 7], acc[:], HD, ln_ready)
                if xh - 2 in HEAD_STAT:
                    h = HEAD_STAT[xh - 2]
                    act.wait_ge(o_f32, h + 1)
                    nc.scalar.copy(q_hi[:, h], o_val).then_inc(o_hi, 1)
                if xh - 1 in HEAD_STAT:
                    h = HEAD_STAT[xh - 1]
                    act.wait_ge(o_stat, h + 1)
                    rough(ps[:, 7], o_inv, P, o_rstd)
                if xh - 2 in UNITS:
                    h, b = UNITS[xh - 2]
                    u = UNIT_NO[h, b]
                    act.wait_ge(pt_done, u + 1)
                    if u:
                        act.wait_ge(pv_done, u)
                    nc.scalar.copy(p_hi[:, 0:b + 1], ps[:, 5, 0:(b + 1) * P].rearrange("p (k n) -> p k n", n=P))\
                        .then_inc(pt_hi, 1)
                if xh in UNITS:
                    h, b = UNITS[xh]
                    u = UNIT_NO[h, b]
                    W, mc = (b + 1) * P, MX[u % 2]
                    act.wait_ge(max_ready, u + 1)
                    for m in range(2):
                        e = nc.scalar.activation(prob[:, u % 2, m, 0:W], prob[:, u % 2, m, 0:W], ACT.Exp,
                                                 bias=misc[:, mc + 2 + m:mc + 3 + m],
                                                 accum_out=misc[:, mc + 4 + m:mc + 5 + m])
                        e.then_inc(exp_ready, 1)
                if xh - 4 in HEAD_END:
                    h = HEAD_END[xh - 4]
                    act.wait_ge(pv_done, TT * (h + 1))
                    if h == 0:
                        act.wait_ge(scan_done, RT)
                    else:
                        act.wait_ge(o_stat, h)
                    nc.scalar.activation(o_square, ps[:, head_bank(h)], ACT.Square).then_inc(o_sq, 1)
                if xh == 2 * N_IN:
                    for n in range(RT):
                        act.wait_ge(gate_out, n + 1)
                        nc.scalar.activation(gate[:, n], gate[:, n], ACT.Gelu_apprx_tanh).then_inc(gelu_ready, 1)
                    nc.scalar.preload_act_table_set(LN_EXP)
                if xh == 2 * N_IN + 1:
                    for n in range(RT):
                        act.wait_ge(rnn_f32, n + 1)
                        nc.scalar.copy(k_hi[:, n], gate[:, n]).then_inc(rnn_hi, 1)
            for q in range(4):
                hi(P_FFN[1] + q, q, raw2(q % 2, 0, KD, q // 2), KD, fresh=(q % 2, 16 * 23))
                for e in range(2):
                    act.wait_ge(sq_added, KD + 2 * q - 1 + e)
                    square(2 * q + e, KD + 2 * q + e)
            rough_rstd(2)
            modulate(2)

            with act.Fori(0, (PAIRS - 1) // 2) as it:
                for m in range(2):
                    for e in range(2):
                        ffn_panels(1, it * 2 + (1 + m), e, ((2, 3), (0, 1))[m],
                                   it * 16 + 16 * (17, 24)[m])
                        hidden(it * 4 + (2 * m + e), e, 1)
            for e in range(2):
                down_panel(1, 0, 2 * e)
                down_panel(1, 0, 2 * e + 1)
                hidden(2 * (PAIRS - 1) + e, e, 1)

            def evict(d):
                act.wait_ge(y_done, d + 1)
                nc.scalar.copy(y_nat[:, d // 2, :, P * (d % 2):P * (d % 2 + 1)],
                               ps[:, 6 + d % 2].rearrange("p (t n) -> p t n", t=TT)).then_inc(y_out, 1)

            for q in range(4, 12):
                down_panel(1, 0, q)
            for q in range(4):
                down_panel(1, 1, q)
            evict(0)
            evict(1)
            for q in range(4, 10):
                down_panel(1, 1, q)
            evict(2)
            evict(3)
            for q in range(10, 12):
                down_panel(1, 1, q)
            for d in range(4, KD):
                evict(d)

        @block.vector
        def _(dve):
            link = lambda ins: dve_chain.link(dve, ins)

            dve.wait_ge(rows_done, 1)
            nc.vector.tensor_copy(cols[:, 0:ROWS_A], ps[:, 6, 0:ROWS_A]).then_inc(cols_ready, 1)
            dve.wait_ge(cols_ready, 1)

            def ada_chunk(slot, ordv, src=None):
                if src is None:
                    dve.wait_ge(raw_in[slot], ordv)
                    src = raw[:, slot]
                r = src.rearrange("p (k n) -> p k n", n=256)
                link(nc.vector.tensor_scalar(r[:, 0], r[:, 0], cols[:, 0:1], None, ALU.mult))
                for k in range(1, KD):
                    i = nc.vector.scalar_tensor_tensor(out=r[:, 0], in0=r[:, k], scalar=cols[:, k:k + 1],
                                                       in1=r[:, 0], op0=ALU.mult, op1=ALU.add)
                    if k < KD - 1:
                        link(i)
                i.then_inc(ada_sum, 1)

            def variance(n):
                v, y, t = (misc[:, q:q + TT] for q in (VAR, RSTD, NEWT))
                if n == 0:
                    dve.wait_ge(x_squared, TT)
                    sums = y
                else:
                    dve.wait_ge(stat_done, n)
                    sums = ps[:, 5, 0:TT]
                nc.vector.tensor_scalar(v, sums, 1.0 / D, EPS, ALU.mult, ALU.add).then_inc(var_ready, 1)
                dve.wait_ge(rough_ready, n + 1)
                link(nc.vector.tensor_tensor(t, y, y, ALU.mult))
                link(nc.vector.tensor_tensor(t, t, v, ALU.mult))
                link(nc.vector.tensor_scalar(t, t, -0.5, 1.5, ALU.mult, ALU.add))
                link(nc.vector.tensor_tensor(y, y, t, ALU.mult))
                for q in range(TT):
                    i = nc.vector.tensor_scalar(acc[:, q * P:(q + 1) * P], ident[:], misc[:, RSTD + q:RSTD + q + 1],
                                                None, ALU.mult)
                i.then_inc(diag_ready, 1)

            def modulate(n, blocks=range(KD)):
                dve.wait_ge(rstd_done, n + 1)

                def scaled(d):
                    if d >= 2:
                        dve.wait_ge(split_done, n * KD + (FT if n else 0) + d - 1)
                    nc.vector.scalar_tensor_tensor(
                        out=tmp[:, d % 2], in0=xT[:, d], scalar=cols[:, mod(3 * n + 1, d):mod(3 * n + 1, d) + 1],
                        in1=ps[:, 5], op0=ALU.mult, op1=ALU.mult).then_inc(norm_ready, 1)

                scaled(blocks[0])
                for d in blocks:
                    if d != blocks[-1]:
                        scaled(d + 1)
                    dve.wait_ge(h_hi_ready, n * KD + d + 1)
                    nc.vector.scalar_tensor_tensor(
                        out=h_lo[:, d], in0=tmp[:, d % 2], scalar=cols[:, mod(3 * n, d):mod(3 * n, d) + 1],
                        in1=f(h_hi[:, d]), op0=ALU.add, op1=ALU.subtract).then_inc(split_done, 1)

            def gain(n):
                m = cols[:, mod(3 * n + 1):mod(3 * n + 1) + KD]
                link(nc.vector.scalar_tensor_tensor(out=m, in0=m, scalar=1.0,
                                                    in1=cols[:, G_NORM + n * KD:G_NORM + (n + 1) * KD],
                                                    op0=ALU.add, op1=ALU.mult))

            variance(0)

            def lo(n, slot, src, k, width=P):
                dve.wait_ge(w_hi_ready, n + 1)
                h_, l_ = (t[:, slot, 0:k * width].rearrange("p (k n) -> p k n", n=width) for t in (w_hi, w_lo))
                nc.vector.tensor_tensor(l_, src, f(h_), ALU.subtract).then_inc(w_lo_ready, 1)

            def hidden(j, jl, n):
                dve.wait_ge(silu_ready, j + (n * FT + 1))
                nc.vector.tensor_tensor(tmp[:, jl], tmp[:, jl], ps[:, 2 * jl + 1], ALU.mult).then_inc(prod_ready, 1)
                at_j = (lambda t: t[:, j]) if isinstance(j, int) else (
                    lambda t: t[:, bass.ds(j, 1)].rearrange("p a b -> p (a b)"))
                dve.wait_ge(a_hi_ready, j + (n * FT + 1))
                nc.vector.tensor_tensor(at_j(a_lo), tmp[:, jl], f(at_j(a_hi)), ALU.subtract).then_inc(split_done, 1)

            def ffn_panels(n, j, e, slots):
                for g in range(2):
                    lo(j * 4 + (P_FFN[n] + 2 * e + g), 2 * e + g, raw2(slots[g], 0, KD, e), KD)

            def down_panel(n, it, q):
                r, e = q // 2, q % 2
                k0, k1 = DOWN_CUTS[r % 3]
                lo(it * 12 + (P_DOWN[n] + q), q % 4, raw2((0, 1, 2, 3, 0, 1)[r], 0, k1 - k0, e), k1 - k0)

            def mod_cols(first, count, done):
                dve.wait_ge(ada_done, done)
                m = cols[:, bass.ds(first, count)]
                link(nc.vector.tensor_tensor(m, m, ps[:, 4, 0:count], ALU.add))

            def small_columns():
                dve.wait_ge(rows_done, 2)
                nc.vector.tensor_copy(cols[:, ROWS_A:NCOLS], ps[:, 7, 0:NCOLS - ROWS_A]).then_inc(cols_ready, 1)
                dve.wait_ge(cols_ready, 2)
                dve.wait_ge(s_lam, 16)
                for m in range(2):
                    i = nc.vector.tensor_tensor_reduce(out=lam_pr[:, m], in0=lam_in[:, 2 * m], in1=lam_in[:, 2 * m + 1],
                                                       scale=1.0, scalar=0.0, op0=ALU.mult, op1=ALU.add,
                                                       accum_out=misc[:, LAM_S + m:LAM_S + m + 1])
                i.then_inc(lam_dot, 1)
                nc.vector.scalar_tensor_tensor(out=misc[:, SPT:SPT + RT], in0=cols[:, LRU:LRU + RT], scalar=-1.0,
                                               in1=cols[:, LRU:LRU + RT], op0=ALU.mult, op1=ALU.max).then_inc(sp_exp, 1)

            def lambda_and_softplus():
                dve.wait_ge(lam_exp, 2)
                link(nc.vector.tensor_tensor(misc[:, NEG_LAM:NEG_LAM + 1], misc[:, LAM_E + 1:LAM_E + 2],
                                             misc[:, LAM_E:LAM_E + 1], ALU.subtract))
                link(nc.vector.tensor_scalar(misc[:, NEG_LAM:NEG_LAM + 1], misc[:, NEG_LAM:NEG_LAM + 1], -LAM_INIT,
                                             None, ALU.add))
                link(nc.vector.tensor_scalar(misc[:, HG8:HG8 + 1], cols[:, H_G:H_G + 1], 1.0 - LAM_INIT, None, ALU.mult))
                link(nc.vector.tensor_scalar(cols[:, Q_G:K_G + 1], cols[:, Q_G:K_G + 1], -0.5 / HD, None, ALU.mult))
                e_, s_, q_, a_ = (misc[:, SPT + RT * i:SPT + RT * (i + 1)] for i in range(4))
                link(nc.vector.tensor_scalar(s_, e_, 2.0, None, ALU.add))
                link(nc.vector.reciprocal(q_, s_))
                link(nc.vector.tensor_tensor(s_, e_, q_, ALU.mult))
                link(nc.vector.tensor_tensor(q_, s_, s_, ALU.mult))
                link(nc.vector.memset(a_, 1.0 / 19.0))
                for i in range(17, 0, -2):
                    link(nc.vector.tensor_tensor(a_, a_, q_, ALU.mult))
                    link(nc.vector.tensor_scalar(a_, a_, 1.0 / i, None, ALU.add))
                link(nc.vector.tensor_tensor(a_, a_, s_, ALU.mult))
                link(nc.vector.tensor_scalar(q_, cols[:, LRU:LRU + RT], -1.0, 0.0, ALU.mult, ALU.max))
                link(nc.vector.scalar_tensor_tensor(out=q_, in0=a_, scalar=2.0, in1=q_, op0=ALU.mult, op1=ALU.add))
                link(nc.vector.tensor_scalar(misc[:, SP8:SP8 + RT], q_, RGLRU_C, None, ALU.mult))
                link(nc.vector.tensor_scalar(misc[:, NSP8:NSP8 + RT], q_, -RGLRU_C, None, ALU.mult))

            dve.wait_ge(c_ready, 1)
            for p in range(KD // 2):
                dve.wait_ge(early_in[2 * p + 1], 16)
                ada_chunk(None, None, early[:, 2 * p + 1])
                dve.wait_ge(ada_done, 2 * p + 2)
                sc, sh, g = (cols[:, q + 2 * p:q + 2 * p + 2] for q in (mod(1), mod(0), G_NORM))
                link(nc.vector.tensor_tensor(sc, sc, ps[:, EARLY_BANK[p], 0:2], ALU.add))
                link(nc.vector.tensor_tensor(sh, sh, ps[:, EARLY_BANK[p], 2:4], ALU.add))
                link(nc.vector.scalar_tensor_tensor(out=sc, in0=sc, scalar=1.0, in1=g, op0=ALU.add, op1=ALU.mult))
                modulate(0, range(2 * p, 2 * p + 2))
                if p == 0:
                    for q in range(4):
                        lo(q, q, raw2(q % 2, 0, KD, q // 2), KD)
                    small_columns()
                elif p == 1:
                    lambda_and_softplus()
            LINKS = 2 * (KD - 1) + 1
            for e in range(2):
                ffn_panels(0, 1, e, (0, 1))
                hidden(e, e, 0)
                ada_chunk(2 + e, 16)
            base = dve_chain.at
            with dve.Fori(1, PAIRS - 1) as j:
                dve_chain.at = (j - 1) * LINKS + base
                for e in range(2):
                    ffn_panels(0, j + 1, e, (0, 1))
                    hidden(j * 2 + e, e, 0)
                    if e == 0:
                        mod_cols(j * 4 + (mod(2) - 4), 4, j * 2 + 8)
                    ada_chunk(2 + e, j * 16 + 16)
            dve_chain.at = base + LINKS * (PAIRS - 2)
            for e in range(2):
                down_panel(0, 0, 2 * e)
                down_panel(0, 0, 2 * e + 1)
                hidden(2 * (PAIRS - 1) + e, e, 0)
                if e == 0:
                    mod_cols(mod(2) + 4 * (PAIRS - 2), 4, 8 + 2 * (PAIRS - 1))
                ada_chunk(2 + e, 16 * PAIRS)
            m = cols[:, mod(2):mod(2) + KD]
            link(nc.vector.tensor_scalar(m, m, 0.5, None, ALU.mult))
            gain(1)
            link(nc.vector.memset(acc[:], 0.0))

            def update(off, it, bank, n, panel, upd):
                dve.wait_ge(panel_done, panel)
                if isinstance(it, int):
                    xb, g = xT[:, it * 4 + off], cols[:, mod(3 * n + 2, it * 4 + off):mod(3 * n + 2, it * 4 + off) + 1]
                else:
                    xb = xT[:, bass.ds(it * 4 + off, 1)].rearrange("p a b -> p (a b)")
                    g = cols[:, bass.ds(it * 4 + (mod(3 * n + 2) + off), 1)]
                nc.vector.scalar_tensor_tensor(out=xb, in0=ps[:, bank], scalar=g, in1=xb,
                                               op0=ALU.mult, op1=ALU.add).then_inc(x_updated, 1)

            def add_square(par, value):
                dve.wait_ge(sq_ready, value)
                nc.vector.tensor_tensor(acc[:], acc[:], tmp[:, par], ALU.add).then_inc(sq_added, 1)
                dve.wait_ge(sq_added, value)

            def down1_iteration(it, nxt):
                for half in range(2):
                    down_panel(0, it, 6 * half + 4)
                    down_panel(0, it, 6 * half + 5)
                    if half == 0:
                        for q in range(6, 10):
                            down_panel(0, it, q)
                    else:
                        if it == 0:
                            mod_cols(mod(2) + 4 * (PAIRS - 1), 4, 8 + 2 * PAIRS)
                        for e in range(2):
                            ada_chunk(2 + e, it * 32 + 16 * 13)
                        nxt(it)
                    for e in range(2):
                        update(2 * half + e, it, 2 * half + e, 0, it * 12 + (P_DOWN[0] + 6 * half + 5 + e), None)
                    for e in range(2):
                        add_square(e, it * 4 + (2 * half + e + 1))
                mod_cols(it * 4 + (mod(2) + 4 * PAIRS), 4, it * 2 + (8 + 2 * PAIRS + 2))

            down1_iteration(0, lambda i: [down_panel(0, 1, q) for q in range(4)])

            def mix_panel(m):
                if V0 <= m < QK0:
                    lo(P_MIX + m, m % 4, raw[:, (m // 2) % 2, 1024 * (m % 2):1024 * (m % 2 + 1)]
                       .rearrange("p (k n) -> p k n", n=256), 4, 256)
                elif m < N_IN:
                    lo(P_MIX + m, m % 4, raw2((m // 2) % 2, 0, KD, m % 2), KD)
                else:
                    src = raw[:, (m // 2) % 2].rearrange("p (k n) -> p k n", n=512)[:, :, 256 * (m % 2):256 * (m % 2 + 1)]
                    lo(P_MIX + m, m % 4, src, 4, 256)

            down1_iteration(1, lambda _: [mix_panel(q) for q in range(4)])
            variance(1)
            modulate(1)

            dve.wait_ge(bd_hi_ready, 1)
            nc.vector.tensor_tensor(bd_lo[:], bd[:], f(bd_hi[:]), ALU.subtract).then_inc(bd_ready, 1)

            def head_out(h):
                dve.wait_ge(o_rstd, h + 1)
                if h:
                    dve.wait_ge(o_ready, h)
                nc.vector.scalar_tensor_tensor(out=o_val, in0=ps[:, head_bank(h)], scalar=misc[:, HG8:HG8 + 1],
                                               in1=o_inv, op0=ALU.mult, op1=ALU.mult).then_inc(o_f32, 1)

            def head_lo(h):
                dve.wait_ge(o_hi, h + 1)
                nc.vector.tensor_tensor(q_lo[:, h], o_val, f(q_hi[:, h]), ALU.subtract).then_inc(o_ready, 1)

            def tile_out(t):
                bank = ps[:, tile_bank(t)]
                if t < V0:
                    dve.wait_ge(conv0, t + 1)
                    for lag in range(1, CW):
                        w = CONV_W + (CW - 1 - lag) * RT + t
                        i = nc.vector.scalar_tensor_tensor(
                            out=xr[:, t, lag:S], in0=bank[:, 0:S - lag], scalar=cols[:, w:w + 1],
                            in1=xr[:, t, lag:S], op0=ALU.mult, op1=ALU.add)
                        if lag < CW - 1:
                            link(i)
                    i.then_inc(conv_done, 1)
                    dve.wait_ge(c_hi_ready, t + 1)
                    nc.vector.tensor_tensor(c_lo[t % 2][:], xr[:, t], f(c_hi[t % 2][:]), ALU.subtract)\
                        .then_inc(c_ready2, 1)
                elif t < QK0:
                    n = t - V0
                    tok = 2 * (n % 2)
                    sl = (slice(None), slice(tok, tok + 2), slice(256 * (n // 2), 256 * (n // 2) + 256))
                    dve.wait_ge(v_hi_ready, n + 1)
                    nc.vector.tensor_tensor(v_lo[sl], bank.rearrange("p (t n) -> p t n", t=2), f(v_hi[sl]),
                                            ALU.subtract).then_inc(v_ready, 1)

            for xh in range(LAST):
                s = xh // 2
                if xh % 2 == 0 and 0 < s <= N_IN:
                    for m in panels_at(s):
                        mix_panel(m)
                    tile_out(s - 1)
                if xh in (2 * N_IN + 2, 2 * N_IN + 4, 2 * N_IN + 5, 2 * N_IN + 6):
                    mix_panel(N_IN + 4 + (2 * N_IN + 2, 2 * N_IN + 4, 2 * N_IN + 5, 2 * N_IN + 6).index(xh))
                if xh in range(6, 6 + 2 * RT, 2):
                    n = xh // 2 - 3
                    dve.wait_ge(i_ready, n + 1)
                    nc.vector.tensor_tensor(xr[:, n], xr[:, n], ps[:, 7], ALU.mult).then_inc(ix_ready, 1)
                if xh in (9, 11):
                    ada_chunk(2 + (xh - 9) // 2, 16 * 16)
                if xh == 13:
                    mod_cols(mod(2) + 4 * PAIRS + 8, 4, 9 * KD // 2)
                    gain(2)
                    m = cols[:, mod(8):mod(8) + KD]
                    link(nc.vector.tensor_scalar(m, m, 0.5, None, ALU.mult))
                    dve.wait_ge(alibi_ready, 1)
                    link(nc.vector.memset(alibi[0:CHUNK, :, S - CHUNK:S], MASKED))
                if xh in (14, 15):
                    for n in ((0, 1), (2, 3))[xh - 14]:
                        dve.wait_ge(a_ready, n + 1)
                        link(nc.vector.tensor_tensor(drive[:, n], decay[:, n], decay[:, n], ALU.mult))
                        nc.vector.scalar_tensor_tensor(out=drive[:, n], in0=drive[:, n], scalar=1.0,
                                                       in1=tanh_z[:, n], op0=ALU.add, op1=ALU.mult).then_inc(d_ready, 1)
                if xh in (17, 19):
                    for n in ((0, 1), (2, 3))[(xh - 17) // 2]:
                        dve.wait_ge(sqrt_ready, n + 1)
                        dve.wait_ge(ix_ready, n + 1)
                        link(nc.vector.tensor_tensor(drive[:, n], drive[:, n], xr[:, n], ALU.mult))
                        nc.vector.tensor_tensor_scan(xr[:, n], decay[:, n], drive[:, n], 0.0, ALU.mult, ALU.add)\
                            .then_inc(scan_done, 1)
                if xh % 2 and s - 1 in QK:
                    n, (w, h) = s - 1 - QK0, QK[s - 1]
                    g = (Q_G, K_G)[w]
                    y, t = acc[:], tmp[:, 1]
                    dve.wait_ge(qk_sq_rstd, n + 1)
                    link(nc.vector.scalar_tensor_tensor(out=t, in0=ps[:, 7], scalar=EPS * HD, in1=t,
                                                        op0=ALU.add, op1=ALU.mult))
                    link(nc.vector.scalar_tensor_tensor(out=y, in0=t, scalar=-3.0 * HD, in1=y,
                                                        op0=ALU.add, op1=ALU.mult))
                    nc.vector.scalar_tensor_tensor(out=t, in0=ps[:, tile_bank(s - 1)], scalar=cols[:, g:g + 1], in1=y,
                                                   op0=ALU.mult, op1=ALU.mult).then_inc(qk_f32, 1)
                if xh - 1 in HEAD_STAT:
                    head_out(HEAD_STAT[xh - 1])
                if xh - 2 in HEAD_STAT:
                    head_lo(HEAD_STAT[xh - 2])
                if xh - 1 in UNITS:
                    h, b = UNITS[xh - 1]
                    u = UNIT_NO[h, b]
                    W, mc = (b + 1) * P, MX[u % 2]
                    dve.wait_ge(exp_ready, 2 * u + 2)
                    link(nc.vector.reciprocal(misc[:, mc + 6:mc + 8], misc[:, mc + 4:mc + 6]))
                    link(nc.vector.tensor_tensor(misc[:, mc + 8:mc + 9], misc[:, mc + 7:mc + 8],
                                                 misc[:, NEG_LAM:NEG_LAM + 1], ALU.mult))
                    p0, p1 = prob[:, u % 2, 0, 0:W], prob[:, u % 2, 1, 0:W]
                    link(nc.vector.tensor_scalar(p1, p1, misc[:, mc + 8:mc + 9], None, ALU.mult))
                    nc.vector.scalar_tensor_tensor(out=p0, in0=p0, scalar=misc[:, mc + 6:mc + 7], in1=p1,
                                                   op0=ALU.mult, op1=ALU.add).then_inc(diff_ready, 1)
                if xh - 2 in UNITS:
                    h, b = UNITS[xh - 2]
                    u = UNIT_NO[h, b]
                    dve.wait_ge(pt_hi, u + 1)
                    nc.vector.tensor_tensor(p_lo[:, 0:b + 1], ps[:, 5, 0:(b + 1) * P].rearrange("p (k n) -> p k n", n=P),
                                            f(p_hi[:, 0:b + 1]), ALU.subtract).then_inc(pt_ready, 1)
                if xh in UNITS:
                    h, b = UNITS[xh]
                    u = UNIT_NO[h, b]
                    W, mc = (b + 1) * P, MX[u % 2]
                    if u >= 2:
                        dve.wait_ge(pt_done, u - 1)
                    dve.wait_ge(score_done, u + 1)
                    for m in range(2):
                        i = nc.vector.tensor_tensor_reduce(
                            out=prob[:, u % 2, m, 0:W], in0=ps[:, 3 + m, 0:W], in1=alibi[:, h, S - W:S],
                            scale=HD ** -0.5, scalar=-3e38, op0=ALU.subtract, op1=ALU.max,
                            accum_out=misc[:, mc + m:mc + m + 1])
                    link(i)
                    nc.vector.tensor_scalar(misc[:, mc + 2:mc + 4], misc[:, mc:mc + 2], -1.0, None, ALU.mult)\
                        .then_inc(max_ready, 1)
                if xh == 2 * N_IN:
                    for n in range(RT):
                        dve.wait_ge(gelu_ready, n + 1)
                        nc.vector.tensor_tensor(gate[:, n], gate[:, n], xr[:, n], ALU.mult).then_inc(rnn_f32, 1)
                if xh == 2 * N_IN + 1:
                    for n in range(RT):
                        dve.wait_ge(rnn_hi, n + 1)
                        nc.vector.tensor_tensor(k_lo[:, n], gate[:, n], f(k_hi[:, n]), ALU.subtract).then_inc(rnn_ready, 1)
            link(nc.vector.memset(acc[:], 0.0))
            for q in range(4):
                lo(P_FFN[1] + q, q, raw2(q % 2, 0, KD, q // 2), KD)
                for e in range(2):
                    update(2 * (q % 2) + e, q // 2, OUT_BANK[2 * q + e], 1, P_MIX + N_IN + 4 + q + 1, None)
                for e in range(2):
                    add_square(e, KD + 2 * q + e + 1)
            variance(2)
            modulate(2)

            with dve.Fori(0, (PAIRS - 1) // 2) as it:
                for m in range(2):
                    for e in range(2):
                        ffn_panels(1, it * 2 + (1 + m), e, ((2, 3), (0, 1))[m])
                        hidden(it * 4 + (2 * m + e), e, 1)
            for e in range(2):
                down_panel(1, 0, 2 * e)
                down_panel(1, 0, 2 * e + 1)
                hidden(2 * (PAIRS - 1) + e, e, 1)
            for it in range(2):
                for half in range(2):
                    down_panel(1, it, 6 * half + 4)
                    down_panel(1, it, 6 * half + 5)
                    if half == 0:
                        for q in range(6, 10):
                            down_panel(1, it, q)
                    elif it == 0:
                        for q in range(4):
                            down_panel(1, 1, q)
                    for e in range(2):
                        update(2 * half + e, it, 2 * half + e, 2, it * 12 + (P_DOWN[1] + 6 * half + 5 + e), None)

        @block.tensor
        def _(pe):
            def mm3(o, w, r, first, last):
                nc.tensor.matmul(o, w[0], r[0], start=first, stop=False)
                nc.tensor.matmul(o, w[0], r[1], start=False, stop=False)
                return nc.tensor.matmul(o, w[1], r[0], start=False, stop=last)

            def wblk(slot, k):
                return w_hi[:, slot, k * P:(k + 1) * P], w_lo[:, slot, k * P:(k + 1) * P]

            def ada_cols(src, n, col, bank=4):
                pe.wait_ge(ada_sum, n)
                for e in range(2):
                    i = nc.tensor.matmul(ps[:, bank, col + e:col + e + 1], src[:, e * P:(e + 1) * P],
                                         ones[:, 0:1], start=True, stop=True)
                i.then_inc(ada_done, 1)

            pe.wait_ge(s_const, 2)
            pe.wait_ge(s_rows, 16 * 3)
            nc.tensor.transpose(ps[:, 6, 0:ROWS_A], row_in[0:ROWS_A, 0], ident[0:ROWS_A, 0:ROWS_A]).then_inc(rows_done, 1)
            pe.wait_ge(cols_ready, 1)
            for d in range(KD):
                if d >= 2:
                    pe.wait_ge(xt_out, d - 1)
                for t in range(TT):
                    if d == 0:
                        pe.wait_ge(x_in[t], 16)
                    i = nc.tensor.transpose(ps[:, 6 + d % 2, t * P:(t + 1) * P], x_nat[:, t, d * P:(d + 1) * P], ident[:])
                i.then_inc(xt_done, 1)

            def early_ada(n):
                if n % 2:
                    return ada_cols(early[:, n], n // 2 + 1, 2, EARLY_BANK[n // 2])
                pe.wait_ge(early_in[n], 16)
                w = early[:, n].rearrange("p (k n) -> p k n", n=256)
                for e in range(2):
                    for k in range(KD):
                        i = nc.tensor.matmul(ps[:, EARLY_BANK[n // 2], e:e + 1], w[:, k, e * P:(e + 1) * P],
                                             cols[:, k:k + 1], start=k == 0, stop=k == KD - 1)
                i.then_inc(ada_done, 1)

            def spread_rstd(n):
                pe.wait_ge(diag_ready, n + 1)
                nc.tensor.matmul(ps[:, 5], ones[:], acc[:], start=True, stop=True).then_inc(rstd_done, 1)

            def row_stats(n, added):
                pe.wait_ge(sq_added, added)
                if n == 2:
                    pe.wait_ge(x_updated, 2 * KD)
                for t in range(TT):
                    i = nc.tensor.matmul(ps[:, 5, t:t + 1], acc[:, t * P:(t + 1) * P], ones[:, 0:1], start=True, stop=True)
                i.then_inc(stat_done, 1)
                spread_rstd(n)


            def hidden_block(n, j, e, first):
                if not first:
                    pe.wait_ge(prod_ready, j + (n * FT - 1))
                for g in range(2):
                    slot = 2 * e + g
                    pe.wait_ge(w_lo_ready, j * 2 + (P_FFN[n] + g + 1))
                    for k in range(KD):
                        if first and e == 0 and g == 0:
                            pe.wait_ge(split_done, SPLIT_FFN[n] - KD + k + 1)
                        i = mm3(ps[:, slot], wblk(slot, k), (h_hi[:, k], h_lo[:, k]), k == 0, k == KD - 1)
                    i.then_inc(panel_done, 1)

            def down_pair(n, it, half, after_first_cut=None):
                for r, (k0, k1) in enumerate(DOWN_CUTS):
                    for e in range(2):
                        q = 6 * half + 2 * r + e
                        pe.wait_ge(w_lo_ready, it * 12 + (P_DOWN[n] + q + 1))
                        if isinstance(it, int) and it == 0 and half == 0:
                            pe.wait_ge(split_done, SPLIT_FFN[n] + k1)
                        for k in range(k0, k1):
                            i = mm3(ps[:, 2 * half + e], wblk(q % 4, k - k0), (a_hi[:, k], a_lo[:, k]),
                                    k == 0, k == FT - 1)
                        i.then_inc(panel_done, 1)
                    if r == 0 and after_first_cut:
                        after_first_cut()

            pe.wait_ge(c_ready, 1)
            pe.wait_ge(xt_out, KD)
            early_ada(0)
            early_ada(1)
            spread_rstd(0)
            for p in range(KD // 2):
                if p == 1:
                    pe.wait_ge(cols_ready, 2)
                if p < KD // 2 - 1:
                    early_ada(2 * p + 2)
                if p == 0:
                    pe.wait_ge(s_rows_b, 16 * 8)
                    nb = NCOLS - ROWS_A
                    nc.tensor.transpose(ps[:, 7, 0:nb], row_in[0:nb, 1], ident[0:nb, 0:nb]).then_inc(rows_done, 1)
                for k in (2 * p, 2 * p + 1):
                    pe.wait_ge(split_done, k + 1)
                    for q in range(4):
                        if k == 0:
                            pe.wait_ge(w_lo_ready, q + 1)
                        i = mm3(ps[:, q], wblk(q, k), (h_hi[:, k], h_lo[:, k]), k == 0, k == KD - 1)
                        if k == KD - 1:
                            i.then_inc(panel_done, 1)
                if p < KD // 2 - 1:
                    early_ada(2 * p + 3)
            hidden_block(0, 2, 0, False)
            ada_cols(raw[:, 2], 5, 0)
            ada_cols(raw[:, 3], 6, 2)
            hidden_block(0, 3, 1, False)
            ada_cols(raw[:, 2], 7, 0)
            with pe.Fori(2, PAIRS) as j:
                hidden_block(0, j * 2, 0, False)
                ada_cols(raw[:, 3], j * 2 + 4, 2)
                hidden_block(0, j * 2 + 1, 1, False)
                ada_cols(raw[:, 2], j * 2 + 5, 0)
            for it in range(2):
                for half in range(2):
                    if it == 1:
                        pe.wait_ge(x_updated, 2 * half + 2)
                    elif half == 0:
                        pe.wait_ge(prod_ready, FT - 1)
                    else:
                        pe.wait_ge(prod_ready, FT)
                    down_pair(0, it, half, (lambda: ada_cols(raw[:, 3], 4 + 2 * PAIRS, 2)) if it + half == 0 else None)
                ada_cols(raw[:, 2], 4 + 2 * PAIRS + 2 * it + 1, 0)
                ada_cols(raw[:, 3], 4 + 2 * PAIRS + 2 * it + 2, 2)
            row_stats(1, KD)

            def spread(xh):
                if xh - 2 in UNITS:
                    h, b = UNITS[xh - 2]
                    u = UNIT_NO[h, b]
                    pe.wait_ge(diff_ready, u + 1)
                    if u:
                        pe.wait_ge(pt_ready, u)
                    for k in range(b + 1):
                        i = nc.tensor.transpose(ps[:, 5, k * P:(k + 1) * P], prob[:, u % 2, 0, k * P:(k + 1) * P], ident[:])
                    i.then_inc(pt_done, 1)
                if xh - 3 in UNITS:
                    h, b = UNITS[xh - 3]
                    u = UNIT_NO[h, b]
                    pe.wait_ge(pt_ready, u + 1)
                    if b == 0 and h >= 2:
                        pe.wait_ge(o_f32, h - 1)
                    if b == 0 and h == 1:
                        pe.wait_ge(qk_f32, 4)
                    if u == 0:
                        pe.wait_ge(v_ready, 4)
                    for k in range(b + 1):
                        i = mm3(ps[:, head_bank(h), b * P:(b + 1) * P],
                                (v_hi[:, k, h * P:(h + 1) * P], v_lo[:, k, h * P:(h + 1) * P]),
                                (p_hi[:, k], p_lo[:, k]), k == 0, k == b)
                    i.then_inc(pv_done, 1)
                if xh in UNITS:
                    h, b = UNITS[xh]
                    u = UNIT_NO[h, b]
                    if u:
                        pe.wait_ge(max_ready, u)
                    pe.wait_ge(qk_ready, max(QK_BY_HEAD[h]) + 1)
                    for m in range(2):
                        r = slice(m * HD, (m + 1) * HD)
                        i = mm3(ps[:, 3 + m, 0:(b + 1) * P],
                                (q_hi[r, h, b * P:(b + 1) * P], q_lo[r, h, b * P:(b + 1) * P]),
                                (k_hi[r, h, 0:(b + 1) * P], k_lo[r, h, 0:(b + 1) * P]), True, True)
                    i.then_inc(score_done, 1)
                if xh % 2 == 0 and xh // 2 - 1 in QK:
                    n = xh // 2 - 1 - QK0
                    pe.wait_ge(sqh_ready, n + 1)
                    if n:
                        pe.wait_ge(qk_f32, n)
                    else:
                        pe.wait_ge(half_ready, 2)
                        pe.wait_ge(ix_ready, RT)
                    nc.tensor.matmul(ps[:, 7], ones_half[:], tmp[:, 0], start=True, stop=True).then_inc(sth_done, 1)
                if xh in range(5, 5 + 2 * RT, 2):
                    n = (xh - 5) // 2
                    pe.wait_ge(c_ready2, n + 1)
                    if n == 0:
                        pe.wait_ge(bd_ready, 1)
                    for g in range(2):
                        if n:
                            pe.wait_ge((r_ready, ix_ready)[g], n)
                        mm3(ps[:, 6 + g], (bd_hi[:, g, n], bd_lo[:, g, n]), (c_hi[n % 2][:], c_lo[n % 2][:]), True, True)\
                            .then_inc(logit_done, 1)
                if xh in HEAD_STAT:
                    h = HEAD_STAT[xh]
                    pe.wait_ge(o_sq, h + 1)
                    if h:
                        pe.wait_ge(o_rstd, h)
                    else:
                        pe.wait_ge(qk_f32, len(QK))
                    nc.tensor.matmul(ps[:, 7], ones[:], o_square, start=True, stop=True).then_inc(o_stat, 1)

            def tile_left(t):
                if t < V0:
                    pe.wait_ge(conv_done, t + 1)
                elif t < QK0:
                    pe.wait_ge(v_ready, t - V0 + 1)
                elif t < GATE0:
                    pe.wait_ge(qk_f32, t - QK0 + 1)
                else:
                    pe.wait_ge(gate_out, t - GATE0 + 1)

            for k in range(KD):
                pe.wait_ge(split_done, SPLIT_FFN[0] + FT + k + 1)
                for t in range(2):
                    if k == 0:
                        pe.wait_ge(w_lo_ready, P_MIX + t + 1)
                    i = mm3(ps[:, t], wblk(t, k), (h_hi[:, k], h_lo[:, k]), k == 0, k == KD - 1)
                    if k == KD - 1:
                        i.then_inc(panel_done, 1)
            for s in range(2, N_IN):
                if s == 6:
                    ada_cols(raw[:, 2], 31, 0)
                    ada_cols(raw[:, 3], 32, 2)
                prev = max([q for q in range(s) if tile_bank(q) == tile_bank(s)], default=None)
                if prev is not None:
                    tile_left(prev)
                bank = ps[:, tile_bank(s)]
                for e in range(2):
                    xh = 2 * s + e
                    if V0 <= s < QK0:
                        n = s - V0
                        t, pair = 2 * (n % 2) + e, 2 * (n // 2)
                        pe.wait_ge(w_lo_ready, P_MIX + V0 + 2 * (n // 2) + 2)
                        for k in range(KD):
                            sl, kk = pair + k // 4, k % 4
                            w = [q[:, sl, kk * 256:(kk + 1) * 256] for q in (w_hi, w_lo)]
                            tok = slice(t * P, (t + 1) * P)
                            i = mm3(bank[:, e * 256:(e + 1) * 256], (h_hi[:, k, tok], h_lo[:, k, tok]), w,
                                    k == 0, k == KD - 1)
                        if e == 1 and n % 2:
                            i.then_inc(panel_done, 2)
                        elif e == 1:
                            i.then_inc(v_half_done, 1)
                    else:
                        pe.wait_ge(w_lo_ready, P_MIX + s + 1)
                        for k in range(4 * e, 4 * e + 4):
                            i = mm3(bank, wblk(s % 4, k), (h_hi[:, k], h_lo[:, k]), k == 0, k == KD - 1)
                        if e == 1:
                            i.then_inc(panel_done, 1)
                    spread(xh)

            spread(2 * N_IN)
            spread(2 * N_IN + 1)
            pe.wait_ge(gate_out, RT)
            pe.wait_ge(max_ready, NH * TT)
            for q in range(8):
                pe.wait_ge(w_lo_ready, P_MIX + N_IN + q + 1)
                src = (k_hi, k_lo) if q < 4 else (q_hi, q_lo)
                if q == 2:
                    pe.wait_ge(pt_ready, NH * TT)
                    pe.wait_ge(o_f32, NH - 1)
                if q == 3:
                    pe.wait_ge(o_f32, NH)
                for e in range(2):
                    for k in range(4):
                        if q in (0, 4) and e == 0:
                            pe.wait_ge((rnn_ready, o_ready)[q // 4], k + 1)
                        w = [t[:, q % 4, k * 256 + e * P:k * 256 + (e + 1) * P] for t in (w_hi, w_lo)]
                        i = mm3(ps[:, OUT_BANK[2 * (q % 4) + e]], w, (src[0][:, k], src[1][:, k]),
                                q < 4 and k == 0, q >= 4 and k == 3)
                i.then_inc(panel_done, 1)
                if q == 0:
                    spread(2 * N_IN + 2)
                if q == 1:
                    spread(2 * N_IN + 3)
                    spread(2 * N_IN + 4)
            row_stats(2, 2 * KD)

            for e in range(2):
                hidden_block(1, e, e, True)
            with pe.Fori(1, PAIRS) as j:
                for e in range(2):
                    hidden_block(1, j * 2 + e, e, False)

            def to_tokens(d):
                pe.wait_ge(x_updated, 2 * KD + d + 1)
                if d >= 2:
                    pe.wait_ge(y_out, d - 1)
                for t in range(TT):
                    i = nc.tensor.transpose(ps[:, 6 + d % 2, t * P:(t + 1) * P], xT[:, d, t * P:(t + 1) * P], ident[:])
                i.then_inc(y_done, 1)

            for it in range(2):
                for half in range(2):
                    if it == 1:
                        pe.wait_ge(x_updated, 2 * KD + 2 * half + 2)
                    else:
                        pe.wait_ge(prod_ready, 2 * FT - 1 + half)
                    down_pair(1, it, half)
                    if it + half:
                        dp = 2 * it + half - 1
                        to_tokens(2 * dp)
                        to_tokens(2 * dp + 1)
            to_tokens(KD - 2)
            to_tokens(KD - 1)


_INS = ["x", "c", "w_ada", "b_ada", "g_norm", "ffn1_w_gate", "ffn1_w_up", "ffn1_w_down", "w_in", "q_norm_g",
        "k_norm_g", "lambda_params", "head_norm_g", "conv_w", "conv_b", "w_rg_a", "b_rg_a", "w_rg_x", "b_rg_x",
        "lru_lambda", "w_out", "ffn2_w_gate", "ffn2_w_up", "ffn2_w_down"]


def kernel(**inputs):
    import numpy as _np
    import concourse.bacc as _bacc
    from concourse import mybir as _mybir
    from concourse.bass_utils import run_bass_kernel_spmd as _run

    nc = _bacc.Bacc("TRN2", target_bir_lowering=False, num_devices=1)
    arrays, args = {}, []
    for name in _INS:
        a = _np.ascontiguousarray(inputs[name])
        arrays[f"in_{name}_dram"] = a
        args.append(nc.dram_tensor(f"in_{name}_dram", a.shape, _mybir.dt.from_np(a.dtype), kind="ExternalInput").ap())
    out = nc.dram_tensor("out_0_dram", inputs["x"].shape, _mybir.dt.float32, kind="ExternalOutput").ap()
    encoder_layer(nc, *args, out)
    r = _run(nc, [arrays], core_ids=[0])
    return r.results[0]["out_0_dram"]
```

```python
from contextlib import ExitStack

import concourse.bass as bass
from concourse import mybir

F32 = mybir.dt.float32
F32R = mybir.dt.float32r
I32 = mybir.dt.int32
ALU = mybir.AluOpType
ACT = mybir.ActivationFunctionType
AX_X = mybir.AxisListType.X

P = 128
EPS = 1e-6
MASKED = 1e30
LAM_INIT = 0.2
RGLRU_C = 8.0
CHUNK = 64
LN_EXP = "natural_log_exp_and_others"


class Chain:

    def __init__(self, sem):
        self.sem, self.at = sem, 0

    def link(self, eng, ins):
        ins.then_inc(self.sem, 1)
        self.at = self.at + 1
        eng.wait_ge(self.sem, self.at)


def encoder_layer(nc, x, c, w_ada, b_ada, g_norm, ffn1_w_gate, ffn1_w_up, ffn1_w_down, w_in, q_norm_g,
                  k_norm_g, lambda_params, head_norm_g, conv_w, conv_b, w_rg_a, b_rg_a, w_rg_x, b_rg_x,
                  lru_lambda, w_out, ffn2_w_gate, ffn2_w_up, ffn2_w_down, out):
    S, D = x.shape[1], x.shape[2]
    FF = ffn1_w_gate.shape[2]
    KD, FT, TT = D // P, FF // P, S // P
    PAIRS = FT // 2
    DA = D // 2
    NH = DA // P
    HD = P // 2
    RT = DA // P
    CW = conv_w.shape[1]
    DOWN_CUTS = [(0, 8), (8, 16), (16, FT)]

    C_ACT, B_ADA, G_NORM = 0, KD, KD + 9 * KD
    ROWS_A = G_NORM + 3 * KD
    Q_G, K_G, H_G = ROWS_A, ROWS_A + 1, ROWS_A + 2
    CONV_W = H_G + 1
    CONV_B = CONV_W + CW * RT
    B_A, B_X, LRU = CONV_B + RT, CONV_B + 2 * RT, CONV_B + 3 * RT
    NCOLS = LRU + RT

    def mod(group, d=0):
        return B_ADA + group * KD + d

    P_FFN = [0, 4 * PAIRS + 3 * KD + 28]
    P_DOWN = [p + 4 * PAIRS for p in P_FFN]
    P_MIX = P_DOWN[0] + 3 * KD
    N_IN = 20
    SPLIT_FFN = [KD, 3 * KD + FT]

    with ExitStack() as ctx:
        def sem(name):
            return ctx.enter_context(nc.semaphore(name))

        top = [(nc.sbuf_base + 31) // 32 * 32]

        def place(name, shape, dt, offset=None):
            size = 4
            for n in shape[1:]:
                size *= n
            if offset is None:
                offset = top[0]
                top[0] += (size + 31) // 32 * 32
            return nc.alloc_sbuf_tensor_at(name, shape, dt, offset=offset), offset

        xT, _ = place("xT", [P, KD, S], F32)
        raw, raw_at = place("raw", [P, 4, 2048], F32)
        w_hi, _ = place("w_hi", [P, 4, 1024], F32R)
        w_lo, _ = place("w_lo", [P, 4, 1024], F32R)
        h_hi, h_at = place("h_hi", [P, KD, S], F32R)
        h_lo, h_lo_at = place("h_lo", [P, KD, S], F32R)
        a_hi, m_at = place("a_hi", [P, FT, S], F32R)
        a_lo, _ = place("a_lo", [P, FT, S], F32R)
        m_end = top[0]
        tmp, _ = place("tmp", [P, 2, S], F32)
        acc, _ = place("acc", [P, S], F32)
        ident, _ = place("ident", [P, P], F32)
        ones, _ = place("ones", [P, P], F32)
        cols, _ = place("cols", [P, NCOLS], F32)
        misc, _ = place("misc", [P, 64], F32)
        assert top[0] <= nc.sbuf_usable_end

        CHUNK_BYTES = 4 * 2048
        x_nat, _ = place("x_nat", [P, TT, D], F32, h_at)
        early, _ = place("early", [P, KD, 2048], F32, m_at)
        small_at = m_at + KD * CHUNK_BYTES
        row_in, _ = place("row_in", [P, 2, P], F32, small_at)
        lam_in, _ = place("lam_in", [P, 4, HD], F32, small_at + 1024)
        lam_pr, _ = place("lam_pr", [P, 2, HD], F32, small_at + 2048)
        x_sq, _ = place("x_sq", [P, 2, D], F32, small_at + 4096)
        scale_rows, _ = place("scale_rows", [P, KD // 2, 256], F32, small_at + 4096 + 2 * 4 * D)
        y_nat, _ = place("y_nat", [P, KD // 2, TT, 2 * P], F32, h_at)

        at = m_at
        mix = {}
        for name, shape, dt in [("q_hi", [P, NH, S], F32R), ("q_lo", [P, NH, S], F32R),
                                ("k_hi", [P, NH, S], F32R), ("k_lo", [P, NH, S], F32R),
                                ("v_hi", [P, TT, S], F32R), ("v_lo", [P, TT, S], F32R),
                                ("xr", [P, RT, S], F32), ("gate", [P, RT, S], F32),
                                ("alibi", [P, NH, S], F32), ("prob", [P, 2, 2, S], F32),
                                ("p_hi", [P, TT, P], F32R), ("p_lo", [P, TT, P], F32R),
                                ("c_hi", [P, S], F32R), ("c_lo", [P, S], F32R)]:
            mix[name], _ = place(name, shape, dt, at)
            n = 4
            for q in shape[1:]:
                n *= q
            at += n
        assert at <= m_end
        gate_at = m_at + 4 * S * (4 * NH + 2 * TT + RT)
        c_hi2, _ = place("c_hi2", [P, S], F32R, gate_at + 4 * S * 2)
        c_lo2, _ = place("c_lo2", [P, S], F32R, gate_at + 4 * S * 3)
        q_hi, q_lo, k_hi, k_lo, v_hi, v_lo = (mix[n] for n in ("q_hi", "q_lo", "k_hi", "k_lo", "v_hi", "v_lo"))
        xr, gate, alibi, prob = (mix[n] for n in ("xr", "gate", "alibi", "prob"))
        p_hi, p_lo = mix["p_hi"], mix["p_lo"]
        c_hi, c_lo = (mix["c_hi"], c_hi2), (mix["c_lo"], c_lo2)
        bd_hi, _ = place("bd_hi", [P, 2, RT, P], F32R, m_at)
        bd_lo, _ = place("bd_lo", [P, 2, RT, P], F32R, m_at + 4096)
        decay, _ = place("decay", [P, RT, S], F32, m_at + 2 * 4 * S * NH)
        heads, _ = place("heads", [P, 3, S], F32, raw_at + 3 * 8192)
        prob_at = gate_at + 4 * S * (RT + NH)
        bd, _ = place("bd", [P, 2, RT, P], F32, prob_at)
        dist, _ = place("dist", [P, S], I32, prob_at + 4096)
        drive, _ = place("drive", [P, RT, S], F32, prob_at)
        tanh_z, _ = place("tanh_z", [P, RT, S], F32, gate_at)
        ones_half, _ = place("ones_half", [P, P], F32, prob_at + 4 * S * 4 + 2 * 4 * S)

        o_square, o_inv, o_val = heads[:, 0], heads[:, 1], heads[:, 2]
        ps = ctx.enter_context(nc.psum_tensor("ps", [P, 8, 512], F32))

        EPS_C, NEG_LAM, LAM_E, LAM_S = 0, 1, 2, 4
        VAR, RSTD, NEWT = 8, 12, 16
        SP8, NSP8, HEAD_G = 20, 24, 28
        MX = [32, 44]
        SPT = 32

        raw_in = [sem(f"raw_in{i}") for i in range(4)]
        w_hi_ready, w_lo_ready = sem("w_hi_ready"), sem("w_lo_ready")
        panel_done = sem("panel_done")
        ada_sum, ada_done = sem("ada_sum"), sem("ada_done")
        out_half_done = sem("out_half_done")
        row_done, row_out = sem("scale_row_done"), sem("scale_row_out")
        early_in = [sem(f"early_in{i}") for i in range(KD)]
        norm_ready, h_hi_ready = sem("norm_ready"), sem("h_hi_ready")
        silu_ready, prod_ready, a_hi_ready = sem("silu_ready"), sem("prod_ready"), sem("a_hi_ready")
        split_done = sem("split_done")
        x_updated, sq_ready, sq_added = sem("x_updated"), sem("sq_ready"), sem("sq_added")
        stat_done, var_ready, rough_ready = sem("stat_done"), sem("var_ready"), sem("rough_ready")
        diag_ready, rstd_done = sem("diag_ready"), sem("rstd_done")
        consts_ready, rows_in, small_rows_in, lambda_in = (sem(n) for n in (
            "consts_ready", "rows_in", "small_rows_in", "lambda_in"))
        rows_done, cols_ready = sem("rows_transposed"), sem("cols_ready")
        c_ready = sem("c_ready")
        xt_done, xt_out, x_squared = sem("x_transposed"), sem("x_evicted"), sem("x_squared")
        x_in = [sem(f"x_in{t}") for t in range(TT)]
        lam_dot, lam_exp, sp_exp = sem("lambda_dots"), sem("lambda_exps"), sem("softplus_exps")
        y_done, y_out, y_stored = sem("y_transposed"), sem("y_evicted"), sem("y_stored")
        dist_ready, bd_zero, bd_in, bd_hi_ready, bd_ready = (sem(n) for n in (
            "dist_ready", "bd_zeroed", "bd_in", "bd_hi_ready", "bd_ready"))
        alibi_ready = sem("alibi_ready")
        v_half_done, v_ready, gate_out = sem("v_half_done"), sem("v_ready"), sem("gate_evicted")
        half_ready, conv_done, scan_done = sem("half_selector_ready"), sem("conv_done"), sem("scan_done")
        qk_sq_rstd, o_rstd = sem("qk_rstd_squared"), sem("o_rstd")
        v_hi_ready, qk_squared, qk_summed = sem("v_hi_ready"), sem("qk_squared"), sem("qk_summed")
        qk_rough, qk_f32, qk_hi, qk_ready = sem("qk_rough_rstd"), sem("qk_scaled"), sem("qk_hi_ready"), sem("qk_ready")
        score_done, max_ready, exp_ready, diff_ready = (sem(n) for n in (
            "score_done", "max_ready", "exp_ready", "diff_ready"))
        pt_done, pt_hi, pt_ready, pv_done = sem("pt_done"), sem("pt_hi_ready"), sem("pt_ready"), sem("pv_done")
        o_sq, o_stat, o_f32, o_hi, o_ready = (sem(n) for n in (
            "o_squared", "o_summed", "o_scaled", "o_hi_ready", "o_ready"))
        conv_started, c_hi_ready, conv_split = sem("conv_started"), sem("c_hi_ready"), sem("conv_split")
        logit_done, r_ready, i_ready, ix_ready = sem("logit_done"), sem("r_ready"), sem("i_ready"), sem("ix_ready")
        gelu_ready, tanh_ready, a_ready, d_ready, sqrt_ready, rnn_f32, rnn_hi, rnn_ready = (sem(n) for n in (
            "gelu_ready", "tanh_ready", "decay_ready", "drive_ready", "sqrt_ready", "rnn_f32", "rnn_hi_ready",
            "rnn_ready"))
        act_chain, dve_chain, pool_chain = (Chain(sem(n)) for n in ("act_chain", "dve_chain", "pool_chain"))

        def f(ap):
            return ap.bitcast(F32)

        gate_v = [w.rearrange("l (k p) n -> p (l k) n", p=P) for w in (ffn1_w_gate, ffn2_w_gate)]
        up_v = [w.rearrange("l (k p) n -> p (l k) n", p=P) for w in (ffn1_w_up, ffn2_w_up)]
        down_v = [w.rearrange("l (k p) n -> p (l k) n", p=P) for w in (ffn1_w_down, ffn2_w_down)]
        ada_v = w_ada.rearrange("l (k p) n -> p (l k) n", p=P)
        in_v = w_in.rearrange("l (k p) n -> p (l k) n", p=P)
        out_v = w_out.rearrange("l (k p) n -> p (l k) n", p=P)
        x_v = x.rearrange("b (t p) d -> p (b t) d", p=P)
        y_v = out.rearrange("b (t p) d -> p (b t) d", p=P)
        IN_COLS = [4 * DA, 4 * DA + 256, 2 * DA, 2 * DA + 256, 0, DA, 256, DA + 256, 3 * DA, 3 * DA + 256]
        V0, QK0, GATE0 = 4, 8, 16
        QK = {8: (0, 0), 9: (0, 1), 10: (1, 0), 11: (1, 1), 12: (0, 2), 13: (0, 3), 14: (1, 2), 15: (1, 3)}
        QK_BY_HEAD = {h: [n for n, s in enumerate(sorted(QK)) if QK[s][1] == h] for h in range(NH)}

        def tile_bank(s):
            return s % 3 if s < 12 else s % 2

        def panels_at(s):
            return {1: (4,), 2: (5,), 3: (6,), 4: (7,), 6: (8, 9), 8: (10, 11)}.get(s, (s + 3,) if s > 8 else ())

        def head_bank(h):
            return (6, 2)[h % 2]

        OUT_BANK = [0, 1, 3, 4, 5, 6, 2, 7]

        AS_H_COMES = [(0,), (1,), (2,), (3,), (4, 5, 6, 7)]
        EARLY_BANK = (4, 6, 7, 4)

        UNITS = {24 + TT * h + b: (h, b) for h in range(NH) for b in range(TT)}
        UNIT_NO = {u: n for n, u in enumerate(UNITS[k] for k in sorted(UNITS))}
        HEAD_END = {24 + TT * h + TT - 1: h for h in range(NH)}
        HEAD_STAT = {x + (4 if h == 0 else 5): h for x, h in HEAD_END.items()}
        LAST = 2 * N_IN + 7

        def raw2(slot, k0, k1, half):
            return raw[:, slot].rearrange("p (k n) -> p k n", n=256)[:, k0:k1, half * P:(half + 1) * P]

        block = ctx.enter_context(nc.Block())

        @block.sync
        def _(sp):
            def load(slot, src):
                n = src.shape[1] * src.shape[2]
                dst = raw[:, slot, 0:n].rearrange("p (k n) -> p k n", k=src.shape[1])
                sp.dma_start(dst, src).then_inc(raw_in[slot], 16)

            def load_ada(slot, ch):
                load(slot, ada_v[:, :, bass.ds(ch * 256, 256)])

            for t in range(TT):
                sp.dma_start(x_nat[:, t], x_v[:, t]).then_inc(x_in[t], 16)
            for i in range(8):
                if i == 2:
                    for slot, w in ((0, gate_v[0]), (1, up_v[0])):
                        load(slot, w[:, :, 0:256])
                ch = KD // 2 * (1 - i % 2) + i // 2
                sp.dma_start(early[:, i].rearrange("p (k n) -> p k n", n=256), ada_v[:, :, 256 * ch:256 * (ch + 1)])\
                    .then_inc(early_in[i], 16)
            row = 0
            for v in (q_norm_g.rearrange("l m d -> l (m d)"), k_norm_g.rearrange("l m d -> l (m d)"), head_norm_g,
                      conv_w.rearrange("l i (t p) -> (l i t) p", p=P), conv_b.rearrange("l (t p) -> (l t) p", p=P),
                      b_rg_a.rearrange("l (t p) -> (l t) p", p=P), b_rg_x.rearrange("l (t p) -> (l t) p", p=P),
                      lru_lambda.rearrange("l (t p) -> (l t) p", p=P)):
                sp.dma_start(row_in[row:row + v.shape[0], 1], v).then_inc(small_rows_in, 16)
                row += v.shape[0]
            sp.dma_start(lam_in[:], lambda_params.to_broadcast([P, 4, HD])).then_inc(lambda_in, 16)
            for slot, w in ((0, gate_v[0]), (1, up_v[0])):
                sp.wait_ge(w_lo_ready, 3 + slot)
                load(slot, w[:, :, 256:512])
            for slot in (2, 3):
                load_ada(slot, 6 + slot)
            with sp.Fori(2, PAIRS) as j:
                sp.wait_ge(w_lo_ready, j * 4 - 1)
                load(0, gate_v[0][:, :, bass.ds(j * 256, 256)])
                sp.wait_ge(w_lo_ready, j * 4)
                load(1, up_v[0][:, :, bass.ds(j * 256, 256)])
                sp.wait_ge(ada_done, j * 2 + 5)
                load_ada(2, j * 2 + 6)
                sp.wait_ge(ada_done, j * 2 + 6)
                load_ada(3, j * 2 + 7)

            def down(n, it, waits):
                base = P_DOWN[n]
                for q in range(6):
                    k0, k1 = DOWN_CUTS[q % 3]
                    if n == 0 and it == 0 and q == 2:
                        for slot in (2, 3):
                            sp.wait_ge(ada_done, 2 * PAIRS + 3 + slot)
                            load_ada(slot, 2 * PAIRS + 4 + slot)
                    s, v = waits[q]
                    sp.wait_ge(s, v)
                    load((0, 1, 2, 3, 0, 1)[q], down_v[n][:, k0:k1, bass.ds(it * 512 + 256 * (q // 3), 256)])

            for it in range(2):
                b = P_DOWN[0]
                down(0, it, [(w_lo_ready, it * 12 + (b - 1)), (w_lo_ready, it * 12 + b),
                             (ada_done, it * 2 + 29), (ada_done, it * 2 + 30),
                             (w_lo_ready, it * 12 + (b + 2)), (w_lo_ready, it * 12 + (b + 4))])
                sp.wait_ge(w_lo_ready, it * 12 + (b + 6))
                load_ada(2, it * 2 + 30)
                sp.wait_ge(w_lo_ready, it * 12 + (b + 8))
                load_ada(3, it * 2 + 31)
            for r in range(10):
                sp.wait_ge(w_lo_ready, P_MIX - 2 + 2 * r)
                load(r % 2, in_v[:, :, IN_COLS[r]:IN_COLS[r] + 256])
                if r == 1:
                    for slot in (2, 3):
                        sp.wait_ge(ada_done, 31 + slot)
                        load_ada(slot, 32 + slot)
            for r in range(4):
                sp.wait_ge(w_lo_ready, P_MIX - 2 + 2 * (10 + r))
                load(r % 2, out_v[:, 4 - 4 * (r // 2):8 - 4 * (r // 2), 512 * (r % 2):512 * (r % 2) + 512])
            b = P_FFN[1]
            for slot, w in ((0, gate_v[1]), (1, up_v[1])):
                sp.wait_ge(w_lo_ready, b - 2 + 2 * slot)
                load(slot, w[:, :, 0:256])
            sp.wait_ge(ada_done, 9 * KD // 2)
            sp.wait_ge(o_ready, NH)
            with sp.Fori(0, (PAIRS - 1) // 2) as it:
                for e in range(2):
                    sp.wait_ge(w_lo_ready, it * 8 + (b - 1 + 4 * e))
                    load(2 - 2 * e, gate_v[1][:, :, bass.ds(it * 512 + 256 * (1 + e), 256)])
                    sp.wait_ge(w_lo_ready, it * 8 + (b + 4 * e))
                    load(3 - 2 * e, up_v[1][:, :, bass.ds(it * 512 + 256 * (1 + e), 256)])
            with sp.Fori(0, 2) as it:
                b = P_DOWN[1]
                down(1, it, [(w_lo_ready, it * 12 + (b - 1)), (w_lo_ready, it * 12 + b),
                             (w_lo_ready, it * 12 + (b - 5)), (w_lo_ready, it * 12 + (b - 4)),
                             (w_lo_ready, it * 12 + (b + 2)), (w_lo_ready, it * 12 + (b + 4))])
            for dp in range(KD // 2):
                sp.wait_ge(y_out, 2 * (dp + 1))
                sp.dma_start(y_v[:, :, 256 * dp:256 * (dp + 1)], y_nat[:, dp]).then_inc(y_stored, 16)
            sp.wait_ge(y_stored, 16 * (KD // 2))

        @block.gpsimd
        def _(pool):
            pool_chain.link(pool, nc.gpsimd.memset(ident[:], 0.0))
            pool_chain.link(pool, nc.gpsimd.affine_select(
                out=ident[:], in_=ident[:], compare_op=ALU.not_equal, fill=1.0, base=0,
                pattern=[[-1, P]], channel_multiplier=1))
            nc.gpsimd.memset(misc[:, EPS_C:EPS_C + 1], EPS).then_inc(consts_ready, 1)
            nc.gpsimd.memset(ones[:], 1.0).then_inc(consts_ready, 1)

            def late_lo(base, m, src):
                pool.wait_ge(w_hi_ready, base + m + 1)
                l_, h_ = (t[:, m].rearrange("p (k n) -> p k n", n=P) for t in (w_lo, w_hi))
                nc.gpsimd.tensor_tensor(l_, src, f(h_), ALU.subtract).then_inc(w_lo_ready, 1)

            for m in (2, 3):
                pool.wait_ge(w_lo_ready, P_MIX + m)
                late_lo(P_MIX, m, raw2(1, 0, KD, m % 2))
            pool.wait_ge(panel_done, P_MIX)
            nc.gpsimd.iota(dist[:], pattern=[[-1, S]], base=S - P, channel_multiplier=1).then_inc(dist_ready, 1)
            nc.gpsimd.memset(bd[:], 0.0).then_inc(bd_zero, 1)
            pool.wait_ge(bd_zero, 1)
            for g, w in enumerate((w_rg_a, w_rg_x)):
                wv = w.rearrange("l (t e) c d -> e c (l t) d", e=2)
                for e in range(2):
                    pool.dma_start(bd[e * HD:(e + 1) * HD, g, :, e * HD:(e + 1) * HD], wv[e]).then_inc(bd_in, 16)
            pool.wait_ge(logit_done, 2 * RT)
            pool_chain.link(pool, nc.gpsimd.memset(ones_half[:], 0.0))
            nc.gpsimd.memset(ones_half[0:HD, 0:HD], 1.0).then_inc(half_ready, 1)
            nc.gpsimd.memset(ones_half[HD:P, HD:P], 1.0).then_inc(half_ready, 1)
            for n, t in enumerate(sorted(QK)):
                w, h = QK[t]
                pool.wait_ge(qk_rough, n + 1)
                if n:
                    pool.wait_ge(qk_ready, n)
                nc.gpsimd.tensor_tensor(tmp[:, 1], acc[:], acc[:], ALU.mult).then_inc(qk_sq_rstd, 1)
                pool.wait_ge(qk_hi, n + 1)
                nc.gpsimd.tensor_tensor((q_lo, k_lo)[w][:, h], tmp[:, 1], f((q_hi, k_hi)[w][:, h]), ALU.subtract)\
                    .then_inc(qk_ready, 1)
            for m in (2, 3):
                pool.wait_ge(w_lo_ready, P_FFN[1] + m)
                late_lo(P_FFN[1], m, raw2(m % 2, 0, KD, 1))

        @block.scalar
        def _(act):
            act.dma_start(row_in[0:KD, 0], c.rearrange("b (k p) -> (b k) p", p=P)).then_inc(rows_in, 16)
            act.dma_start(row_in[B_ADA:G_NORM, 0], b_ada.rearrange("l (k p) -> (l k) p", p=P)).then_inc(rows_in, 16)
            act.dma_start(row_in[G_NORM:ROWS_A, 0],
                          g_norm.rearrange("l s (k p) -> (l s k) p", p=P)).then_inc(rows_in, 16)
            def rough_rstd(n):
                nc.scalar.preload_act_table_set(LN_EXP)
                act.wait_ge(var_ready, n + 1)
                act_chain.link(act, nc.scalar.activation(misc[:, RSTD:RSTD + TT], misc[:, VAR:VAR + TT], ACT.Ln))
                nc.scalar.activation(misc[:, RSTD:RSTD + TT], misc[:, RSTD:RSTD + TT], ACT.Exp, scale=-0.5)\
                    .then_inc(rough_ready, 1)

            for t in range(TT):
                act.wait_ge(x_in[t], 16)
                i = nc.scalar.activation(x_sq[:, t % 2], x_nat[:, t], ACT.Square,
                                         accum_out=misc[:, RSTD + t:RSTD + t + 1])
                i.then_inc(x_squared, 1)
                if t < TT - 2:
                    act.wait_ge(x_squared, t + 1)
            rough_rstd(0)
            act.wait_ge(cols_ready, 1)
            nc.scalar.activation(cols[:, 0:KD], cols[:, 0:KD], ACT.Silu).then_inc(c_ready, 1)

            def hi(n, slot, src, k, width=P, fresh=None, wait=True):
                if wait:
                    act.wait_ge(panel_done, n - 3)
                if fresh is not None:
                    act.wait_ge(raw_in[fresh[0]], fresh[1])
                dst = w_hi[:, slot, 0:k * width].rearrange("p (k n) -> p k n", n=width)
                nc.scalar.copy(dst, src).then_inc(w_hi_ready, 1)

            def modulate(n, blocks=range(KD)):
                for d in blocks:
                    act.wait_ge(norm_ready, n * KD + d + 1)
                    nc.scalar.activation(h_hi[:, d], tmp[:, d % 2], ACT.Identity,
                                         bias=cols[:, mod(3 * n, d):mod(3 * n, d) + 1]).then_inc(h_hi_ready, 1)

            def square(d, upd):
                act.wait_ge(x_updated, upd + 1)
                nc.scalar.activation(tmp[:, d % 2], xT[:, d], ACT.Square).then_inc(sq_ready, 1)

            def hidden(j, jl, n):
                act.wait_ge(panel_done, j * 2 + (P_FFN[n] + 2))
                act.wait_ge(split_done, j + (SPLIT_FFN[n] - 1))
                nc.scalar.activation(tmp[:, jl], ps[:, 2 * jl], ACT.Silu).then_inc(silu_ready, 1)
                act.wait_ge(prod_ready, j + (n * FT + 1))
                nc.scalar.copy(a_hi[:, j] if isinstance(j, int) else a_hi[:, bass.ds(j, 1)].rearrange(
                    "p a b -> p (a b)"), tmp[:, jl]).then_inc(a_hi_ready, 1)

            def ffn_panels(n, j, e, slots, ords):
                for g in range(2):
                    hi(j * 4 + (P_FFN[n] + 2 * e + g), 2 * e + g, raw2(slots[g], 0, KD, e), KD,
                       fresh=(slots[g], ords) if e == 0 else None)

            def down_panel(n, it, q):
                r, e = q // 2, q % 2
                slot = (0, 1, 2, 3, 0, 1)[r]
                k0, k1 = DOWN_CUTS[r % 3]
                per = 2
                if n == 0:
                    first = (12, 12, 12, 12, 13, 13)[r]
                else:
                    first, per = (29, 29, 22, 22, 30, 30)[r], (2, 2, 1, 1, 2, 2)[r]
                hi(it * 12 + (P_DOWN[n] + q), q % 4, raw2(slot, 0, k1 - k0, e), k1 - k0,
                   fresh=(slot, it * (16 * per) + 16 * first) if e == 0 else None)

            for p in range(KD // 2):
                act.wait_ge(row_done, p + 1)
                nc.scalar.copy(scale_rows[0:1, p], ps[0:1, EARLY_BANK[p], 256:512]).then_inc(row_out, 1)
                modulate(0, range(2 * p, 2 * p + 2))
                if p == 0:
                    for q in range(4):
                        hi(q, q, raw2(q % 2, 0, KD, q // 2), KD, fresh=(q % 2, 16), wait=False)
            for e in range(2):
                ffn_panels(0, 1, e, (0, 1), 16 * 2)
                hidden(e, e, 0)
            act.wait_ge(lam_dot, 1)
            nc.scalar.activation(misc[:, LAM_E:LAM_E + 2], misc[:, LAM_S:LAM_S + 2], ACT.Exp).then_inc(lam_exp, 1)
            act.wait_ge(sp_exp, 1)
            nc.scalar.activation(misc[:, SPT:SPT + RT], misc[:, SPT:SPT + RT], ACT.Exp, scale=-1.0)\
                .then_inc(lam_exp, 1)
            with act.Fori(1, PAIRS - 1) as j:
                for e in range(2):
                    ffn_panels(0, j + 1, e, (0, 1), j * 16 + 16 * 2)
                    hidden(j * 2 + e, e, 0)
            for e in range(2):
                down_panel(0, 0, 2 * e)
                down_panel(0, 0, 2 * e + 1)
                hidden(2 * (PAIRS - 1) + e, e, 0)

            def down1_half(it, half, nxt):
                down_panel(0, it, 6 * half + 4)
                down_panel(0, it, 6 * half + 5)
                nxt(0)
                nxt(1)
                for e in range(2):
                    d = 4 * it + 2 * half + e
                    if d >= 2:
                        act.wait_ge(sq_added, d - 1)
                    square(d, d)
                nxt(2)
                if it + half < 2:
                    nxt(3)

            def mix_panel(m):
                fresh = ((m // 2) % 2, 16 * (16 + m // 4)) if m % 2 == 0 else None
                if V0 <= m < QK0:
                    hi(P_MIX + m, m % 4, raw[:, (m // 2) % 2, 1024 * (m % 2):1024 * (m % 2 + 1)]
                       .rearrange("p (k n) -> p k n", n=256), 4, 256, fresh=fresh)
                elif m < N_IN:
                    hi(P_MIX + m, m % 4, raw2((m // 2) % 2, 0, KD, m % 2), KD, fresh=fresh)
                else:
                    src = raw[:, (m // 2) % 2].rearrange("p (k n) -> p k n", n=512)[:, :, 256 * (m % 2):256 * (m % 2 + 1)]
                    hi(P_MIX + m, m % 4, src, 4, 256, fresh=fresh)

            for it in range(2):
                down1_half(it, 0, lambda q: down_panel(0, it, 6 + q))
                down1_half(it, 1, lambda q: mix_panel(q) if it else down_panel(0, 1, q))
            rough_rstd(1)
            mix_panel(3)
            modulate(1)

            act.wait_ge(bd_in, 64)
            nc.scalar.copy(bd_hi[:], bd[:]).then_inc(bd_hi_ready, 1)
            act.wait_ge(dist_ready, 1)
            for h in range(NH):
                slope = 2.0 ** (-8.0 * (h + 1) / NH) * HD ** 0.5
                i = nc.scalar.activation(alibi[:, h], dist[:], ACT.Abs, scale=slope)
            i.then_inc(alibi_ready, 1)

            def tile_out(t):
                bank = ps[:, tile_bank(t)]
                if t in (V0, V0 + 2):
                    act.wait_ge(v_half_done, (t - V0) // 2 + 1)
                else:
                    act.wait_ge(panel_done, P_MIX + t + 1)
                if t < V0:
                    nc.scalar.activation(xr[:, t], bank, ACT.Identity,
                                         scale=cols[:, CONV_W + 3 * RT + t:CONV_W + 3 * RT + t + 1],
                                         bias=cols[:, CONV_B + t:CONV_B + t + 1]).then_inc(conv_started, 1)
                elif t < QK0:
                    n = t - V0
                    tok = 2 * (n % 2)
                    nc.scalar.copy(v_hi[:, tok:tok + 2, 256 * (n // 2):256 * (n // 2) + 256],
                                   bank.rearrange("p (t n) -> p t n", t=2)).then_inc(v_hi_ready, 1)
                elif t in QK:
                    n = t - QK0
                    if n:
                        act.wait_ge(qk_summed, n)
                    nc.scalar.activation(tmp[:, 0], bank, ACT.Square).then_inc(qk_squared, 1)
                else:
                    n = t - GATE0
                    nc.scalar.copy(gate[:, n], bank).then_inc(gate_out, 1)

            def rough(src, dst, count, done):
                act_chain.link(act, nc.scalar.activation(dst, src, ACT.Ln, scale=1.0 / count,
                                                         bias=misc[:, EPS_C:EPS_C + 1]))
                nc.scalar.activation(dst, dst, ACT.Exp, scale=-0.5).then_inc(done, 1)

            def conv_hi_part(t):
                act.wait_ge(conv_done, t + 1)
                if t >= 2:
                    act.wait_ge(logit_done, 2 * t - 2)
                nc.scalar.copy(c_hi[t % 2][:], xr[:, t]).then_inc(c_hi_ready, 1)

            def head_rough(h):
                act.wait_ge(o_stat, h + 1)
                rough(ps[:, 7], o_inv, P, o_rstd)

            def unit_exp(x):
                h, b = UNITS[x]
                u = UNIT_NO[h, b]
                W, mc = (b + 1) * P, MX[u % 2]
                act.wait_ge(max_ready, u + 1)
                for m in range(2):
                    nc.scalar.activation(prob[:, u % 2, m, 0:W], prob[:, u % 2, m, 0:W], ACT.Exp,
                                         bias=misc[:, mc + 2 + m:mc + 3 + m],
                                         accum_out=misc[:, mc + 4 + m:mc + 5 + m]).then_inc(exp_ready, 1)

            def qk_hi_part(t):
                n, (w, h) = t - QK0, QK[t]
                act.wait_ge(qk_f32, n + 1)
                nc.scalar.copy((q_hi, k_hi)[w][:, h], tmp[:, 1]).then_inc(qk_hi, 1)

            for xh in range(LAST):
                s = xh // 2
                if xh in range(6, 6 + 2 * RT, 2):
                    n = xh // 2 - 3
                    act.wait_ge(logit_done, 2 * n + 2)
                    nc.scalar.activation(decay[:, n], ps[:, 6], ACT.Sigmoid,
                                         bias=cols[:, B_A + n:B_A + n + 1]).then_inc(r_ready, 1)
                    nc.scalar.activation(ps[:, 7], ps[:, 7], ACT.Sigmoid,
                                         bias=cols[:, B_X + n:B_X + n + 1]).then_inc(i_ready, 1)
                if xh - 1 in HEAD_STAT and xh != 2 * N_IN + 1:
                    head_rough(HEAD_STAT[xh - 1])
                if xh % 2 == 0 and 0 < s <= N_IN:
                    tile_out(s - 1)
                if xh % 2 == 0 and xh - 1 in UNITS:
                    unit_exp(xh - 1)
                if xh % 2 == 0 and s - 2 in QK:
                    qk_hi_part(s - 2)
                if xh % 2 == 0 and 0 < s < N_IN:
                    for m in panels_at(s):
                        mix_panel(m)
                    if s <= V0:
                        conv_hi_part(s - 1)
                    if s - 1 in QK:
                        act.wait_ge(qk_summed, s - QK0)
                        rough(ps[:, 7], acc[:], HD, qk_rough)
                if xh == 13:
                    for n in range(RT):
                        act.wait_ge(r_ready, n + 1)
                        nc.scalar.activation(tanh_z[:, n], decay[:, n], ACT.Tanh,
                                             scale=misc[:, SP8 + n:SP8 + n + 1]).then_inc(tanh_ready, 1)
                    for n in range(RT):
                        act.wait_ge(tanh_ready, n + 1)
                        nc.scalar.activation(decay[:, n], decay[:, n], ACT.Exp,
                                             scale=misc[:, NSP8 + n:NSP8 + n + 1]).then_inc(a_ready, 1)
                if xh == 16:
                    for n in range(RT):
                        act.wait_ge(d_ready, n + 1)
                        nc.scalar.activation(drive[:, n], drive[:, n], ACT.Sqrt).then_inc(sqrt_ready, 1)
                    nc.scalar.preload_act_table_set(LN_EXP)
                if xh - 2 in HEAD_STAT:
                    h = HEAD_STAT[xh - 2]
                    act.wait_ge(o_f32, h + 1)
                    nc.scalar.copy(q_hi[:, h], o_val).then_inc(o_hi, 1)
                if xh - 2 in UNITS:
                    h, b = UNITS[xh - 2]
                    u = UNIT_NO[h, b]
                    act.wait_ge(pt_done, u + 1)
                    if u:
                        act.wait_ge(pv_done, u)
                    nc.scalar.copy(p_hi[:, 0:b + 1], ps[:, 5, 0:(b + 1) * P].rearrange("p (k n) -> p k n", n=P))\
                        .then_inc(pt_hi, 1)
                if xh % 2 == 0 and xh in UNITS:
                    unit_exp(xh)
                if xh - 4 in HEAD_END:
                    h = HEAD_END[xh - 4]
                    act.wait_ge(pv_done, TT * (h + 1))
                    if h == 0:
                        act.wait_ge(scan_done, RT)
                    else:
                        act.wait_ge(o_stat, h)
                    nc.scalar.activation(o_square, ps[:, head_bank(h)], ACT.Square).then_inc(o_sq, 1)
                if xh == 2 * N_IN:
                    for n in range(RT):
                        act.wait_ge(gate_out, n + 1)
                        nc.scalar.activation(gate[:, n], gate[:, n], ACT.Gelu_apprx_tanh).then_inc(gelu_ready, 1)
                if xh == 2 * N_IN + 1:
                    for n in range(RT):
                        act.wait_ge(rnn_f32, n + 1)
                        nc.scalar.copy(k_hi[:, n], gate[:, n]).then_inc(rnn_hi, 1)
                    nc.scalar.preload_act_table_set(LN_EXP)
                    head_rough(HEAD_STAT[xh - 1])
                    mix_panel(N_IN + 3)
                if xh == 2 * N_IN + 4:
                    mix_panel(N_IN + 4)
            for m in range(N_IN + 5, N_IN + 8):
                mix_panel(m)
            for q in range(4):
                if q < 2:
                    hi(P_FFN[1] + q, q, raw2(q % 2, 0, KD, q // 2), KD, fresh=(q % 2, 16 * 23))
                for e in range(2):
                    act.wait_ge(sq_added, KD + 2 * q - 1 + e)
                    square(2 * q + e, KD + 2 * q + e)
                if q == 2:
                    hi(P_FFN[1] + q, q, raw2(q % 2, 0, KD, q // 2), KD)
            rough_rstd(2)
            hi(P_FFN[1] + 3, 3, raw2(1, 0, KD, 1), KD)
            modulate(2)

            with act.Fori(0, (PAIRS - 1) // 2) as it:
                for m in range(2):
                    for e in range(2):
                        ffn_panels(1, it * 2 + (1 + m), e, ((2, 3), (0, 1))[m],
                                   it * 16 + 16 * (17, 24)[m])
                        hidden(it * 4 + (2 * m + e), e, 1)
            for e in range(2):
                down_panel(1, 0, 2 * e)
                down_panel(1, 0, 2 * e + 1)
                hidden(2 * (PAIRS - 1) + e, e, 1)

            def evict(d):
                act.wait_ge(y_done, d + 1)
                nc.scalar.copy(y_nat[:, d // 2, :, P * (d % 2):P * (d % 2 + 1)],
                               ps[:, 6 + d % 2].rearrange("p (t n) -> p t n", t=TT)).then_inc(y_out, 1)

            for q in range(4, 12):
                down_panel(1, 0, q)
            for q in range(4):
                down_panel(1, 1, q)
            evict(0)
            evict(1)
            for q in range(4, 10):
                down_panel(1, 1, q)
            evict(2)
            evict(3)
            for q in range(10, 12):
                down_panel(1, 1, q)
            for d in range(4, KD):
                evict(d)

        @block.vector
        def _(dve):
            link = lambda ins: dve_chain.link(dve, ins)

            dve.wait_ge(rows_done, 1)
            nc.vector.tensor_copy(cols[:, 0:ROWS_A], ps[:, 6, 0:ROWS_A]).then_inc(cols_ready, 1)
            dve.wait_ge(cols_ready, 1)

            def ada_chunk(slot, ordv, src=None):
                if src is None:
                    dve.wait_ge(raw_in[slot], ordv)
                    src = raw[:, slot]
                r = src.rearrange("p (k n) -> p k n", n=256)
                link(nc.vector.tensor_scalar(r[:, 0], r[:, 0], cols[:, 0:1], None, ALU.mult))
                for k in range(1, KD):
                    i = nc.vector.scalar_tensor_tensor(out=r[:, 0], in0=r[:, k], scalar=cols[:, k:k + 1],
                                                       in1=r[:, 0], op0=ALU.mult, op1=ALU.add)
                    if k < KD - 1:
                        link(i)
                i.then_inc(ada_sum, 1)

            def variance(n):
                v, y, t = (misc[:, q:q + TT] for q in (VAR, RSTD, NEWT))
                if n == 0:
                    dve.wait_ge(x_squared, TT)
                    sums = y
                else:
                    dve.wait_ge(stat_done, n)
                    sums = ps[:, 5, 0:TT]
                nc.vector.tensor_scalar(v, sums, 1.0 / D, EPS, ALU.mult, ALU.add).then_inc(var_ready, 1)
                dve.wait_ge(rough_ready, n + 1)
                link(nc.vector.tensor_tensor(t, y, y, ALU.mult))
                link(nc.vector.tensor_tensor(t, t, v, ALU.mult))
                link(nc.vector.scalar_tensor_tensor(out=y, in0=t, scalar=-3.0, in1=y, op0=ALU.add, op1=ALU.mult))
                for q in range(TT):
                    i = nc.vector.tensor_scalar(acc[:, q * P:(q + 1) * P], ident[:], misc[:, RSTD + q:RSTD + q + 1],
                                                -0.5, ALU.mult, ALU.mult)
                i.then_inc(diag_ready, 1)

            def modulate(n, blocks=range(KD)):
                dve.wait_ge(rstd_done, n + 1)

                def scaled(d):
                    if d >= 2:
                        dve.wait_ge(split_done, n * KD + (FT if n else 0) + d - 1)
                    nc.vector.scalar_tensor_tensor(
                        out=tmp[:, d % 2], in0=xT[:, d], scalar=cols[:, mod(3 * n + 1, d):mod(3 * n + 1, d) + 1],
                        in1=ps[:, 5], op0=ALU.mult, op1=ALU.mult).then_inc(norm_ready, 1)

                scaled(blocks[0])
                for d in blocks:
                    if d != blocks[-1]:
                        scaled(d + 1)
                    dve.wait_ge(h_hi_ready, n * KD + d + 1)
                    nc.vector.scalar_tensor_tensor(
                        out=h_lo[:, d], in0=tmp[:, d % 2], scalar=cols[:, mod(3 * n, d):mod(3 * n, d) + 1],
                        in1=f(h_hi[:, d]), op0=ALU.add, op1=ALU.subtract).then_inc(split_done, 1)

            def gain(n):
                m = cols[:, mod(3 * n + 1):mod(3 * n + 1) + KD]
                link(nc.vector.scalar_tensor_tensor(out=m, in0=m, scalar=1.0,
                                                    in1=cols[:, G_NORM + n * KD:G_NORM + (n + 1) * KD],
                                                    op0=ALU.add, op1=ALU.mult))

            for d in range(KD):
                dve.wait_ge(xt_done, d + 1)
                nc.vector.tensor_copy(xT[:, d], ps[:, 6 + d % 2]).then_inc(xt_out, 1)
                if d == 1:
                    variance(0)

            def lo(n, slot, src, k, width=P):
                dve.wait_ge(w_hi_ready, n + 1)
                h_, l_ = (t[:, slot, 0:k * width].rearrange("p (k n) -> p k n", n=width) for t in (w_hi, w_lo))
                nc.vector.tensor_tensor(l_, src, f(h_), ALU.subtract).then_inc(w_lo_ready, 1)

            def hidden(j, jl, n):
                dve.wait_ge(silu_ready, j + (n * FT + 1))
                nc.vector.tensor_tensor(tmp[:, jl], tmp[:, jl], ps[:, 2 * jl + 1], ALU.mult).then_inc(prod_ready, 1)
                at_j = (lambda t: t[:, j]) if isinstance(j, int) else (
                    lambda t: t[:, bass.ds(j, 1)].rearrange("p a b -> p (a b)"))
                dve.wait_ge(a_hi_ready, j + (n * FT + 1))
                nc.vector.tensor_tensor(at_j(a_lo), tmp[:, jl], f(at_j(a_hi)), ALU.subtract).then_inc(split_done, 1)

            def ffn_panels(n, j, e, slots):
                for g in range(2):
                    lo(j * 4 + (P_FFN[n] + 2 * e + g), 2 * e + g, raw2(slots[g], 0, KD, e), KD)

            def down_panel(n, it, q):
                r, e = q // 2, q % 2
                k0, k1 = DOWN_CUTS[r % 3]
                lo(it * 12 + (P_DOWN[n] + q), q % 4, raw2((0, 1, 2, 3, 0, 1)[r], 0, k1 - k0, e), k1 - k0)

            def mod_cols(first, count, done):
                dve.wait_ge(ada_done, done)
                m = cols[:, bass.ds(first, count)]
                link(nc.vector.tensor_tensor(m, m, ps[:, 4, 0:count], ALU.add))

            def small_columns():
                dve.wait_ge(rows_done, 2)
                nc.vector.tensor_copy(cols[:, ROWS_A:NCOLS], ps[:, 7, 0:NCOLS - ROWS_A]).then_inc(cols_ready, 1)
                dve.wait_ge(cols_ready, 2)
                dve.wait_ge(lambda_in, 16)
                for m in range(2):
                    i = nc.vector.tensor_tensor_reduce(out=lam_pr[:, m], in0=lam_in[:, 2 * m], in1=lam_in[:, 2 * m + 1],
                                                       scale=1.0, scalar=0.0, op0=ALU.mult, op1=ALU.add,
                                                       accum_out=misc[:, LAM_S + m:LAM_S + m + 1])
                i.then_inc(lam_dot, 1)
                nc.vector.scalar_tensor_tensor(out=misc[:, SPT:SPT + RT], in0=cols[:, LRU:LRU + RT], scalar=-1.0,
                                               in1=cols[:, LRU:LRU + RT], op0=ALU.mult, op1=ALU.max).then_inc(sp_exp, 1)

            def lambda_and_softplus():
                dve.wait_ge(lam_exp, 2)
                link(nc.vector.tensor_tensor(misc[:, NEG_LAM:NEG_LAM + 1], misc[:, LAM_E + 1:LAM_E + 2],
                                             misc[:, LAM_E:LAM_E + 1], ALU.subtract))
                link(nc.vector.tensor_scalar(misc[:, NEG_LAM:NEG_LAM + 1], misc[:, NEG_LAM:NEG_LAM + 1], -LAM_INIT,
                                             None, ALU.add))
                link(nc.vector.tensor_scalar(misc[:, HEAD_G:HEAD_G + 1], cols[:, H_G:H_G + 1], 1.0 - LAM_INIT, None, ALU.mult))
                link(nc.vector.tensor_scalar(cols[:, Q_G:K_G + 1], cols[:, Q_G:K_G + 1], -0.5 / HD, None, ALU.mult))
                e_, s_, q_, a_ = (misc[:, SPT + RT * i:SPT + RT * (i + 1)] for i in range(4))
                link(nc.vector.tensor_scalar(s_, e_, 2.0, None, ALU.add))
                link(nc.vector.reciprocal(q_, s_))
                link(nc.vector.tensor_tensor(s_, e_, q_, ALU.mult))
                link(nc.vector.tensor_tensor(q_, s_, s_, ALU.mult))
                link(nc.vector.memset(a_, 1.0 / 19.0))
                for i in range(17, 0, -2):
                    link(nc.vector.tensor_tensor(a_, a_, q_, ALU.mult))
                    link(nc.vector.tensor_scalar(a_, a_, 1.0 / i, None, ALU.add))
                link(nc.vector.tensor_tensor(a_, a_, s_, ALU.mult))
                link(nc.vector.tensor_scalar(q_, cols[:, LRU:LRU + RT], -1.0, 0.0, ALU.mult, ALU.max))
                link(nc.vector.scalar_tensor_tensor(out=q_, in0=a_, scalar=2.0, in1=q_, op0=ALU.mult, op1=ALU.add))
                link(nc.vector.tensor_scalar(misc[:, SP8:SP8 + RT], q_, RGLRU_C, None, ALU.mult))
                link(nc.vector.tensor_scalar(misc[:, NSP8:NSP8 + RT], q_, -RGLRU_C, None, ALU.mult))

            dve.wait_ge(c_ready, 1)
            for p in range(KD // 2):
                dve.wait_ge(early_in[2 * p + 1], 16)
                ada_chunk(None, None, early[:, 2 * p + 1])
                dve.wait_ge(ada_done, 2 * p + 2)
                sc, sh, g = (cols[:, q + 2 * p:q + 2 * p + 2] for q in (mod(1), mod(0), G_NORM))
                link(nc.vector.tensor_tensor(sc, sc, ps[:, EARLY_BANK[p], 0:2], ALU.add))
                link(nc.vector.tensor_tensor(sh, sh, ps[:, EARLY_BANK[p], 2:4], ALU.add))
                link(nc.vector.scalar_tensor_tensor(out=sc, in0=sc, scalar=1.0, in1=g, op0=ALU.add, op1=ALU.mult))
                modulate(0, range(2 * p, 2 * p + 2))
                if p == 0:
                    for q in range(4):
                        lo(q, q, raw2(q % 2, 0, KD, q // 2), KD)
            LINKS = 2 * (KD - 1) + 1
            for e in range(2):
                ffn_panels(0, 1, e, (0, 1))
                hidden(e, e, 0)
                ada_chunk(2 + e, 16)
            small_columns()
            base = dve_chain.at
            with dve.Fori(1, PAIRS - 1) as j:
                dve_chain.at = (j - 1) * LINKS + base
                for e in range(2):
                    ffn_panels(0, j + 1, e, (0, 1))
                    hidden(j * 2 + e, e, 0)
                    if e == 0:
                        mod_cols(j * 4 + (mod(2) - 4), 4, j * 2 + 8)
                    ada_chunk(2 + e, j * 16 + 16)
            dve_chain.at = base + LINKS * (PAIRS - 2)
            for e in range(2):
                down_panel(0, 0, 2 * e)
                down_panel(0, 0, 2 * e + 1)
                hidden(2 * (PAIRS - 1) + e, e, 0)
                if e == 0:
                    mod_cols(mod(2) + 4 * (PAIRS - 2), 4, 8 + 2 * (PAIRS - 1))
                ada_chunk(2 + e, 16 * PAIRS)
            m = cols[:, mod(2):mod(2) + KD]
            link(nc.vector.tensor_scalar(m, m, 0.5, None, ALU.mult))
            gain(1)
            link(nc.vector.memset(acc[:], 0.0))

            def update(off, it, bank, n, panel):
                dve.wait_ge(panel_done, panel)
                if isinstance(it, int):
                    xb, g = xT[:, it * 4 + off], cols[:, mod(3 * n + 2, it * 4 + off):mod(3 * n + 2, it * 4 + off) + 1]
                else:
                    xb = xT[:, bass.ds(it * 4 + off, 1)].rearrange("p a b -> p (a b)")
                    g = cols[:, bass.ds(it * 4 + (mod(3 * n + 2) + off), 1)]
                nc.vector.scalar_tensor_tensor(out=xb, in0=ps[:, bank], scalar=g, in1=xb,
                                               op0=ALU.mult, op1=ALU.add).then_inc(x_updated, 1)

            def add_square(par, value):
                dve.wait_ge(sq_ready, value)
                nc.vector.tensor_tensor(acc[:], acc[:], tmp[:, par], ALU.add).then_inc(sq_added, 1)
                dve.wait_ge(sq_added, value)

            def down1_half(it, half, nxt):
                down_panel(0, it, 6 * half + 4)
                down_panel(0, it, 6 * half + 5)
                if half:
                    if it == 0:
                        mod_cols(mod(2) + 4 * (PAIRS - 1), 4, 8 + 2 * PAIRS)
                    for e in range(2):
                        ada_chunk(2 + e, it * 32 + 16 * 13)
                nxt(0)
                nxt(1)
                for e in range(2):
                    update(2 * half + e, it, 2 * half + e, 0, it * 12 + (P_DOWN[0] + 6 * half + 5 + e))
                for e in range(2):
                    add_square(e, it * 4 + (2 * half + e + 1))
                if it + half < 2:
                    nxt(2)
                    nxt(3)
                if half:
                    mod_cols(it * 4 + (mod(2) + 4 * PAIRS), 4, it * 2 + (8 + 2 * PAIRS + 2))

            def mix_panel(m):
                if V0 <= m < QK0:
                    lo(P_MIX + m, m % 4, raw[:, (m // 2) % 2, 1024 * (m % 2):1024 * (m % 2 + 1)]
                       .rearrange("p (k n) -> p k n", n=256), 4, 256)
                elif m < N_IN:
                    lo(P_MIX + m, m % 4, raw2((m // 2) % 2, 0, KD, m % 2), KD)
                else:
                    src = raw[:, (m // 2) % 2].rearrange("p (k n) -> p k n", n=512)[:, :, 256 * (m % 2):256 * (m % 2 + 1)]
                    lo(P_MIX + m, m % 4, src, 4, 256)

            for it in range(2):
                down1_half(it, 0, lambda q: down_panel(0, it, 6 + q))
                if it == 0:
                    lambda_and_softplus()
                down1_half(it, 1, lambda q: mix_panel(q) if it else down_panel(0, 1, q))
            variance(1)
            modulate(1)

            dve.wait_ge(bd_hi_ready, 1)
            nc.vector.tensor_tensor(bd_lo[:], bd[:], f(bd_hi[:]), ALU.subtract).then_inc(bd_ready, 1)

            def head_out(h):
                dve.wait_ge(o_rstd, h + 1)
                if h:
                    dve.wait_ge(o_ready, h)
                nc.vector.scalar_tensor_tensor(out=o_val, in0=ps[:, head_bank(h)], scalar=misc[:, HEAD_G:HEAD_G + 1],
                                               in1=o_inv, op0=ALU.mult, op1=ALU.mult).then_inc(o_f32, 1)

            def head_lo(h):
                dve.wait_ge(o_hi, h + 1)
                nc.vector.tensor_tensor(q_lo[:, h], o_val, f(q_hi[:, h]), ALU.subtract).then_inc(o_ready, 1)

            def tile_out(t):
                bank = ps[:, tile_bank(t)]
                if t < V0:
                    dve.wait_ge(conv_started, t + 1)
                    for lag in range(1, CW):
                        w = CONV_W + (CW - 1 - lag) * RT + t
                        i = nc.vector.scalar_tensor_tensor(
                            out=xr[:, t, lag:S], in0=bank[:, 0:S - lag], scalar=cols[:, w:w + 1],
                            in1=xr[:, t, lag:S], op0=ALU.mult, op1=ALU.add)
                        if lag < CW - 1:
                            link(i)
                    i.then_inc(conv_done, 1)
                elif t < QK0:
                    n = t - V0
                    tok = 2 * (n % 2)
                    sl = (slice(None), slice(tok, tok + 2), slice(256 * (n // 2), 256 * (n // 2) + 256))
                    dve.wait_ge(v_hi_ready, n + 1)
                    nc.vector.tensor_tensor(v_lo[sl], bank.rearrange("p (t n) -> p t n", t=2), f(v_hi[sl]),
                                            ALU.subtract).then_inc(v_ready, 1)

            for xh in range(LAST):
                s = xh // 2
                if xh in range(6, 6 + 2 * RT, 2):
                    n = xh // 2 - 3
                    dve.wait_ge(i_ready, n + 1)
                    nc.vector.tensor_tensor(xr[:, n], xr[:, n], ps[:, 7], ALU.mult).then_inc(ix_ready, 1)
                if xh % 2 == 0 and 0 < s < N_IN:
                    tile_out(s - 1)
                    if xh not in UNITS:
                        for m in panels_at(s):
                            mix_panel(m)
                    if s <= V0:
                        t = s - 1
                        dve.wait_ge(c_hi_ready, t + 1)
                        nc.vector.tensor_tensor(c_lo[t % 2][:], xr[:, t], f(c_hi[t % 2][:]), ALU.subtract)\
                            .then_inc(conv_split, 1)
                if xh in (9, 11):
                    ada_chunk(2 + (xh - 9) // 2, 16 * 16)
                if xh == 16:
                    mod_cols(mod(2) + 4 * PAIRS + 8, 4, 9 * KD // 2)
                    gain(2)
                    m = cols[:, mod(8):mod(8) + KD]
                    link(nc.vector.tensor_scalar(m, m, 0.5, None, ALU.mult))
                    dve.wait_ge(alibi_ready, 1)
                    link(nc.vector.memset(alibi[0:CHUNK, :, S - CHUNK:S], MASKED))
                if xh in (14, 15):
                    for n in ((0, 1), (2, 3))[xh - 14]:
                        dve.wait_ge(a_ready, n + 1)
                        link(nc.vector.tensor_tensor(drive[:, n], decay[:, n], decay[:, n], ALU.mult))
                        nc.vector.scalar_tensor_tensor(out=drive[:, n], in0=drive[:, n], scalar=1.0,
                                                       in1=tanh_z[:, n], op0=ALU.add, op1=ALU.mult).then_inc(d_ready, 1)
                if xh % 2 and s - 1 in QK:
                    n, (w, h) = s - 1 - QK0, QK[s - 1]
                    g = (Q_G, K_G)[w]
                    y, t = acc[:], tmp[:, 1]
                    dve.wait_ge(qk_sq_rstd, n + 1)
                    link(nc.vector.scalar_tensor_tensor(out=t, in0=ps[:, 7], scalar=EPS * HD, in1=t,
                                                        op0=ALU.add, op1=ALU.mult))
                    link(nc.vector.scalar_tensor_tensor(out=y, in0=t, scalar=-3.0 * HD, in1=y,
                                                        op0=ALU.add, op1=ALU.mult))
                    nc.vector.scalar_tensor_tensor(out=t, in0=ps[:, tile_bank(s - 1)], scalar=cols[:, g:g + 1], in1=y,
                                                   op0=ALU.mult, op1=ALU.mult).then_inc(qk_f32, 1)
                if xh in (17, 19):
                    for n in ((0, 1), (2, 3))[(xh - 17) // 2]:
                        dve.wait_ge(sqrt_ready, n + 1)
                        dve.wait_ge(ix_ready, n + 1)
                        link(nc.vector.tensor_tensor(drive[:, n], drive[:, n], xr[:, n], ALU.mult))
                        nc.vector.tensor_tensor_scan(xr[:, n], decay[:, n], drive[:, n], 0.0, ALU.mult, ALU.add)\
                            .then_inc(scan_done, 1)
                if xh - 1 in HEAD_STAT and xh != 2 * N_IN + 1:
                    head_out(HEAD_STAT[xh - 1])
                if xh - 2 in HEAD_STAT:
                    head_lo(HEAD_STAT[xh - 2])
                if xh - 1 in UNITS:
                    h, b = UNITS[xh - 1]
                    u = UNIT_NO[h, b]
                    W, mc = (b + 1) * P, MX[u % 2]
                    dve.wait_ge(exp_ready, 2 * u + 2)
                    link(nc.vector.reciprocal(misc[:, mc + 6:mc + 8], misc[:, mc + 4:mc + 6]))
                    link(nc.vector.tensor_tensor(misc[:, mc + 8:mc + 9], misc[:, mc + 7:mc + 8],
                                                 misc[:, NEG_LAM:NEG_LAM + 1], ALU.mult))
                    p0, p1 = prob[:, u % 2, 0, 0:W], prob[:, u % 2, 1, 0:W]
                    link(nc.vector.tensor_scalar(p1, p1, misc[:, mc + 8:mc + 9], None, ALU.mult))
                    nc.vector.scalar_tensor_tensor(out=p0, in0=p0, scalar=misc[:, mc + 6:mc + 7], in1=p1,
                                                   op0=ALU.mult, op1=ALU.add).then_inc(diff_ready, 1)
                if xh - 2 in UNITS:
                    h, b = UNITS[xh - 2]
                    u = UNIT_NO[h, b]
                    dve.wait_ge(pt_hi, u + 1)
                    nc.vector.tensor_tensor(p_lo[:, 0:b + 1], ps[:, 5, 0:(b + 1) * P].rearrange("p (k n) -> p k n", n=P),
                                            f(p_hi[:, 0:b + 1]), ALU.subtract).then_inc(pt_ready, 1)
                if xh in UNITS:
                    h, b = UNITS[xh]
                    u = UNIT_NO[h, b]
                    W, mc = (b + 1) * P, MX[u % 2]
                    if u >= 2:
                        dve.wait_ge(pt_done, u - 1)
                    dve.wait_ge(score_done, u + 1)
                    for m in range(2):
                        i = nc.vector.tensor_tensor_reduce(
                            out=prob[:, u % 2, m, 0:W], in0=ps[:, 3 + m, 0:W], in1=alibi[:, h, S - W:S],
                            scale=HD ** -0.5, scalar=-3e38, op0=ALU.subtract, op1=ALU.max,
                            accum_out=misc[:, mc + m:mc + m + 1])
                    link(i)
                    nc.vector.tensor_scalar(misc[:, mc + 2:mc + 4], misc[:, mc:mc + 2], -1.0, None, ALU.mult)\
                        .then_inc(max_ready, 1)
                if xh % 2 == 0 and xh in UNITS:
                    for m in panels_at(s):
                        mix_panel(m)
                if xh == 2 * N_IN:
                    for n in range(RT):
                        dve.wait_ge(gelu_ready, n + 1)
                        nc.vector.tensor_tensor(gate[:, n], gate[:, n], xr[:, n], ALU.mult).then_inc(rnn_f32, 1)
                if xh == 2 * N_IN + 1:
                    for n in range(RT):
                        dve.wait_ge(rnn_hi, n + 1)
                        nc.vector.tensor_tensor(k_lo[:, n], gate[:, n], f(k_hi[:, n]), ALU.subtract).then_inc(rnn_ready, 1)
                    head_out(HEAD_STAT[xh - 1])
                    mix_panel(N_IN + 3)
                if xh == 2 * N_IN + 4:
                    mix_panel(N_IN + 4)
            for m in range(N_IN + 5, N_IN + 8):
                mix_panel(m)
            link(nc.vector.memset(acc[:], 0.0))
            for q in range(4):
                if q < 2:
                    lo(P_FFN[1] + q, q, raw2(q % 2, 0, KD, q // 2), KD)
                for e in range(2):
                    if e == 0:
                        dve.wait_ge(out_half_done, q + 1)
                    update(2 * (q % 2) + e, q // 2, OUT_BANK[2 * q + e], 1, P_MIX + N_IN + 4 + q + e)
                for e in range(2):
                    add_square(e, KD + 2 * q + e + 1)
            variance(2)
            modulate(2)

            with dve.Fori(0, (PAIRS - 1) // 2) as it:
                for m in range(2):
                    for e in range(2):
                        ffn_panels(1, it * 2 + (1 + m), e, ((2, 3), (0, 1))[m])
                        hidden(it * 4 + (2 * m + e), e, 1)
            for e in range(2):
                down_panel(1, 0, 2 * e)
                down_panel(1, 0, 2 * e + 1)
                hidden(2 * (PAIRS - 1) + e, e, 1)
            for it in range(2):
                for half in range(2):
                    down_panel(1, it, 6 * half + 4)
                    down_panel(1, it, 6 * half + 5)
                    if half == 0:
                        for q in range(6, 10):
                            down_panel(1, it, q)
                    elif it == 0:
                        for q in range(4):
                            down_panel(1, 1, q)
                    for e in range(2):
                        update(2 * half + e, it, 2 * half + e, 2, it * 12 + (P_DOWN[1] + 6 * half + 5 + e))

        @block.tensor
        def _(pe):
            def mm3(o, w, r, first, last):
                nc.tensor.matmul(o, w[0], r[0], start=first, stop=False)
                nc.tensor.matmul(o, w[0], r[1], start=False, stop=False)
                return nc.tensor.matmul(o, w[1], r[0], start=False, stop=last)

            def wblk(slot, k):
                return w_hi[:, slot, k * P:(k + 1) * P], w_lo[:, slot, k * P:(k + 1) * P]

            def ada_cols(src, n, col, bank=4):
                pe.wait_ge(ada_sum, n)
                for e in range(2):
                    i = nc.tensor.matmul(ps[:, bank, col + e:col + e + 1], src[:, e * P:(e + 1) * P],
                                         ones[:, 0:1], start=True, stop=True)
                i.then_inc(ada_done, 1)

            pe.wait_ge(consts_ready, 2)
            pe.wait_ge(rows_in, 16 * 3)
            nc.tensor.transpose(ps[:, 6, 0:ROWS_A], row_in[0:ROWS_A, 0], ident[0:ROWS_A, 0:ROWS_A]).then_inc(rows_done, 1)
            pe.wait_ge(cols_ready, 1)
            for d in range(KD):
                if d >= 2:
                    pe.wait_ge(xt_out, d - 1)
                for t in range(TT):
                    if d == 0:
                        pe.wait_ge(x_in[t], 16)
                    i = nc.tensor.transpose(ps[:, 6 + d % 2, t * P:(t + 1) * P], x_nat[:, t, d * P:(d + 1) * P], ident[:])
                i.then_inc(xt_done, 1)

            def scale_row(p):
                pe.wait_ge(early_in[2 * p], 16)
                w = early[:, 2 * p].rearrange("p (k n) -> p k n", n=256)
                for k in range(KD):
                    i = nc.tensor.matmul(ps[0:1, EARLY_BANK[p], 256:512], cols[:, k:k + 1], w[:, k],
                                         start=k == 0, stop=k == KD - 1)
                i.then_inc(row_done, 1)

            def early_cols(p):
                pe.wait_ge(row_out, p + 1)
                for e in range(2):
                    i = nc.tensor.matmul(ps[:, EARLY_BANK[p], e:e + 1], scale_rows[0:1, p, e * P:(e + 1) * P],
                                         ones[0:1, 0:1], start=True, stop=True)
                i.then_inc(ada_done, 1)
                ada_cols(early[:, 2 * p + 1], p + 1, 2, EARLY_BANK[p])

            def spread_rstd(n):
                pe.wait_ge(diag_ready, n + 1)
                nc.tensor.matmul(ps[:, 5], ones[:], acc[:], start=True, stop=True).then_inc(rstd_done, 1)

            def row_stats(n, added):
                pe.wait_ge(sq_added, added)
                if n == 2:
                    pe.wait_ge(x_updated, 2 * KD)
                for t in range(TT):
                    i = nc.tensor.matmul(ps[:, 5, t:t + 1], acc[:, t * P:(t + 1) * P], ones[:, 0:1], start=True, stop=True)
                i.then_inc(stat_done, 1)
                spread_rstd(n)


            def side_by_side(panels, base, split_base, blocks):
                for q in range(panels):
                    if blocks[0] == 0:
                        pe.wait_ge(w_lo_ready, base + (4 if base else q + 1))
                    for k in blocks:
                        if q == 0:
                            pe.wait_ge(split_done, split_base + k + 1)
                        i = mm3(ps[:, q], wblk(q, k), (h_hi[:, k], h_lo[:, k]), k == 0, k == KD - 1)
                    if k == KD - 1:
                        i.then_inc(panel_done, 1)

            def hidden_block(n, j, e):
                pe.wait_ge(prod_ready, j + (n * FT - 1))
                for g in range(2):
                    slot = 2 * e + g
                    pe.wait_ge(w_lo_ready, j * 2 + (P_FFN[n] + g + 1))
                    for k in range(KD):
                        i = mm3(ps[:, slot], wblk(slot, k), (h_hi[:, k], h_lo[:, k]), k == 0, k == KD - 1)
                    i.then_inc(panel_done, 1)

            def down_pair(n, it, half, after_first_cut=None):
                for r, (k0, k1) in enumerate(DOWN_CUTS):
                    for e in range(2):
                        q = 6 * half + 2 * r + e
                        pe.wait_ge(w_lo_ready, it * 12 + (P_DOWN[n] + q + 1))
                        if isinstance(it, int) and it == 0 and half == 0:
                            pe.wait_ge(split_done, SPLIT_FFN[n] + k1)
                        for k in range(k0, k1):
                            i = mm3(ps[:, 2 * half + e], wblk(q % 4, k - k0), (a_hi[:, k], a_lo[:, k]),
                                    k == 0, k == FT - 1)
                        i.then_inc(panel_done, 1)
                    if r == 0 and after_first_cut:
                        after_first_cut()

            pe.wait_ge(c_ready, 1)
            pe.wait_ge(xt_out, KD)
            scale_row(0)
            early_cols(0)
            spread_rstd(0)
            for p in range(KD // 2):
                if p < KD // 2 - 1:
                    scale_row(p + 1)
                side_by_side(4, P_FFN[0], SPLIT_FFN[0] - KD, (2 * p, 2 * p + 1))
                if p < KD // 2 - 1:
                    early_cols(p + 1)
            pe.wait_ge(small_rows_in, 16 * 8)
            nb = NCOLS - ROWS_A
            nc.tensor.transpose(ps[:, 7, 0:nb], row_in[0:nb, 1], ident[0:nb, 0:nb]).then_inc(rows_done, 1)
            hidden_block(0, 2, 0)
            ada_cols(raw[:, 2], 5, 0)
            ada_cols(raw[:, 3], 6, 2)
            hidden_block(0, 3, 1)
            ada_cols(raw[:, 2], 7, 0)
            with pe.Fori(2, PAIRS) as j:
                hidden_block(0, j * 2, 0)
                ada_cols(raw[:, 3], j * 2 + 4, 2)
                hidden_block(0, j * 2 + 1, 1)
                ada_cols(raw[:, 2], j * 2 + 5, 0)
            for it in range(2):
                for half in range(2):
                    if it == 1:
                        pe.wait_ge(x_updated, 2 * half + 2)
                    elif half == 0:
                        pe.wait_ge(prod_ready, FT - 1)
                    else:
                        pe.wait_ge(prod_ready, FT)
                    down_pair(0, it, half, (lambda: ada_cols(raw[:, 3], 4 + 2 * PAIRS, 2)) if it + half == 0 else None)
                ada_cols(raw[:, 2], 4 + 2 * PAIRS + 2 * it + 1, 0)
                ada_cols(raw[:, 3], 4 + 2 * PAIRS + 2 * it + 2, 2)
            row_stats(1, KD)

            def spread(xh):
                if xh - 2 in UNITS:
                    h, b = UNITS[xh - 2]
                    u = UNIT_NO[h, b]
                    pe.wait_ge(diff_ready, u + 1)
                    if u:
                        pe.wait_ge(pt_ready, u)
                    for k in range(b + 1):
                        i = nc.tensor.transpose(ps[:, 5, k * P:(k + 1) * P], prob[:, u % 2, 0, k * P:(k + 1) * P], ident[:])
                    i.then_inc(pt_done, 1)
                if xh - 3 in UNITS:
                    h, b = UNITS[xh - 3]
                    u = UNIT_NO[h, b]
                    pe.wait_ge(pt_ready, u + 1)
                    if b == 0 and h >= 2:
                        pe.wait_ge(o_f32, h - 1)
                    if b == 0 and h == 1:
                        pe.wait_ge(qk_f32, 4)
                    if u == 0:
                        pe.wait_ge(v_ready, 4)
                    for k in range(b + 1):
                        i = mm3(ps[:, head_bank(h), b * P:(b + 1) * P],
                                (v_hi[:, k, h * P:(h + 1) * P], v_lo[:, k, h * P:(h + 1) * P]),
                                (p_hi[:, k], p_lo[:, k]), k == 0, k == b)
                    i.then_inc(pv_done, 1)
                if xh in UNITS:
                    h, b = UNITS[xh]
                    u = UNIT_NO[h, b]
                    if u:
                        pe.wait_ge(max_ready, u)
                    pe.wait_ge(qk_ready, max(QK_BY_HEAD[h]) + 1)
                    for m in range(2):
                        r = slice(m * HD, (m + 1) * HD)
                        i = mm3(ps[:, 3 + m, 0:(b + 1) * P],
                                (q_hi[r, h, b * P:(b + 1) * P], q_lo[r, h, b * P:(b + 1) * P]),
                                (k_hi[r, h, 0:(b + 1) * P], k_lo[r, h, 0:(b + 1) * P]), True, True)
                    i.then_inc(score_done, 1)
                if xh in range(5, 5 + 2 * RT, 2):
                    n = (xh - 5) // 2
                    pe.wait_ge(conv_split, n + 1)
                    if n == 0:
                        pe.wait_ge(bd_ready, 1)
                    for g in range(2):
                        if n:
                            pe.wait_ge((r_ready, ix_ready)[g], n)
                        mm3(ps[:, 6 + g], (bd_hi[:, g, n], bd_lo[:, g, n]), (c_hi[n % 2][:], c_lo[n % 2][:]), True, True)\
                            .then_inc(logit_done, 1)
                if xh in HEAD_STAT:
                    h = HEAD_STAT[xh]
                    pe.wait_ge(o_sq, h + 1)
                    if h:
                        pe.wait_ge(o_rstd, h)
                    else:
                        pe.wait_ge(qk_f32, len(QK) - 1)
                    nc.tensor.matmul(ps[:, 7], ones[:], o_square, start=True, stop=True).then_inc(o_stat, 1)

            def qk_stat(t):
                n = t - QK0
                pe.wait_ge(qk_squared, n + 1)
                if n == len(QK) - 1:
                    pe.wait_ge(o_rstd, 1)
                elif n:
                    pe.wait_ge(qk_f32, n)
                else:
                    pe.wait_ge(half_ready, 2)
                    pe.wait_ge(ix_ready, RT)
                nc.tensor.matmul(ps[:, 7], ones_half[:], tmp[:, 0], start=True, stop=True).then_inc(qk_summed, 1)

            def tile_left(t):
                if t < V0:
                    pe.wait_ge(conv_done, t + 1)
                elif t < QK0:
                    pe.wait_ge(v_ready, t - V0 + 1)
                elif t < GATE0:
                    pe.wait_ge(qk_f32, t - QK0 + 1)
                else:
                    pe.wait_ge(gate_out, t - GATE0 + 1)

            for blocks in AS_H_COMES:
                side_by_side(2, P_MIX, SPLIT_FFN[0] + FT, blocks)
            for s in range(2, N_IN):
                if s == 7:
                    ada_cols(raw[:, 2], 31, 0)
                    ada_cols(raw[:, 3], 32, 2)
                prev = max([q for q in range(s) if tile_bank(q) == tile_bank(s)], default=None)
                if prev is not None:
                    tile_left(prev)
                bank = ps[:, tile_bank(s)]
                for e in range(2):
                    xh = 2 * s + e
                    if V0 <= s < QK0:
                        n = s - V0
                        t, pair = 2 * (n % 2) + e, 2 * (n // 2)
                        pe.wait_ge(w_lo_ready, P_MIX + V0 + 2 * (n // 2) + 2)
                        for k in range(KD):
                            sl, kk = pair + k // 4, k % 4
                            w = [q[:, sl, kk * 256:(kk + 1) * 256] for q in (w_hi, w_lo)]
                            tok = slice(t * P, (t + 1) * P)
                            i = mm3(bank[:, e * 256:(e + 1) * 256], (h_hi[:, k, tok], h_lo[:, k, tok]), w,
                                    k == 0, k == KD - 1)
                        if e == 1 and n % 2:
                            i.then_inc(panel_done, 2)
                        elif e == 1:
                            i.then_inc(v_half_done, 1)
                    else:
                        pe.wait_ge(w_lo_ready, P_MIX + s + 1)
                        for k in range(4 * e, 4 * e + 4):
                            i = mm3(bank, wblk(s % 4, k), (h_hi[:, k], h_lo[:, k]), k == 0, k == KD - 1)
                            if k == 1 and s - 1 in QK:
                                qk_stat(s - 1)
                        if e == 1:
                            i.then_inc(panel_done, 1)
                    spread(xh)

            for xh in range(2 * N_IN, 2 * N_IN + 3):
                spread(xh)
            pe.wait_ge(gate_out, RT)
            pe.wait_ge(max_ready, NH * TT)
            for q in range(8):
                pe.wait_ge(w_lo_ready, P_MIX + N_IN + q + 1)
                src = (k_hi, k_lo) if q < 4 else (q_hi, q_lo)
                if q == 2:
                    pe.wait_ge(pt_ready, NH * TT)
                    pe.wait_ge(o_f32, NH - 1)
                if q == 3:
                    pe.wait_ge(o_f32, NH)
                for e in range(2):
                    for k in range(4):
                        if q in (0, 4) and e == 0:
                            pe.wait_ge((rnn_ready, o_ready)[q // 4], k + 1)
                        w = [t[:, q % 4, k * 256 + e * P:k * 256 + (e + 1) * P] for t in (w_hi, w_lo)]
                        i = mm3(ps[:, OUT_BANK[2 * (q % 4) + e]], w, (src[0][:, k], src[1][:, k]),
                                q < 4 and k == 0, q >= 4 and k == 3)
                    if q >= 4 and e == 0:
                        i.then_inc(out_half_done, 1)
                i.then_inc(panel_done, 1)
                if q == 0:
                    spread(2 * N_IN + 3)
                    spread(2 * N_IN + 4)
            row_stats(2, 2 * KD)

            for blocks in AS_H_COMES:
                side_by_side(4, P_FFN[1], SPLIT_FFN[1] - KD, blocks)
            with pe.Fori(1, PAIRS) as j:
                for e in range(2):
                    hidden_block(1, j * 2 + e, e)

            def to_tokens(d):
                pe.wait_ge(x_updated, 2 * KD + d + 1)
                if d >= 2:
                    pe.wait_ge(y_out, d - 1)
                for t in range(TT):
                    i = nc.tensor.transpose(ps[:, 6 + d % 2, t * P:(t + 1) * P], xT[:, d, t * P:(t + 1) * P], ident[:])
                i.then_inc(y_done, 1)

            for it in range(2):
                for half in range(2):
                    if it == 1:
                        pe.wait_ge(x_updated, 2 * KD + 2 * half + 2)
                    else:
                        pe.wait_ge(prod_ready, 2 * FT - 1 + half)
                    down_pair(1, it, half)
                    if it + half:
                        dp = 2 * it + half - 1
                        to_tokens(2 * dp)
                        to_tokens(2 * dp + 1)
            to_tokens(KD - 2)
            to_tokens(KD - 1)


_INS = ["x", "c", "w_ada", "b_ada", "g_norm", "ffn1_w_gate", "ffn1_w_up", "ffn1_w_down", "w_in", "q_norm_g",
        "k_norm_g", "lambda_params", "head_norm_g", "conv_w", "conv_b", "w_rg_a", "b_rg_a", "w_rg_x", "b_rg_x",
        "lru_lambda", "w_out", "ffn2_w_gate", "ffn2_w_up", "ffn2_w_down"]


def kernel(**inputs):
    import numpy as _np
    import concourse.bacc as _bacc
    from concourse import mybir as _mybir
    from concourse.bass_utils import run_bass_kernel_spmd as _run

    nc = _bacc.Bacc("TRN2", target_bir_lowering=False, num_devices=1)
    arrays, args = {}, []
    for name in _INS:
        a = _np.ascontiguousarray(inputs[name])
        arrays[f"in_{name}_dram"] = a
        args.append(nc.dram_tensor(f"in_{name}_dram", a.shape, _mybir.dt.from_np(a.dtype), kind="ExternalInput").ap())
    out = nc.dram_tensor("out_0_dram", inputs["x"].shape, _mybir.dt.float32, kind="ExternalOutput").ap()
    encoder_layer(nc, *args, out)
    r = _run(nc, [arrays], core_ids=[0])
    return r.results[0]["out_0_dram"]
```
